# Optimizing a Trainium2 kernel written in Bass

```python
import jax, jax.numpy as jnp
from jax import lax
import numpy as np

D_MODEL = 1024
BATCH = 1
SEQ = 256
DEPTH = 2

N_A_LAYERS = DEPTH // 2
N_B_LAYERS = DEPTH - N_A_LAYERS
N_DENSE = (DEPTH + 1) // 2
N_MOE = DEPTH // 2

DN_HEADS = 8
DN_DK = 128
DN_DV = 128
DN_CONV = 4
DN_CHUNK = 64

SW_Q_HEADS = 16
SW_KV_HEADS = 4
SW_HEAD_DIM = 64
SW_WINDOW = 128
SW_BLOCK = 128

D_FF = 2816
N_EXPERTS = 8
TOP_K = 2
D_EXPERT = 2816

DEEP_ALPHA = (2 * DEPTH) ** 0.25
DEEP_BETA = (8 * DEPTH) ** -0.25
LN_EPS = 1e-5
RMS_EPS = 1e-6

kernel_name = "yoco_deltanet_swa_sink_alibi_moe_deepnorm"

def layer_norm(x, g, b):
    xf = x.astype(jnp.float32)
    mu = jnp.mean(xf, axis=-1, keepdims=True)
    xc = xf - mu
    var = jnp.mean(xc * xc, axis=-1, keepdims=True)
    y = xc * lax.rsqrt(var + LN_EPS) * g.astype(jnp.float32) + b.astype(jnp.float32)
    return y.astype(x.dtype)

def l2_normalize(a):
    return a * lax.rsqrt(jnp.sum(a * a, axis=-1, keepdims=True) + RMS_EPS)

def causal_short_conv(x, w):
    K = w.shape[0]
    T = x.shape[1]
    xp = jnp.pad(x, ((0, 0), (K - 1, 0), (0, 0)))
    return sum(xp[:, i:i + T] * w[i] for i in range(K))

def gated_delta_chunked(q, k, v, g, beta):
    B_, T, H, dk = q.shape
    dv = v.shape[-1]
    C = DN_CHUNK
    N = T // C

    def chunks(a):
        a = a.reshape((B_, N, C, H) + a.shape[3:])
        return jnp.moveaxis(a, 3, 1)

    q, k, v, g, beta = chunks(q), chunks(k), chunks(v), chunks(g), chunks(beta)
    G = jnp.cumsum(g, axis=-1)
    idx = jnp.arange(C)
    incl = idx[:, None] >= idx[None, :]
    strict = idx[:, None] > idx[None, :]
    decay = jnp.exp(jnp.where(incl, G[..., :, None] - G[..., None, :], -jnp.inf))

    kb = k * beta[..., None]
    vb = v * beta[..., None]
    L = jnp.where(strict, jnp.einsum('bhncd,bhnsd->bhncs', kb, k) * decay, 0.0)
    eye = jnp.eye(C, dtype=q.dtype)
    rhs = jnp.concatenate([vb, kb * jnp.exp(G)[..., None]], axis=-1)
    sol = lax.linalg.triangular_solve(eye + L, rhs, left_side=True, lower=True,
                                      unit_diagonal=True)
    U = sol[..., :dv]
    W = sol[..., dv:]

    Aqk = jnp.einsum('bhncd,bhnsd->bhncs', q, k) * decay
    qg = q * jnp.exp(G)[..., None]
    kdec = k * jnp.exp(G[..., -1:] - G)[..., None]
    glast = jnp.exp(G[..., -1])

    xs = tuple(jnp.moveaxis(a, 2, 0) for a in (U, W, qg, Aqk, kdec, glast))

    def step(S, inp):
        u, w, qc, aqk, kd, gl = inp
        v_new = u - jnp.einsum('bhck,bhkv->bhcv', w, S)
        o = jnp.einsum('bhck,bhkv->bhcv', qc, S) + jnp.einsum('bhcs,bhsv->bhcv', aqk, v_new)
        S = S * gl[..., None, None] + jnp.einsum('bhck,bhcv->bhkv', kd, v_new)
        return S, o

    S0 = jnp.zeros((B_, H, dk, dv), q.dtype)
    _, o = lax.scan(step, S0, xs)
    return o.transpose(1, 0, 3, 2, 4).reshape(B_, T, H, dv)

def deltanet_mixer(x, w_in, conv_w, a_log, dt_bias, norm_w, w_out):
    B_, T, _ = x.shape
    H, dk, dv = DN_HEADS, DN_DK, DN_DV
    proj = x @ w_in
    n_qkv = 2 * H * dk + H * dv
    qkv = proj[..., :n_qkv]
    z = proj[..., n_qkv:n_qkv + H * dv]
    b_logit = proj[..., n_qkv + H * dv:n_qkv + H * dv + H]
    a_logit = proj[..., n_qkv + H * dv + H:]
    qkv = jax.nn.silu(causal_short_conv(qkv, conv_w)).astype(jnp.float32)
    q = qkv[..., :H * dk].reshape(B_, T, H, dk)
    k = qkv[..., H * dk:2 * H * dk].reshape(B_, T, H, dk)
    v = qkv[..., 2 * H * dk:].reshape(B_, T, H, dv)
    q = l2_normalize(q) * (dk ** -0.5)
    k = l2_normalize(k)
    beta = jax.nn.sigmoid(b_logit.astype(jnp.float32))
    g = -jnp.exp(a_log.astype(jnp.float32)) * jax.nn.softplus(
        a_logit.astype(jnp.float32) + dt_bias.astype(jnp.float32))
    o = gated_delta_chunked(q, k, v, g, beta)
    o = o * lax.rsqrt(jnp.mean(o * o, axis=-1, keepdims=True) + RMS_EPS) * norm_w.astype(jnp.float32)
    o = o * jax.nn.silu(z.reshape(B_, T, H, dv).astype(jnp.float32))
    return o.reshape(B_, T, H * dv).astype(x.dtype) @ w_out

def shared_kv(x, w_kv):
    B_, T, _ = x.shape
    kv = x @ w_kv
    n = SW_KV_HEADS * SW_HEAD_DIM
    k = kv[..., :n].reshape(B_, T, SW_KV_HEADS, SW_HEAD_DIM)
    v = kv[..., n:].reshape(B_, T, SW_KV_HEADS, SW_HEAD_DIM)
    return k, v

def alibi_slopes(n):
    return 2.0 ** (-8.0 * jnp.arange(1, n + 1, dtype=jnp.float32) / n)

def sliding_window_mixer(x, k_sh, v_sh, w_q, sinks, w_out):
    B_, T, _ = x.shape
    Hq, Hk, hd = SW_Q_HEADS, SW_KV_HEADS, SW_HEAD_DIM
    G = Hq // Hk
    W = SW_BLOCK
    nb = T // W
    q = (x @ w_q).astype(jnp.float32).reshape(B_, nb, W, Hk, G, hd) * (hd ** -0.5)

    def band(a):
        a = a.astype(jnp.float32)
        ap = jnp.pad(a, ((0, 0), (W, 0), (0, 0), (0, 0)))
        prev = ap[:, :T].reshape(B_, nb, W, Hk, hd)
        cur = a.reshape(B_, nb, W, Hk, hd)
        return jnp.concatenate([prev, cur], axis=2)

    kb, vb = band(k_sh), band(v_sh)
    s = jnp.einsum('bnqkgd,bnskd->bnkgqs', q, kb)
    qi = jnp.arange(W)
    sj = jnp.arange(2 * W)
    dist = qi[:, None] + W - sj[None, :]
    kpos = jnp.arange(nb)[:, None] * W - W + sj[None, :]
    valid = ((dist >= 0) & (dist < SW_WINDOW))[None] & (kpos >= 0)[:, None, :]
    slopes = alibi_slopes(Hq).reshape(Hk, G)
    s = s - slopes[:, :, None, None] * dist.astype(jnp.float32)
    s = jnp.where(valid[None, :, None, None], s, -jnp.inf)
    sink = sinks.astype(jnp.float32).reshape(Hk, G)[:, :, None, None]
    m = jnp.maximum(jnp.max(s, axis=-1, keepdims=True), sink)
    p = jnp.exp(s - m)
    p = p / (jnp.sum(p, axis=-1, keepdims=True) + jnp.exp(sink - m))
    o = jnp.einsum('bnkgqs,bnskd->bnqkgd', p, vb).reshape(B_, T, Hq * hd)
    return o.astype(x.dtype) @ w_out

def dense_swiglu(x, w_gu, w_down):
    h = x @ w_gu
    gate, up = h[..., :D_FF], h[..., D_FF:]
    return (jax.nn.silu(gate) * up) @ w_down

def moe_swiglu(x, w_router, w_gu, w_down):
    B_, T, D = x.shape
    xt = x.reshape(-1, D)
    logits = (xt @ w_router).astype(jnp.float32)
    top_v, top_i = lax.top_k(logits, TOP_K)
    top_w = jax.nn.softmax(top_v, axis=-1)
    gates = jnp.sum(jax.nn.one_hot(top_i, N_EXPERTS, dtype=jnp.float32) * top_w[..., None], axis=1)
    out = jnp.zeros_like(xt)
    for e in range(N_EXPERTS):
        h = xt @ w_gu[e]
        y = (jax.nn.silu(h[:, :D_EXPERT]) * h[:, D_EXPERT:]) @ w_down[e]
        out = out + gates[:, e:e + 1].astype(xt.dtype) * y
    return out.reshape(B_, T, D)

def setup_inputs(seed: int = 0) -> dict:
    key = jax.random.key(seed)
    ks = jax.random.split(key, 20)
    f32 = jnp.float32
    D = D_MODEL

    def nrm(k, shape, scale):
        return jax.random.normal(k, shape, f32) * scale

    dn_in_width = 2 * DN_HEADS * DN_DK + 2 * DN_HEADS * DN_DV + 2 * DN_HEADS
    dt = jnp.exp(jax.random.uniform(ks[3], (N_A_LAYERS, DN_HEADS), f32,
                                    math_log(1e-3), math_log(1e-1)))
    dt_bias = dt + jnp.log(-jnp.expm1(-dt))
    n_kv = SW_KV_HEADS * SW_HEAD_DIM
    w_k = nrm(ks[7], (D, n_kv), D ** -0.5)
    w_v = nrm(ks[8], (D, n_kv), D ** -0.5 * DEEP_BETA)
    return {
        "x": jax.random.normal(ks[0], (BATCH, SEQ, D), f32),
        "dn_w_in": nrm(ks[1], (N_A_LAYERS, D, dn_in_width), D ** -0.5),
        "dn_conv_w": nrm(ks[2], (N_A_LAYERS, DN_CONV, 2 * DN_HEADS * DN_DK + DN_HEADS * DN_DV), DN_CONV ** -0.5),
        "dn_a_log": jnp.log(jax.random.uniform(ks[4], (N_A_LAYERS, DN_HEADS), f32, 1.0, 16.0)),
        "dn_dt_bias": dt_bias,
        "dn_norm_w": 1.0 + nrm(ks[5], (N_A_LAYERS, DN_DV), 0.02),
        "dn_w_out": nrm(ks[6], (N_A_LAYERS, DN_HEADS * DN_DV, D), (DN_HEADS * DN_DV) ** -0.5 * DEEP_BETA),
        "w_kv_shared": jnp.concatenate([w_k, w_v], axis=1),
        "sw_w_q": nrm(ks[9], (N_B_LAYERS, D, SW_Q_HEADS * SW_HEAD_DIM), D ** -0.5),
        "sw_sinks": nrm(ks[10], (N_B_LAYERS, SW_Q_HEADS), 1.0),
        "sw_w_out": nrm(ks[11], (N_B_LAYERS, SW_Q_HEADS * SW_HEAD_DIM, D), (SW_Q_HEADS * SW_HEAD_DIM) ** -0.5 * DEEP_BETA),
        "ffn_w_gu": nrm(ks[12], (N_DENSE, D, 2 * D_FF), D ** -0.5),
        "ffn_w_down": nrm(ks[13], (N_DENSE, D_FF, D), D_FF ** -0.5 * DEEP_BETA),
        "moe_w_router": nrm(ks[14], (N_MOE, D, N_EXPERTS), D ** -0.5),
        "moe_w_gu": nrm(ks[15], (N_MOE, N_EXPERTS, D, 2 * D_EXPERT), D ** -0.5),
        "moe_w_down": nrm(ks[16], (N_MOE, N_EXPERTS, D_EXPERT, D), D_EXPERT ** -0.5 * DEEP_BETA),
        "ln_g": 1.0 + nrm(ks[17], (DEPTH, 2, D), 0.02),
        "ln_b": nrm(ks[18], (DEPTH, 2, D), 0.02),
    }

def math_log(v):
    return float(np.log(v))

def reference(x, dn_w_in, dn_conv_w, dn_a_log, dn_dt_bias, dn_norm_w, dn_w_out,
              w_kv_shared, sw_w_q, sw_sinks, sw_w_out, ffn_w_gu, ffn_w_down,
              moe_w_router, moe_w_gu, moe_w_down, ln_g, ln_b):
    k_sh, v_sh = None, None
    for layer in range(DEPTH):
        if layer < N_A_LAYERS:
            i = layer
            h = deltanet_mixer(x, dn_w_in[i], dn_conv_w[i], dn_a_log[i], dn_dt_bias[i],
                               dn_norm_w[i], dn_w_out[i])
        else:
            if layer == N_A_LAYERS:
                k_sh, v_sh = shared_kv(x, w_kv_shared)
            i = layer - N_A_LAYERS
            h = sliding_window_mixer(x, k_sh, v_sh, sw_w_q[i], sw_sinks[i], sw_w_out[i])
        x = layer_norm(DEEP_ALPHA * x + h, ln_g[layer, 0], ln_b[layer, 0])
        j = layer // 2
        if layer % 2 == 0:
            h = dense_swiglu(x, ffn_w_gu[j], ffn_w_down[j])
        else:
            h = moe_swiglu(x, moe_w_router[j], moe_w_gu[j], moe_w_down[j])
        x = layer_norm(DEEP_ALPHA * x + h, ln_g[layer, 1], ln_b[layer, 1])
    return x


_drawn_inputs = setup_inputs


def setup_inputs(seed=0):
    import zlib

    import numpy as np

    out = dict(_drawn_inputs(seed))
    spreads = {}
    factors = {'dn_norm_w': 8.0, 'sw_sinks': 4.658}
    for name, (base, spread) in spreads.items():
        noise = np.random.default_rng([zlib.crc32(name.encode()), seed]).standard_normal(out[name].shape)
        drawn = base * np.exp(spread * noise) if base else spread * noise
        out[name] = __import__('jax').numpy.asarray(drawn.astype(out[name].dtype))
    for name, factor in factors.items():
        out[name] = (out[name] * factor).astype(out[name].dtype)
    return out
```

```python
from contextlib import ExitStack

import concourse.bass as bass
from concourse import mybir

ALU = mybir.AluOpType
ACT = mybir.ActivationFunctionType
AX = mybir.AxisListType
F32 = mybir.dt.float32
F32R = mybir.dt.float32r
U32 = mybir.dt.uint32
I32 = mybir.dt.int32

P = 128
BIG = 1.0e30

UNIT = 2048
RAW = 6
CUT = 3
AHEAD = 3


def trunk(nc, x_in, w_in, conv_w, a_log, dt_bias, norm_w, w_out, w_kv, w_q, sinks, w_o, w_gu, w_down,
          w_router, moe_gu, moe_down, ln_g, ln_b, out):
    _, T, D = x_in.shape
    NB = T // P
    KD = D // P
    H = a_log.shape[1]
    DK = P
    TAPS = conv_w.shape[1]
    QKV = conv_w.shape[2] // P
    HQ = sinks.shape[1]
    HKV = 4
    GQ = HQ // HKV
    HD = w_kv.shape[1] // (2 * HKV)
    FF = w_down.shape[1]
    FC = FF // 256
    E = w_router.shape[2]
    ALPHA = float(4 ** 0.25)
    assert (T, D, H, FF, E, NB) == (256, 1024, 8, 2816, 8, 2) and HD == 64

    U_QKV = 0
    U_Z = U_QKV + QKV // 2
    U_OUT = U_Z + 4
    U_GU = U_OUT + 4
    U_DOWN = U_GU + 2 * FC
    U_KV = U_DOWN + FC
    U_Q = U_KV + 2
    U_O = U_Q + 4
    U_MOE = U_O + 4
    PER_E = 3 * FC
    PER_IT = 2 * PER_E
    TURNS = E // 2
    assert PER_IT % RAW == 0 and PER_IT % CUT == 0

    ctx = ExitStack()
    with ctx:
        def sb(name, shape, dt=F32, where=None):
            return (where or ctx).enter_context(nc.sbuf_tensor(name, shape, dt))

        def sem(name):
            return ctx.enter_context(nc.semaphore(name))

        raw = sb("raw", [P, RAW, UNIT])
        hi = sb("hi", [P, CUT, UNIT], F32R)
        lo = sb("lo", [P, CUT, UNIT], F32R)
        x = sb("x", [P, NB, D])
        lng = sb("lng", [P, D])
        lnb = sb("lnb", [P, D])
        ident = sb("ident", [P, P])
        ones = sb("ones", [P, P])
        tri_incl = sb("tri_incl", [P, P])
        mhalf = sb("mhalf", [P, 64])
        bnst = sb("bnst", [P, NB, 2, 6])
        bnmv = sb("bnmv", [P, NB, 2])
        lnve = sb("lnve", [P, NB])
        lnrs = sb("lnrs", [P, NB])
        ps = ctx.enter_context(nc.psum_tensor("ps", [P, 8, 512], F32))

        with ExitStack() as a:
            Dm = sb("Dm", [P, NB * H, P], where=a)
            DT = sb("DT", [P, NB * H, P], where=a)
            conv = sb("conv", [P, QKV, T], where=a)
            zn = sb("zn", [P, NB, D], where=a)
            kt = sb("kt", [P, NB, H, P], where=a)
            vb = sb("vb", [P, NB, H, P], where=a)
            Tm = sb("Tm", [P, NB * H, P], where=a)
            Nm = sb("Nm", [P, NB * H, P], where=a)
            masks = sb("masks", [P, 7, P], where=a)
            masksT = sb("masksT", [P, 7, P], where=a)
            mup = sb("mup", [P, P], where=a)
            mlow = sb("mlow", [P, P], where=a)
            cw_rows = sb("cw_rows", [TAPS * QKV, P], where=a)
            cw = sb("cw", [P, TAPS * QKV], where=a)
            wab = sb("wab", [P, KD, 2 * H], where=a)
            wab_hi = sb("wab_hi", [P, KD, 2 * H], F32R, where=a)
            wab_lo = sb("wab_lo", [P, KD, 2 * H], F32R, where=a)
            alog = sb("alog", [P, H], where=a)
            dtb = sb("dtb", [P, H], where=a)
            nw = sb("nw", [P, DK], where=a)
            ab = sb("ab", [P, NB, 2 * H], where=a)
            beta = sb("beta", [P, NB, H], where=a)
            nbeta = sb("nbeta", [P, NB, H], where=a)
            g = sb("g", [P, NB, H], where=a)
            G = sb("G", [P, NB, H], where=a)
            sp = [sb(f"sp{i}", [P, NB, H], where=a) for i in range(6)]
            ea = sb("ea", [P, H], where=a)
            egl = sb("egl", [P, H], where=a)
            eg = sb("eg", [P, H], where=a)
            ss = sb("ss", [P, 2, H, NB], where=a)
            rqk = sb("rqk", [P, 2, H, NB], where=a)
            ms = sb("ms", [P, NB * H], where=a)
            rms = sb("rms", [P, NB * H], where=a)
        xT_hi = sb("xT_hi", [P, KD, T], F32R)
        xT_lo = sb("xT_lo", [P, KD, T], F32R)
        with ExitStack() as a:
            hT_hi = sb("hT_hi", [P, 2 * FC, T], F32R, where=a)
            hT_lo = sb("hT_lo", [P, 2 * FC, T], F32R, where=a)
            sg = sb("sg", [P, 2, 512], where=a)
            hf = sb("hf", [P, 2, 512], where=a)
        with ExitStack() as a:
            kT2 = sb("kT2", [P, HKV, 2, T], where=a)
            vB = sb("vB", [P, NB, HKV * HD], where=a)
            qT = sb("qT", [P, KD, T], where=a)
            dist = sb("dist", [P, 3 * P], where=a)
            sS = sb("sS", [P, 2, GQ, 3 * P], where=a)
            pT = sb("pT", [P, 3 * GQ, P], where=a)
            sk = sb("sk", [P, HQ], where=a)
            smax = sb("smax", [P, 2, NB, GQ], where=a)
            nmax = sb("nmax", [P, 2, NB, GQ], where=a)
            ske = sb("ske", [P, 2, NB, GQ], where=a)
            ssum = sb("ssum", [P, 2, NB, GQ], where=a)
            sinv = sb("sinv", [P, 2, NB, GQ], where=a)
        x3_hi = sb("x3_hi", [P, NB, D], F32R)
        x3_lo = sb("x3_lo", [P, NB, D], F32R)
        xg_hi = sb("xg_hi", [P, KD, P], F32R)
        xg_lo = sb("xg_lo", [P, KD, P], F32R)
        sgE = sb("sgE", [P, 2, 256])
        actE = sb("actE", [P, 2, 256])
        hE_hi = sb("hE_hi", [P, 2 * FC, P], F32R)
        hE_lo = sb("hE_lo", [P, 2 * FC, P], F32R)
        y_hi = sb("y_hi", [P, D], F32R)
        y_lo = sb("y_lo", [P, D], F32R)
        oneh = sb("oneh", [P, NB, P], F32R)
        onehT = sb("onehT", [P, 2, NB, P], F32R)
        gslot = sb("gslot", [P, 2])
        iota = sb("iota", [P, 2, P])
        tri_strict = sb("tri_strict", [P, P])
        wr = sb("wr", [P, KD, E])
        wr_hi = sb("wr_hi", [P, KD, E], F32R)
        wr_lo = sb("wr_lo", [P, KD, E], F32R)
        rev = sb("rev", [P, E])
        lg = sb("lg", [P, NB, E])
        lg2 = sb("lg2", [P, NB, E])
        eq = sb("eq", [P, NB, E])
        oh1 = sb("oh1", [P, NB, E])
        oh2 = sb("oh2", [P, NB, E])
        sel = sb("sel", [P, NB, E])
        m1 = sb("m1", [P, NB, 1])
        m2 = sb("m2", [P, NB, 1])
        rr = sb("rr", [P, NB, 1])
        gw = sb("gw", [P, NB, 4])
        pos = sb("pos", [P, NB, E + 1])
        gates = sb("gates", [P, NB, E + 1])
        cmax = sb("cmax", [P, 1])
        cint = sb("cint", [P, 1], I32)

        raw_in = [sem(f"raw_in{i}") for i in range(RAW)]
        hi_ready, lo_ready, unit_used = sem("hi_ready"), sem("lo_ready"), sem("unit_used")
        x_here, small_here, bcast_here = sem("x_here"), sem("small_here"), sem("bcast_here")
        ln_here, sink_here = sem("ln_here"), sem("sink_here")
        consts = sem("consts")
        turned, turn_hi, turn_lo = sem("turned"), sem("turn_hi"), sem("turn_lo")
        ln_var, ln_rstd, ln_done = sem("ln_var"), sem("ln_rstd"), sem("ln_done")
        conv_step, tap_ready, silu_done = sem("conv_step"), sem("tap_ready"), sem("silu_done")
        z_done, cw_turned, cw_here = sem("z_done"), sem("cw_turned"), sem("cw_here")
        ab_cut, ab_mm, ab_here = sem("ab_cut"), sem("ab_mm"), sem("ab_here")
        g_act, g_dve, g_pe = sem("g_act"), sem("g_dve"), sem("g_pe")
        sq_done, ss_mm, ss_here, rqk_here = sem("sq_done"), sem("ss_mm"), sem("ss_here"), sem("rqk_here")
        kv_turned, kv_taken = sem("kv_turned"), sem("kv_taken")
        gdiff, darg, dexp, dmul = sem("gdiff"), sem("darg"), sem("dexp"), sem("dmul")
        kback, kback_taken = sem("kback"), sem("kback_taken")
        kk_mm, kk_taken = sem("kk_mm"), sem("kk_taken")
        kscaled, qg_here = sem("kscaled"), sem("qg_here")
        inv_p, inv_pc, inv_r, inv_rc = sem("inv_p"), sem("inv_pc"), sem("inv_r"), sem("inv_rc")
        scan_mm, scan_ev = sem("scan_mm"), sem("scan_ev")
        o_mm, o_scaled, o_sq, o_sum, o_ms, o_rms, o_z, o_done = (
            sem(f"o_{n}") for n in ("mm", "scaled", "sq", "sum", "ms", "rms", "z", "done"))
        zn_done = sem("zn_done")
        ffn_silu, ffn_act, ffn_hi, ffn_lo = sem("ffn_silu"), sem("ffn_act"), sem("ffn_hi"), sem("ffn_lo")
        kB_act, kB_dve, vB_here, qB_here = sem("kB_act"), sem("kB_dve"), sem("vB_here"), sem("qB_here")
        sc_mm, sc_max, sc_exp, sc_prob = sem("sc_mm"), sem("sc_max"), sem("sc_exp"), sem("sc_prob")
        pt_mm, pt_taken, pv_mm, pv_hi, pv_lo = (sem(f"{n}") for n in ("pt_mm", "pt_taken", "pv_mm", "pv_hi", "pv_lo"))
        sc_bias = sem("sc_bias")
        wr_cut, x3_cut, lg_mm, sel_here, w2_here = (sem(n) for n in ("wr_cut", "x3_cut", "lg_mm", "sel_here", "w2_here"))
        w2_arg, pos_mm, route_here, moe_zero = (sem(n) for n in ("w2_arg", "pos_mm", "route_here", "moe_zero"))
        oneh_here, gathered, xg_hi_here, xg_here = (sem(n) for n in ("oneh_here", "gathered", "xg_hi_here", "xg_here"))
        slots_here = sem("slots_here")
        silu_here, act_here, ff_turned, h_hi, h_here = (sem(n) for n in ("silu_here", "act_here", "ff_turned", "h_hi", "h_here"))
        y_hi_here, y_here, scattered, acc_added = (sem(n) for n in ("y_hi_here", "y_here", "scattered", "acc_added"))
        out_done = sem("out_done")
        dve_chain, act_chain, pool_chain = sem("dve_chain"), sem("act_chain"), sem("pool_chain")

        def columns(w, n0, n1, width):
            return w[:, n0:n1].rearrange("(k p) (c n) -> c p k n", p=P, n=width)

        qkv_v = columns(w_in[0], 0, QKV * P, 256)
        z_v = w_in[0][:, QKV * P:QKV * P + D].rearrange("(a k p) (c n) -> a c p k n", p=P, k=4, n=512)
        out_v = w_out[0].rearrange("(u k p) n -> u p k n", p=P, k=2)
        gu_v = columns(w_gu[0], 0, 2 * FF, 256)
        down_v = w_down[0].rearrange("(u k p) n -> u p k n", p=P, k=2)
        kv_v = columns(w_kv, 0, 2 * HKV * HD, 256)
        q_v = columns(w_q[0], 0, D, 256)
        o_v = w_o[0].rearrange("(u k p) n -> u p k n", p=P, k=2)
        mgu_v = moe_gu[0].rearrange("e (a k p) (t c n) -> a c e p k t n", p=P, k=4, t=2, n=256)
        mdown_v = moe_down[0].rearrange("e (u k p) n -> u e p k n", p=P, k=2)

        block = ctx.enter_context(nc.Block())

        def slot(buf, j):
            return buf[:, j % (RAW if buf is raw else CUT), :]

        @block.sync
        def _(sp_):
            def load(j, it, src, view, **dims):
                if j >= RAW:
                    sp_.wait_ge(lo_ready, j - RAW + 1 + PER_IT * it)
                dst = slot(raw, j).rearrange(view, **dims)
                for half in range(2):
                    if len(dst.shape) == 4:
                        d, s = dst[:, :, half, :], src[:, :, half, :]
                    else:
                        k = slice(half * dst.shape[1] // 2, (half + 1) * dst.shape[1] // 2)
                        d, s = dst[:, k, :], src[:, k, :]
                    sp_.dma_start(d, s).then_inc(raw_in[j % RAW], 16)

            for u in range(QKV // 2):
                load(U_QKV + u, 0, qkv_v[u], "p (k n) -> p k n", k=KD)
            for u in range(4):
                load(U_Z + u, 0, z_v[u % 2, u // 2], "p (k n) -> p k n", k=4)
            for u in range(4):
                load(U_OUT + u, 0, out_v[u], "p (k n) -> p k n", k=2)
            for c in range(FC):
                for t in range(2):
                    load(U_GU + 2 * c + t, 0, gu_v[t * FC + c], "p (k n) -> p k n", k=KD)
            for u in range(FC):
                load(U_DOWN + u, 0, down_v[u], "p (k n) -> p k n", k=2)
            for u in range(2):
                load(U_KV + u, 0, kv_v[u], "p (k n) -> p k n", k=KD)
            for u in range(4):
                load(U_Q + u, 0, q_v[u], "p (k n) -> p k n", k=KD)
            for u in range(4):
                load(U_O + u, 0, o_v[u], "p (k n) -> p k n", k=2)

            def expert_unit(base, l, it):
                e = 2 * it + l // PER_E
                if l // PER_E == 2:
                    e = e % E
                u = l % PER_E
                if u < 2 * FC:
                    load(base + l, it, mgu_v[u % 2, u // 2][e], "p (k t n) -> p k t n", k=4, t=2)
                else:
                    load(base + l, it, mdown_v[u - 2 * FC][e], "p (k n) -> p k n", k=2)

            for l in range(AHEAD):
                expert_unit(U_MOE, l, 0)

            def experts(base):
                with sp_.Fori(0, TURNS) as it:
                    for l in range(AHEAD, PER_IT + AHEAD):
                        expert_unit(base, l, it)

            experts(U_MOE)
            sp_.wait_ge(route_here, 1)
            full = sp_.value_load(cint[0:1, 0:1], min_val=0, max_val=T)
            with sp_.If(full > P):
                experts(U_MOE + E * PER_E)
            for b in range(NB):
                sp_.wait_ge(ln_done, 2 * 3 + b + 1)
                sp_.dma_start(out[0].rearrange("(b p) d -> b p d", p=P)[b], x[:, b, :]).then_inc(out_done, 16)
            sp_.wait_ge(out_done, 16 * NB)

        @block.gpsimd
        def _(pool):
            n = [0]

            def link(ins):
                n[0] += 1
                ins.then_inc(pool_chain, 1)

            def settle():
                pool.wait_ge(pool_chain, n[0])

            def select(t, op, fill, base, pattern, mult):
                settle()
                link(pool.affine_select(out=t, in_=t, compare_op=op, fill=fill, base=base,
                                        pattern=pattern, channel_multiplier=mult))

            link(pool.memset(ident[:, :], 0.0))
            select(ident[:, :], ALU.not_equal, 1.0, 0, [[-1, P]], 1)
            settle()
            pool.sem_inc(consts, 1)
            pool.dma_start(alog[:, :], a_log[0].partition_broadcast(P)).then_inc(bcast_here, 16)
            pool.dma_start(dtb[:, :], dt_bias[0].partition_broadcast(P)).then_inc(bcast_here, 16)
            pool.dma_start(nw[:, :], norm_w[0].partition_broadcast(P)).then_inc(bcast_here, 16)

            def load_ln(layer, i):
                pool.dma_start(lng[:, :], ln_g[layer, i].partition_broadcast(P)).then_inc(ln_here, 16)
                pool.dma_start(lnb[:, :], ln_b[layer, i].partition_broadcast(P)).then_inc(ln_here, 16)

            load_ln(0, 0)
            link(pool.memset(mhalf[:, :], -0.5))
            link(pool.memset(ones[:, :], 1.0))
            link(pool.memset(tri_incl[:, :], 1.0))
            select(tri_incl[:, :], ALU.is_ge, 0.0, 0, [[1, P]], -1)
            link(pool.memset(mup[:, :], 0.0))
            select(mup[:, :], ALU.is_ge, -BIG, 0, [[1, P]], -1)
            link(pool.memset(mlow[:, :], 0.0))
            select(mlow[:, :], ALU.is_gt, -BIG, 0, [[-1, P]], 1)
            link(pool.memset(masks[:, :, :], 0.0))
            link(pool.memset(masksT[:, :, :], 0.0))
            settle()
            for i in range(7):
                b = 1 << i
                m = masks[:, i, :].rearrange("p (n h b) -> p n h b", h=2, b=b)[:, :, 0, :]
                mt = masksT[:, i, :].rearrange("p (n h b) -> p n h b", h=2, b=b)[:, :, 1, :]
                nb = P // (2 * b)
                link(pool.memset(m, 1.0))
                link(pool.memset(mt, 1.0))
                select(m, ALU.is_ge, 0.0, -b, [[-2 * b, nb], [0, b]], 1)
                select(m, ALU.is_ge, 0.0, 2 * b - 1, [[2 * b, nb], [0, b]], -1)
                select(mt, ALU.is_ge, 0.0, 0, [[-2 * b, nb], [0, b]], 1)
                select(mt, ALU.is_ge, 0.0, b - 1, [[2 * b, nb], [0, b]], -1)
            settle()
            pool.sem_inc(consts, 1)

            def rsqrt(dst, src):
                return pool.tensor_tensor(dst, src, mhalf[:, 0:src.shape[1]], ALU.pow)

            pool.wait_ge(ss_here, 1)
            rsqrt(rqk[:, :, :, :].rearrange("p a h b -> p (a h b)"),
                  ss[:, :, :, :].rearrange("p a h b -> p (a h b)")).then_inc(rqk_here, 1)
            for gr in range(4):
                s = slice(4 * gr, 4 * gr + 4)
                pool.wait_ge(gdiff, gr + 1)
                pool.tensor_tensor(Dm[:, s, :], mlow[:, :].unsqueeze(1).to_broadcast([P, 4, P]),
                                   Nm[:, s, :], ALU.subtract).then_inc(darg, 1)
            for gr in range(4):
                s = slice(4 * gr, 4 * gr + 4)
                pool.wait_ge(dexp, 2 * gr + 1)
                pool.tensor_tensor(Dm[:, s, :], Dm[:, s, :],
                                   nbeta[:, gr // 2, 4 * (gr % 2):4 * (gr % 2) + 4].unsqueeze(2).to_broadcast([P, 4, P]),
                                   ALU.mult).then_inc(dmul, 1)
            pool.wait_ge(kback, 4)
            for c, s in ((0, egl), (1, eg)):
                pool.tensor_tensor(kt[:, c, :, :], kt[:, c, :, :],
                                   s[:, :].unsqueeze(2).to_broadcast([P, H, P]), ALU.mult).then_inc(kscaled, 1)
            pool.wait_ge(z_done, 4)
            pool.wait_ge(bcast_here, 48)
            for b in range(NB):
                v = zn[:, b, :].rearrange("p (h d) -> p h d", h=H)
                pool.tensor_tensor(v, v, nw[:, :].unsqueeze(1).to_broadcast([P, H, P]), ALU.mult).then_inc(zn_done, 1)
            for gr in range(4):
                pool.wait_ge(o_sq, gr + 1)
                s = Tm[:, 4 * gr:4 * gr + 4, :].rearrange("p h d -> p (h d)")
                if gr == 0:
                    pool.wait_ge(zn_done, 2)
                pool.tensor_tensor(s, s, zn[:, gr // 2, 512 * (gr % 2):512 * (gr % 2) + 512], ALU.mult).then_inc(o_z, 1)
                pool.wait_ge(o_ms, gr + 1)
                rsqrt(rms[:, 4 * gr:4 * gr + 4], ms[:, 4 * gr:4 * gr + 4]).then_inc(o_rms, 1)

            def norm(i):
                for b in range(NB):
                    pool.wait_ge(ln_var, 2 * i + b + 1)
                    rsqrt(lnrs[:, b:b + 1], lnve[:, b:b + 1]).then_inc(ln_rstd, 1)
                if i < 3:
                    pool.wait_ge(ln_done, 2 * i + 2)
                    load_ln((i + 1) // 2, (i + 1) % 2)

            norm(0)
            norm(1)
            link(pool.memset(kT2[64:128, :, 0, :], 0.0))
            link(pool.memset(kT2[0:64, :, 1, :], 0.0))
            settle()
            pool.dma_start(sk[:, :], sinks[0].partition_broadcast(P)).then_inc(sink_here, 16)
            for c, (base, op) in enumerate(((0, ALU.is_ge), (P, ALU.is_gt), (0, ALU.is_ge))):
                d = dist[:, c * P:(c + 1) * P]
                link(pool.iota(d, [[-1, P]], base=base, channel_multiplier=1, allow_small_or_imprecise_dtypes=True))
                if c == 1:
                    select(d, ALU.is_gt, BIG, 0, [[1, P]], -1)
                else:
                    select(d, ALU.is_ge, BIG, 0, [[-1, P]], 1)
            settle()
            pool.sem_inc(consts, 1)
            norm(2)
            link(pool.memset(tri_strict[:, :], 1.0))
            select(tri_strict[:, :], ALU.is_gt, 0.0, 0, [[1, P]], -1)
            for i in range(2):
                link(pool.iota(iota[:, i, :], [[1, P]], base=i * P, channel_multiplier=0,
                               allow_small_or_imprecise_dtypes=True))
            link(pool.iota(rev[:, :], [[-1, E]], base=E, channel_multiplier=0, allow_small_or_imprecise_dtypes=True))
            link(pool.memset(pos[:, :, :], -1.0))
            link(pool.memset(gates[:, :, :], 0.0))
            link(pool.memset(onehT[:, 1, :, :].bitcast(F32), 0.0))
            pool.dma_start(wr[:, :, :], w_router[0].rearrange("(k p) e -> p k e", p=P)).then_inc(sink_here, 16)
            settle()
            pool.sem_inc(consts, 1)
            for i in range(2):
                if i == 1:
                    pool.wait_ge(route_here, 1)
                    full = pool.value_load(cint[0:1, 0:1], min_val=0, max_val=T)
                with (pool.If(full > P) if i == 1 else ExitStack()):
                    if i == 1:
                        pool.wait_ge(scattered, 2 * (E + 1))
                    pool.memset(y_hi[:, :].bitcast(F32), 0.0).then_inc(moe_zero, 1)
                    pool.memset(y_lo[:, :].bitcast(F32), 0.0).then_inc(moe_zero, 1)
            norm(3)

        def scan_moves():
            vn = vb[:, 0, :, :], vb[:, 1, :, :]
            Wt = Dm[:, 0:H, :]
            S = Dm[:, H:2 * H, :]
            return [(vn[0][:, 0:4, :], 0), (vn[0][:, 4:8, :], 1), (Wt[:, 0:4, :], 2), (Wt[:, 4:8, :], 3),
                    (S[:, 0:4, :], 4), (S[:, 4:8, :], 5), (vn[1][:, 0:4, :], 0), (vn[1][:, 4:8, :], 1)]

        @block.scalar
        def _(act):
            def cut_hi(j, it=0):
                act.wait_ge(raw_in[j % RAW], 32 * (j // RAW + 1) + 32 * (PER_IT // RAW) * it)
                if j >= CUT:
                    act.wait_ge(unit_used, j - CUT + 1 + PER_IT * it)
                act.activation(slot(hi, j), slot(raw, j), ACT.Copy).then_inc(hi_ready, 1)

            def used(j, it=0):
                act.wait_ge(unit_used, j + 1 + PER_IT * it)

            def copy(dst, src, scale=1.0):
                return act.activation(dst, src, ACT.Copy, scale=scale)

            def turn(i):
                for q in range(2):
                    act.wait_ge(turned, 2 * i + q + 1)
                    copy(xT_hi[:, 4 * q:4 * q + 4, :], ps[:, 4 + 2 * q:6 + 2 * q, :].rearrange(
                        "p b (k t) -> p (b k) t", k=2)).then_inc(turn_hi, 1)

            act.dma_start(x[:, :, :], x_in[0].rearrange("(b p) d -> p b d", p=P)).then_inc(x_here, 16)
            act.dma_start(wab[:, :, :], w_in[0][:, QKV * P + D:].rearrange("(k p) n -> p k n", p=P)).then_inc(small_here, 16)
            act.dma_start(cw_rows[:, :], conv_w[0].rearrange("a (c p) -> (a c) p", p=P)).then_inc(small_here, 16)
            for j in range(AHEAD):
                cut_hi(j)
            act.wait_ge(small_here, 32)
            copy(wab_hi[:, :, :], wab[:, :, :]).then_inc(ab_cut, 1)
            act.wait_ge(cw_turned, 1)
            copy(cw[:, :], ps[:, 0, 0:TAPS * QKV]).then_inc(cw_here, 1)
            turn(0)
            act.wait_ge(cw_here, 1)

            def silu_of(u):
                act.wait_ge(conv_step, 12 + 6 * (u + 1))
                act.activation(conv[:, 2 * u:2 * u + 2, :], conv[:, 2 * u:2 * u + 2, :], ACT.Silu).then_inc(silu_done, 1)

            for u in range(QKV // 2):
                cut_hi(U_QKV + u + AHEAD)
                used(U_QKV + u)
                for m in range(2):
                    t = 2 * u + m
                    act.activation(conv[:, t, :], ps[:, t % 4, 0:T], ACT.Copy,
                                   scale=cw[:, (TAPS - 1) * QKV + t:(TAPS - 1) * QKV + t + 1]).then_inc(tap_ready, 1)
                silu_of(u)
            act.wait_ge(silu_done, QKV // 2)
            act.activation(Tm[:, :, :].rearrange("p (h b) t -> p h (b t)", b=2), conv[:, 0:H, :], ACT.Square).then_inc(sq_done, 1)
            act.activation(Nm[:, :, :].rearrange("p (h b) t -> p h (b t)", b=2), conv[:, H:2 * H, :], ACT.Square).then_inc(sq_done, 1)
            act.wait_ge(g_dve, 1)
            act.activation(sp[0][:, :, :], ab[:, :, 0:H], ACT.Exp, scale=-1.0).then_inc(g_act, 1)
            act.activation(sp[3][:, :, :], sp[2][:, :, :], ACT.Exp, scale=-1.0).then_inc(g_act, 1)
            act.wait_ge(bcast_here, 48)
            act.activation(ea[:, :], alog[:, :], ACT.Exp).then_inc(g_act, 1)
            for u in range(4):
                cut_hi(U_Z + u + AHEAD)
                if u == 0:
                    act.wait_ge(g_dve, 2)
                    act.activation(sp[5][:, :, :], sp[4][:, :, :], ACT.Ln).then_inc(g_act, 1)
                used(U_Z + u)
                if u % 2 == 1:
                    c = u // 2
                    for b in range(NB):
                        act.activation(zn[:, b, 512 * c:512 * c + 512], ps[:, 4 + 2 * c + b, :],
                                       ACT.Silu).then_inc(z_done, 1)
            act.wait_ge(g_dve, 4)
            act.activation(eg[:, :], G[:, 1, :], ACT.Exp).then_inc(g_act, 1)
            act.activation(egl[:, :], sp[0][:, 0, :], ACT.Exp).then_inc(g_act, 1)
            for gr in range(4):
                s = slice(4 * gr, 4 * gr + 4)
                act.wait_ge(darg, gr + 1)
                act.activation(Dm[:, s, :], Dm[:, s, :], ACT.Exp).then_inc(dexp, 1)
                act.wait_ge(gdiff, 4 + gr + 1)
                act.activation(DT[:, s, :], DT[:, s, :], ACT.Exp).then_inc(dexp, 1)
            act.wait_ge(kv_turned, 8)
            act.activation(conv[:, 2 * H:2 * H + 4, :].rearrange("p h (b t) -> p (h b) t", b=2),
                           ps[:, 2:4, :].rearrange("p b (h c) -> p (b h) c", c=P), ACT.Exp).then_inc(g_act, 1)
            for gr in range(4):
                act.wait_ge(kback, gr + 1)
                copy(conv[:, H + 4 * (gr % 2):H + 4 * (gr % 2) + 4, P * (gr // 2):P * (gr // 2) + P],
                     ps[:, 4 + gr, :].rearrange("p (h t) -> p h t", h=4)).then_inc(kback_taken, 1)
            Pm = conv[:, 2 * H:3 * H, :].rearrange("p h (b t) -> p (h b) t", b=2)
            for q in range(4, 4 * 7):
                s = slice(4 * (q % 4), 4 * (q % 4) + 4)
                act.wait_ge(inv_p, q + 1)
                copy(Pm[:, s, :], ps[:, q % 2, :].rearrange("p (h c) -> p h c", h=4)).then_inc(inv_pc, 1)
            for i, (dst, bank) in enumerate(scan_moves()):
                act.wait_ge(scan_mm, i + 1)
                act.activation(dst, ps[:, bank, :].rearrange("p (h c) -> p h c", h=4), ACT.Copy,
                               scale=-1.0 if i in (2, 3) else 1.0).then_inc(scan_ev, 1)
            for gr in range(4):
                s = slice(4 * gr, 4 * gr + 4)
                act.wait_ge(o_scaled, gr + 1)
                act.activation(Pm[:, s, :], Tm[:, s, :], ACT.Square).then_inc(o_sq, 1)
            turn(1)
            for u in range(4):
                cut_hi(U_OUT + u + AHEAD)
            turn(2)

            def ffn_round(c):
                act.wait_ge(ffn_act, c + 1)
                copy(hT_hi[:, 2 * c:2 * c + 2, :], hf[:, c % 2, :].rearrange("p (m t) -> p m t", m=2)).then_inc(ffn_hi, 1)

            for c in range(FC):
                cut_hi(U_GU + 2 * c + AHEAD)
                used(U_GU + 2 * c)
                act.activation(sg[:, c % 2, :], ps[:, 2 * (c % 3), :], ACT.Silu).then_inc(ffn_silu, 1)
                cut_hi(U_GU + 2 * c + 1 + AHEAD)
                if c >= 1:
                    ffn_round(c - 1)
            ffn_round(FC - 1)
            for u in range(FC):
                cut_hi(U_DOWN + u + AHEAD)
            turn(3)

            cut_hi(U_KV + AHEAD)
            used(U_KV)
            for m in range(2):
                copy(kT2[0:64, 2 * m, 0, :], ps[0:64, m, 0:T]).then_inc(kB_act, 1)
                copy(kT2[64:128, 2 * m, 1, :], ps[0:64, m, 0:T]).then_inc(kB_act, 1)
            cut_hi(U_KV + 1 + AHEAD)
            for u in range(4):
                cut_hi(U_Q + u + AHEAD)
                used(U_Q + u)
                for m in range(2):
                    t = 2 * u + m
                    copy(qT[:, t, :], ps[:, 4 + t % 4, 0:T], scale=float(HD) ** -0.5).then_inc(qB_here, 1)
            def exps(gi):
                st = gi % 2
                act.wait_ge(sc_max, gi + 1)
                for b in range(NB):
                    for i in range(GQ):
                        s = sS[:, st, i, 0:P] if b == 0 else sS[:, st, i, P:3 * P]
                        act.activation(s, s, ACT.Exp, bias=nmax[:, st, b, i:i + 1],
                                       accum_out=ssum[:, st, b, i:i + 1])
                act.activation(ske[:, st, :, :], ske[:, st, :, :], ACT.Exp).then_inc(sc_exp, 1)

            exps(0)
            for gi in range(HKV):
                if gi + 1 < HKV:
                    exps(gi + 1)
                for r in range(3):
                    act.wait_ge(pt_mm, 3 * gi + r + 1)
                    copy(pT[:, 4 * r:4 * r + 4, :], ps[:, 6, :].rearrange("p (h q) -> p h q", h=4)).then_inc(pt_taken, 1)
                act.wait_ge(pv_mm, gi + 1)
                copy(xT_hi[:, 2 * gi:2 * gi + 2, :], ps[:, 7, :].rearrange("p (k t) -> p k t", k=2)).then_inc(pv_hi, 1)
            for u in range(4):
                cut_hi(U_O + u + AHEAD)

            act.wait_ge(sink_here, 32)
            copy(wr_hi[:, :, :], wr[:, :, :]).then_inc(wr_cut, 1)
            act.wait_ge(ln_done, 6)
            copy(x3_hi[:, :, :], x[:, :, :]).then_inc(x3_cut, 1)
            turn(4)
            act.wait_ge(w2_arg, 1)
            act.activation(gw[:, :, 1:2], gw[:, :, 0:1], ACT.Exp).then_inc(w2_here, 1)

            def experts(p):
                base = U_MOE + p * E * PER_E

                def slots(ge, it, par):
                    act.wait_ge(gathered, 9 * p + ge + 1 + 2 * it)
                    copy(onehT[:, par, :, :], ps[:, 4, 0:2 * P].rearrange("p (b t) -> p b t", b=2))
                    copy(gslot[:, par:par + 1], ps[:, 5, 0:1]).then_inc(slots_here, 1)
                    copy(xg_hi[:, :, :], ps[:, 6:8, :].rearrange("p b (k s) -> p (b k) s", k=4)).then_inc(xg_hi_here, 1)

                def round_h(c, it, b):
                    gc = 88 * p + 11 * b + c
                    act.wait_ge(ff_turned, gc + 1 + 22 * it)
                    copy(hE_hi[:, 2 * c:2 * c + 2, :], ps[:, 6 + gc % 2, 0:2 * P].rearrange(
                        "p (m s) -> p m s", m=2)).then_inc(h_hi, 1)

                slots(0, 0, 0)
                with act.Fori(0, TURNS) as it:
                    for b in range(2):
                        for l in range(PER_E):
                            j = base + PER_E * b + l
                            if l < PER_E - 1:
                                cut_hi(j + AHEAD, it)
                            used(j, it)
                            if l < 2 * FC and l % 2 == 1:
                                c = l // 2
                                gc = 88 * p + 11 * b + c
                                act.activation(sgE[:, gc % 2, :], ps[:, gc % 2, 0:256], ACT.Silu).then_inc(silu_here, 1)
                                if c >= 1:
                                    round_h(c - 1, it, b)
                            elif l == 2 * FC:
                                round_h(FC - 1, it, b)
                            elif l == 2 * FC + 2:
                                slots(b + 1, it, (b + 1) % 2)
                            elif l == PER_E - 1:
                                act.wait_ge(slots_here, 9 * p + b + 1 + 2 * it)
                                act.activation(y_hi[:, :], ps[:, 2:4, :].rearrange("p b n -> p (b n)"), ACT.Copy,
                                               scale=gslot[:, b:b + 1]).then_inc(y_hi_here, 1)
                                cut_hi(j + AHEAD, it)

            experts(0)
            act.wait_ge(route_here, 1)
            full = act.value_load(cint[0:1, 0:1], min_val=0, max_val=T)
            with act.If(full > P):
                experts(1)


        @block.vector
        def _(dve):
            n = [0]

            def link(ins):
                n[0] += 1
                ins.then_inc(dve_chain, 1)

            def settle():
                dve.wait_ge(dve_chain, n[0])

            def step(ins):
                link(ins)
                settle()

            def cut_lo(j, it=0):
                dve.wait_ge(hi_ready, j + 1 + PER_IT * it)
                dve.tensor_tensor(slot(lo, j), slot(raw, j), slot(hi, j).bitcast(F32), ALU.subtract).then_inc(lo_ready, 1)

            def used(j, it=0):
                dve.wait_ge(unit_used, j + 1 + PER_IT * it)

            def turn(i):
                for q in range(2):
                    dve.wait_ge(turn_hi, 2 * i + q + 1)
                    s = xT_hi[:, 4 * q:4 * q + 4, :].bitcast(F32)
                    dve.tensor_tensor(xT_lo[:, 4 * q:4 * q + 4, :],
                                      ps[:, 4 + 2 * q:6 + 2 * q, :].rearrange("p b (k t) -> p (b k) t", k=2),
                                      s, ALU.subtract).then_inc(turn_lo, 1)

            def norm(i, bank):
                for b in range(NB):
                    if bank is not None:
                        step(dve.scalar_tensor_tensor(out=x[:, b, :], in0=x[:, b, :], scalar=ALPHA,
                                                      in1=ps[:, bank + 2 * b:bank + 2 * b + 2, :].rearrange("p b n -> p (b n)"),
                                                      op0=ALU.mult, op1=ALU.add))
                    for q in range(2):
                        link(dve.bn_stats(bnst[:, b, q, :], x[:, b, 512 * q:512 * q + 512]))
                    settle()
                    step(dve.bn_aggr(bnmv[:, b, :], bnst[:, b, :, :].rearrange("p q s -> p (q s)")))
                    dve.tensor_scalar(lnve[:, b:b + 1], bnmv[:, b, 1:2], 1e-5, None, ALU.add).then_inc(ln_var, 1)
                dve.wait_ge(ln_here, 32 * (i + 1))
                for b in range(NB):
                    dve.wait_ge(ln_rstd, 2 * i + b + 1)
                    step(dve.tensor_scalar(x[:, b, :], x[:, b, :], bnmv[:, b, 0:1], lnrs[:, b:b + 1],
                                           ALU.subtract, ALU.mult))
                    step(dve.tensor_tensor(x[:, b, :], x[:, b, :], lng[:, :], ALU.mult))
                    dve.tensor_tensor(x[:, b, :], x[:, b, :], lnb[:, :], ALU.add).then_inc(ln_done, 1)

            def over(v, width=P):
                return v.unsqueeze(2).to_broadcast([P, v.shape[1], width])

            dve.sem_inc(conv_step, 12)
            dve.sem_inc(act_here, 2)
            dve.sem_inc(h_here, 2)
            dve.sem_inc(y_here, 1)
            dve.sem_inc(acc_added, 2)
            for j in range(AHEAD):
                cut_lo(j)
            dve.wait_ge(ab_cut, 1)
            dve.tensor_tensor(wab_lo[:, :, :], wab[:, :, :], wab_hi[:, :, :].bitcast(F32), ALU.subtract).then_inc(ab_cut, 1)
            turn(0)
            dve.wait_ge(ab_mm, 1)
            dve.tensor_copy(ab[:, :, :], ps[:, 7, 0:4 * H].rearrange("p (b n) -> p b n", b=NB)).then_inc(ab_here, 1)
            dve.wait_ge(cw_here, 1)

            for u in range(QKV // 2):
                cut_lo(U_QKV + u + AHEAD)
                for d in range(1, TAPS):
                    for m in range(2):
                        t = 2 * u + m
                        if d == 1:
                            dve.wait_ge(tap_ready, t + 1)
                        else:
                            dve.wait_ge(conv_step, 12 + 6 * u + 2 * (d - 2) + m + 1)
                        w = (TAPS - 1 - d) * QKV + t
                        dve.scalar_tensor_tensor(out=conv[:, t, d:T], in0=ps[:, t % 4, 0:T - d], scalar=cw[:, w:w + 1],
                                                 in1=conv[:, t, d:T], op0=ALU.mult, op1=ALU.add).then_inc(conv_step, 1)
            dve.wait_ge(ab_here, 1)
            dve.wait_ge(bcast_here, 48)
            step(dve.tensor_tensor(sp[1][:, :, :], ab[:, :, H:2 * H], dtb[:, :].unsqueeze(1).to_broadcast([P, NB, H]), ALU.add))
            dve.scalar_tensor_tensor(out=sp[2][:, :, :], in0=sp[1][:, :, :], scalar=-1.0, in1=sp[1][:, :, :],
                                     op0=ALU.mult, op1=ALU.max).then_inc(g_dve, 1)
            cut_lo(U_Z + AHEAD)
            dve.wait_ge(g_act, 2)
            link(dve.tensor_scalar(sp[0][:, :, :], sp[0][:, :, :], 1.0, None, ALU.add))
            dve.tensor_scalar(sp[4][:, :, :], sp[3][:, :, :], 1.0, None, ALU.add).then_inc(g_dve, 1)
            settle()
            step(dve.reciprocal(beta[:, :, :], sp[0][:, :, :]))
            link(dve.tensor_scalar(nbeta[:, :, :], beta[:, :, :], -1.0, None, ALU.mult))
            cut_lo(U_Z + 1 + AHEAD)
            dve.wait_ge(g_dve, 2)
            link(dve.scalar_tensor_tensor(out=sp[3][:, :, :], in0=sp[4][:, :, :], scalar=-1.0, in1=sp[3][:, :, :],
                                          op0=ALU.add, op1=ALU.subtract))
            step(dve.reciprocal(sp[2][:, :, :], sp[4][:, :, :]))
            step(dve.tensor_tensor(sp[3][:, :, :], sp[3][:, :, :], sp[2][:, :, :], ALU.mult))
            dve.wait_ge(g_act, 4)
            step(dve.tensor_tensor(sp[5][:, :, :], sp[5][:, :, :], sp[3][:, :, :], ALU.subtract))
            step(dve.scalar_tensor_tensor(out=sp[1][:, :, :], in0=sp[1][:, :, :], scalar=0.0, in1=sp[5][:, :, :],
                                          op0=ALU.max, op1=ALU.add))
            dve.scalar_tensor_tensor(out=g[:, :, :], in0=sp[1][:, :, :], scalar=-1.0,
                                     in1=ea[:, :].unsqueeze(1).to_broadcast([P, NB, H]),
                                     op0=ALU.mult, op1=ALU.mult).then_inc(g_dve, 1)
            cut_lo(U_Z + 2 + AHEAD)
            cut_lo(U_Z + 3 + AHEAD)
            dve.wait_ge(ss_mm, 1)
            dve.tensor_scalar(ss[:, :, :, :].rearrange("p a h b -> p (a h b)"), ps[:, 7, 0:4 * H], 1e-6, None,
                              ALU.add).then_inc(ss_here, 1)
            dve.wait_ge(g_pe, 1)
            step(dve.tensor_copy(G[:, :, :], ps[:, 6, 0:2 * H].rearrange("p (b h) -> p b h", b=NB)))
            dve.tensor_tensor(sp[0][:, 0, :], ps[:, 6, 2 * H:3 * H], G[:, 0, :], ALU.subtract).then_inc(g_dve, 1)
            for gr in range(4):
                s = slice(4 * gr, 4 * gr + 4)
                dve.wait_ge(g_pe, 2 + gr)
                dve.tensor_tensor(Nm[:, s, :], ps[:, gr, :].rearrange("p (h c) -> p h c", h=4),
                                  over(G[:, gr // 2, 4 * (gr % 2):4 * (gr % 2) + 4]), ALU.subtract).then_inc(gdiff, 1)
            for gr in range(4):
                s = slice(4 * gr, 4 * gr + 4)
                dve.wait_ge(gdiff, gr + 1)
                dve.tensor_tensor(DT[:, s, :], Nm[:, s, :], mup[:, :].unsqueeze(1).to_broadcast([P, 4, P]),
                                  ALU.add).then_inc(gdiff, 1)
            dve.wait_ge(g_act, 5)
            dve.tensor_tensor(eg[:, :], eg[:, :], beta[:, 1, :], ALU.mult).then_inc(g_dve, 1)
            dve.wait_ge(rqk_here, 1)
            for i in range(8):
                gr, hs = i % 4, slice(4 * (i % 2), 4 * (i % 2) + 4)
                b = gr // 2
                dve.wait_ge(kv_turned, i + 1)
                src = ps[:, 4 + i % 2, :].rearrange("p (h d) -> p h d", h=4)
                if i < 4:
                    dve.tensor_tensor(kt[:, b, hs, :], src, over(rqk[:, 1, hs, b]), ALU.mult).then_inc(kv_taken, 1)
                else:
                    dve.tensor_tensor(vb[:, b, hs, :], src, over(beta[:, b, hs]), ALU.mult).then_inc(kv_taken, 1)
            dve.wait_ge(darg, 4)
            dve.wait_ge(gdiff, 8)
            link(dve.tensor_copy(Tm[:, :, :], ident[:, :].unsqueeze(1).to_broadcast([P, NB * H, P])))
            link(dve.tensor_copy(Nm[:, :, :], ident[:, :].unsqueeze(1).to_broadcast([P, NB * H, P])))
            for gr in range(4):
                s = slice(4 * gr, 4 * gr + 4)
                dve.wait_ge(kk_mm, gr + 1)
                dve.wait_ge(dmul, gr + 1)
                dve.tensor_tensor(Dm[:, s, :], ps[:, 2 * (gr % 2), :].rearrange("p (h c) -> p h c", h=4), Dm[:, s, :],
                                  ALU.mult).then_inc(kk_taken, 1)
                dve.wait_ge(dexp, 2 * gr + 2)
                dve.tensor_tensor(DT[:, s, :], ps[:, 2 * (gr % 2) + 1, :].rearrange("p (h c) -> p h c", h=4), DT[:, s, :],
                                  ALU.mult).then_inc(kk_taken, 1)
            dve.wait_ge(g_act, 7)
            dve.tensor_tensor(conv[:, 0:H, P:T], conv[:, 0:H, P:T],
                              conv[:, 2 * H:2 * H + 4, :].rearrange("p h (b t) -> p (h b) t", b=2), ALU.mult).then_inc(qg_here, 1)
            settle()
            for q in range(4 * 7):
                s = slice(4 * (q % 4), 4 * (q % 4) + 4)
                lv = q // 4
                mk = masks[:, lv, :].bitcast(U32).unsqueeze(1).to_broadcast([P, 4, P])
                mt = masksT[:, lv, :].bitcast(U32).unsqueeze(1).to_broadcast([P, 4, P])
                if lv == 0:
                    dve.wait_ge(inv_p, q + 1)
                    dve.wait_ge(kk_taken, 2 * q + 1)
                    dve.copy_predicated(Tm[:, s, :], mk, Dm[:, s, :])
                    dve.copy_predicated(Nm[:, s, :], mt, ps[:, q % 2, :].rearrange("p (h c) -> p h c", h=4)).then_inc(inv_rc, 1)
                else:
                    dve.wait_ge(inv_r, q - 3)
                    if lv < 6:
                        dve.copy_predicated(Tm[:, s, :], mk, ps[:, 2 + q % 2, :].rearrange("p (h c) -> p h c", h=4))
                    dve.copy_predicated(Nm[:, s, :], mt, ps[:, 4 + q % 2, :].rearrange("p (h c) -> p h c", h=4)).then_inc(inv_rc, 1)
            for gr in range(4):
                s = slice(4 * gr, 4 * gr + 4)
                dve.wait_ge(o_mm, gr + 1)
                bank = (6, 7, 2, 3)[gr]
                dve.scalar_tensor_tensor(out=Tm[:, s, :], in0=ps[:, bank, :].rearrange("p (h c) -> p h c", h=4),
                                         scalar=float(DK) ** -0.5, in1=over(rqk[:, 0, 4 * (gr % 2):4 * (gr % 2) + 4, gr // 2]),
                                         op0=ALU.mult, op1=ALU.mult).then_inc(o_scaled, 1)
            Pm = conv[:, 2 * H:3 * H, :].rearrange("p h (b t) -> p (h b) t", b=2)
            for gr in range(4):
                s = slice(4 * gr, 4 * gr + 4)
                dve.wait_ge(o_sq, gr + 1)
                dve.tensor_reduce(ms[:, s], Pm[:, s, :], AX.X, ALU.add).then_inc(o_sum, 1)
                dve.wait_ge(o_sum, gr + 1)
                dve.tensor_scalar(ms[:, s], ms[:, s], 1.0 / DK, 1e-6, ALU.mult, ALU.add).then_inc(o_ms, 1)
            for gr in range(4):
                s = slice(4 * gr, 4 * gr + 4)
                dve.wait_ge(o_z, gr + 1)
                dve.wait_ge(o_rms, gr + 1)
                dve.tensor_tensor(Tm[:, s, :], Tm[:, s, :], over(rms[:, s]), ALU.mult).then_inc(o_done, 1)
            turn(1)
            for u in range(4):
                cut_lo(U_OUT + u + AHEAD)
            used(U_OUT + 3)
            norm(0, 0)
            turn(2)

            def ffn_rest(c):
                dve.wait_ge(ffn_hi, c + 1)
                s = slice(2 * c, 2 * c + 2)
                dve.tensor_tensor(hT_lo[:, s, :], hf[:, c % 2, :].rearrange("p (m t) -> p m t", m=2),
                                  hT_hi[:, s, :].bitcast(F32), ALU.subtract).then_inc(ffn_lo, 1)

            for c in range(FC):
                cut_lo(U_GU + 2 * c + AHEAD)
                if c >= 1:
                    ffn_rest(c - 1)
                cut_lo(U_GU + 2 * c + 1 + AHEAD)
                used(U_GU + 2 * c + 1)
                dve.wait_ge(ffn_silu, c + 1)
                if c >= 2:
                    dve.wait_ge(ffn_lo, c - 1)
                dve.tensor_tensor(hf[:, c % 2, :], ps[:, 2 * (c % 3) + 1, :], sg[:, c % 2, :], ALU.mult).then_inc(ffn_act, 1)
            ffn_rest(FC - 1)
            for u in range(FC):
                cut_lo(U_DOWN + u + AHEAD)
            used(U_DOWN + FC - 1)
            norm(1, 4)
            turn(3)

            cut_lo(U_KV + AHEAD)
            used(U_KV)
            for m in range(2):
                dve.tensor_copy(kT2[0:64, 2 * m + 1, 0, :], ps[64:128, m, 0:T]).then_inc(kB_dve, 1)
                dve.tensor_copy(kT2[64:128, 2 * m + 1, 1, :], ps[64:128, m, 0:T]).then_inc(kB_dve, 1)
            cut_lo(U_KV + 1 + AHEAD)
            used(U_KV + 1)
            dve.tensor_copy(vB[:, :, :], ps[:, 2:4, 0:HKV * HD]).then_inc(vB_here, 1)
            for u in range(4):
                cut_lo(U_Q + u + AHEAD)
            dve.wait_ge(sink_here, 16)
            dve.wait_ge(consts, 3)

            def scores(gi):
                st = gi % 2
                dve.wait_ge(sc_mm, gi + 1)
                if gi >= 2:
                    dve.wait_ge(pt_mm, 3 * (gi - 1))
                for i in range(GQ):
                    slope = 2.0 ** (-8.0 * (GQ * gi + i + 1) / HQ)
                    dve.scalar_tensor_tensor(out=sS[:, st, i, 0:P], in0=dist[:, 0:P], scalar=-slope,
                                             in1=ps[:, 3 * st, i * P:(i + 1) * P], op0=ALU.mult, op1=ALU.add)
                    last = dve.scalar_tensor_tensor(out=sS[:, st, i, P:3 * P], in0=dist[:, P:3 * P], scalar=-slope,
                                                    in1=ps[:, 3 * st + 1 + i // 2, (i % 2) * T:(i % 2) * T + T],
                                                    op0=ALU.mult, op1=ALU.add)
                last.then_inc(sc_bias, 1)
                dve.wait_ge(sc_bias, gi + 1)
                link(dve.tensor_reduce(smax[:, st, 0, :], sS[:, st, :, 0:P], AX.X, ALU.max))
                step(dve.tensor_reduce(smax[:, st, 1, :], sS[:, st, :, P:3 * P], AX.X, ALU.max))
                skb = sk[:, GQ * gi:GQ * gi + GQ].unsqueeze(1).to_broadcast([P, NB, GQ])
                step(dve.tensor_tensor(smax[:, st, :, :], smax[:, st, :, :], skb, ALU.max))
                link(dve.tensor_scalar(nmax[:, st, :, :], smax[:, st, :, :], -1.0, None, ALU.mult))
                dve.tensor_tensor(ske[:, st, :, :], skb, smax[:, st, :, :], ALU.subtract).then_inc(sc_max, 1)

            def probs(gi):
                st = gi % 2
                dve.wait_ge(sc_exp, gi + 1)
                step(dve.tensor_tensor(ssum[:, st, :, :], ssum[:, st, :, :], ske[:, st, :, :], ALU.add))
                step(dve.reciprocal(sinv[:, st, :, :], ssum[:, st, :, :]))
                dve.tensor_tensor(sS[:, st, :, 0:P], sS[:, st, :, 0:P], over(sinv[:, st, 0, :]), ALU.mult)
                dve.tensor_tensor(sS[:, st, :, P:3 * P], sS[:, st, :, P:3 * P], over(sinv[:, st, 1, :], 2 * P),
                                  ALU.mult).then_inc(sc_prob, 1)

            def attended(gi):
                dve.wait_ge(pv_hi, gi + 1)
                s = slice(2 * gi, 2 * gi + 2)
                dve.tensor_tensor(xT_lo[:, s, :], ps[:, 7, :].rearrange("p (k t) -> p k t", k=2),
                                  xT_hi[:, s, :].bitcast(F32), ALU.subtract).then_inc(pv_lo, 1)

            scores(0)
            for gi in range(HKV):
                if gi + 1 < HKV:
                    scores(gi + 1)
                probs(gi)
                if gi >= 1:
                    attended(gi - 1)
            attended(HKV - 1)
            for u in range(4):
                cut_lo(U_O + u + AHEAD)
            used(U_O + 3)
            norm(2, 0)

            dve.wait_ge(wr_cut, 1)
            dve.tensor_tensor(wr_lo[:, :, :], wr[:, :, :], wr_hi[:, :, :].bitcast(F32), ALU.subtract).then_inc(wr_cut, 1)
            dve.wait_ge(x3_cut, 1)
            dve.tensor_tensor(x3_lo[:, :, :], x[:, :, :], x3_hi[:, :, :].bitcast(F32), ALU.subtract).then_inc(x3_cut, 1)
            turn(4)
            dve.wait_ge(turned, 10)
            link(dve.tensor_scalar(x[:, :, :], x[:, :, :], ALPHA, None, ALU.mult))
            dve.wait_ge(lg_mm, 1)
            step(dve.tensor_copy(lg[:, :, :], ps[:, 0, 0:2 * E].rearrange("p (b e) -> p b e", b=NB)))

            def first_max(src, m, oh):
                bc = [P, NB, E]
                step(dve.tensor_reduce(m[:, :, :], src[:, :, :], AX.X, ALU.max))
                step(dve.tensor_tensor(eq[:, :, :], src[:, :, :], m[:, :, :].to_broadcast(bc), ALU.is_equal))
                step(dve.tensor_tensor(eq[:, :, :], eq[:, :, :], rev[:, :].unsqueeze(1).to_broadcast(bc), ALU.mult))
                step(dve.tensor_reduce(rr[:, :, :], eq[:, :, :], AX.X, ALU.max))
                step(dve.tensor_tensor(oh[:, :, :], eq[:, :, :], rr[:, :, :].to_broadcast(bc), ALU.is_equal))

            dve.wait_ge(consts, 4)
            first_max(lg, m1, oh1)
            step(dve.scalar_tensor_tensor(out=lg2[:, :, :], in0=oh1[:, :, :], scalar=-3.0e38, in1=lg[:, :, :],
                                          op0=ALU.mult, op1=ALU.add))
            first_max(lg2, m2, oh2)
            dve.tensor_tensor(gw[:, :, 0:1], m2[:, :, :], m1[:, :, :], ALU.subtract).then_inc(w2_arg, 1)
            dve.tensor_tensor(sel[:, :, :], oh1[:, :, :], oh2[:, :, :], ALU.add).then_inc(sel_here, 1)
            dve.wait_ge(w2_here, 1)
            step(dve.tensor_scalar(gw[:, :, 2:3], gw[:, :, 1:2], 1.0, None, ALU.add))
            step(dve.reciprocal(gw[:, :, 2:3], gw[:, :, 2:3]))
            step(dve.tensor_tensor(gw[:, :, 3:4], gw[:, :, 1:2], gw[:, :, 2:3], ALU.mult))
            for b in range(NB):
                step(dve.tensor_scalar(gates[:, b, 0:E], oh1[:, b, :], gw[:, b, 2:3], None, ALU.mult))
                step(dve.scalar_tensor_tensor(out=gates[:, b, 0:E], in0=oh2[:, b, :], scalar=gw[:, b, 3:4],
                                              in1=gates[:, b, 0:E], op0=ALU.mult, op1=ALU.add))
            dve.wait_ge(pos_mm, 1)
            step(dve.scalar_tensor_tensor(out=lg2[:, :, :], in0=ps[:, 1, 0:2 * E].rearrange("p (b e) -> p b e", b=NB),
                                          scalar=1.0, in1=sel[:, :, :], op0=ALU.add, op1=ALU.mult))
            step(dve.tensor_scalar(pos[:, :, 0:E], lg2[:, :, :], -1.0, None, ALU.add))
            step(dve.tensor_reduce(cmax[:, :], ps[:, 1, 2 * E:3 * E], AX.X, ALU.max))
            dve.tensor_copy(cint[:, :], cmax[:, :]).then_inc(route_here, 1)

            def experts(p):
                base = U_MOE + p * E * PER_E

                def build(ge, it):
                    dve.wait_ge(gathered, 9 * p + ge + 2 * it) if (p or ge) else None
                    e = ge + 2 * it
                    for b in range(NB):
                        last = dve.tensor_scalar(oneh[:, b, :], iota[:, p, :], pos[:, b, bass.ds(e, 1)], None, ALU.is_equal)
                    last.then_inc(oneh_here, 1)

                def rest_xg(ge, it):
                    dve.wait_ge(xg_hi_here, 9 * p + ge + 1 + 2 * it)
                    dve.tensor_tensor(xg_lo[:, :, :], ps[:, 6:8, :].rearrange("p b (k s) -> p (b k) s", k=4),
                                      xg_hi[:, :, :].bitcast(F32), ALU.subtract).then_inc(xg_here, 1)

                def rest_h(c, it, b):
                    gc = 88 * p + 11 * b + c
                    dve.wait_ge(h_hi, gc + 1 + 22 * it)
                    dve.tensor_tensor(hE_lo[:, 2 * c:2 * c + 2, :],
                                      ps[:, 6 + gc % 2, 0:2 * P].rearrange("p (m s) -> p m s", m=2),
                                      hE_hi[:, 2 * c:2 * c + 2, :].bitcast(F32), ALU.subtract).then_inc(h_here, 1)

                def add(s, it, b):
                    dve.wait_ge(scattered, 18 * p + 2 * s + b + 1 + 4 * it)
                    dve.wait_ge(acc_added, 18 * p + 2 * s + b + 1 + 4 * it)
                    bank = 4 if b == 0 else 2
                    dve.tensor_tensor(x[:, b, :], x[:, b, :], ps[:, bank:bank + 2, :].rearrange("p b n -> p (b n)"),
                                      ALU.add).then_inc(acc_added, 1)

                build(0, 0)
                rest_xg(0, 0)
                with dve.Fori(0, TURNS) as it:
                    for b in range(2):
                        for l in range(PER_E):
                            j = base + PER_E * b + l
                            if l < PER_E - 1:
                                cut_lo(j + AHEAD, it)
                            if l < 2 * FC and l % 2 == 1:
                                c = l // 2
                                gc = 88 * p + 11 * b + c
                                used(j, it)
                                dve.wait_ge(silu_here, gc + 1 + 22 * it)
                                dve.tensor_tensor(actE[:, gc % 2, :], sgE[:, gc % 2, :], ps[:, gc % 2, 256:512],
                                                  ALU.mult).then_inc(act_here, 1)
                                if c >= 1:
                                    rest_h(c - 1, it, b)
                            elif l in (4, 6):
                                add(b, it, l // 2 - 2)
                            elif l == 10:
                                build(b + 1, it)
                            elif l == 2 * FC:
                                rest_h(FC - 1, it, b)
                            elif l == 2 * FC + 2:
                                rest_xg(b + 1, it)
                            elif l == PER_E - 1:
                                dve.wait_ge(y_hi_here, 8 * p + b + 1 + 2 * it)
                                dve.scalar_tensor_tensor(out=y_lo[:, :], in0=ps[:, 2:4, :].rearrange("p b n -> p (b n)"),
                                                         scalar=gslot[:, b:b + 1], in1=y_hi[:, :].bitcast(F32),
                                                         op0=ALU.mult, op1=ALU.subtract).then_inc(y_here, 1)
                                cut_lo(j + AHEAD, it)
                add(E, 0, 0)
                add(E, 0, 1)
                dve.wait_ge(acc_added, 18 * p + 20)

            settle()
            experts(0)
            full = dve.value_load(cint[0:1, 0:1], min_val=0, max_val=T)
            with dve.If(full > P):
                experts(1)
            norm(3, None)

        @block.tensor
        def _(pe):
            def mm(dst, lhsT, rhs, start, stop):
                return pe.matmul(dst, lhsT, rhs, start=start, stop=stop)

            def ready(j, it=0):
                pe.wait_ge(lo_ready, j + 1 + PER_IT * it)

            def turn(i, src):
                for q in range(2):
                    for k in range(4 * q, 4 * q + 4):
                        for b in range(NB):
                            last = pe.transpose(ps[:, 4 + k // 2, (k % 2) * T + b * P:(k % 2) * T + b * P + P],
                                                src(b, k), ident[:, :])
                    last.then_inc(turned, 1)

            def turned_in(i):
                pe.wait_ge(turn_lo, 2 * i + 2)

            def to_channels(j, banks):
                ready(j)
                w_hi = slot(hi, j).rearrange("p (k n) -> p k n", k=KD)
                w_lo = slot(lo, j).rearrange("p (k n) -> p k n", k=KD)
                for m in range(2):
                    dst = banks[m]
                    c = slice(m * P, m * P + P)
                    for k in range(KD):
                        mm(dst, w_hi[:, k, c], xT_hi[:, k, :], k == 0, False)
                        mm(dst, w_hi[:, k, c], xT_lo[:, k, :], False, False)
                        last = mm(dst, w_lo[:, k, c], xT_hi[:, k, :], False, k == KD - 1)
                last.then_inc(unit_used, 1)

            def to_tokens(j, k0, nk, first, final, dsts, a_hi, a_lo):
                ready(j)
                w_hi = slot(hi, j).rearrange("p (k n) -> p k n", k=nk)
                w_lo = slot(lo, j).rearrange("p (k n) -> p k n", k=nk)
                width = dsts[0][0].shape[1]
                for kk in range(nk):
                    for b in range(NB):
                        t = slice(b * P, b * P + P)
                        for a, w, p in ((a_hi, w_hi, 0), (a_hi, w_lo, 1), (a_lo, w_hi, 2)):
                            for i, dst in enumerate(dsts[b]):
                                last = mm(dst, a[:, k0 + kk, t], w[:, kk, i * width:(i + 1) * width],
                                          first and kk == 0 and p == 0, final and kk == nk - 1 and p == 2)
                last.then_inc(unit_used, 1)

            def halves(bank):
                return [[ps[:, bank + 2 * b + i, :] for i in range(2)] for b in range(NB)]

            pe.wait_ge(consts, 1)
            pe.wait_ge(small_here, 32)
            pe.transpose(ps[:, 0, 0:TAPS * QKV], cw_rows[:, :], ident[0:TAPS * QKV, 0:TAPS * QKV]).then_inc(cw_turned, 1)
            pe.wait_ge(x_here, 16)
            turn(0, lambda b, k: x[:, b, k * P:(k + 1) * P])
            turned_in(0)
            pe.wait_ge(ab_cut, 2)
            for b in range(NB):
                dst = ps[:, 7, 2 * H * b:2 * H * (b + 1)]
                t = slice(b * P, b * P + P)
                for k in range(KD):
                    mm(dst, xT_hi[:, k, t], wab_hi[:, k, :], k == 0, False)
                    mm(dst, xT_hi[:, k, t], wab_lo[:, k, :], False, False)
                    last = mm(dst, xT_lo[:, k, t], wab_hi[:, k, :], False, k == KD - 1)
            last.then_inc(ab_mm, 1)
            pe.wait_ge(cw_here, 1)
            for u in range(QKV // 2):
                pe.wait_ge(conv_step, 6 * u + 6)
                to_channels(U_QKV + u, [ps[:, (2 * u + m) % 4, 0:T] for m in range(2)])
            pe.wait_ge(ab_here, 1)
            for u in range(4):
                to_tokens(U_Z + u, 4 * (u % 2), 4, u % 2 == 0, u % 2 == 1,
                          [[ps[:, 4 + 2 * (u // 2) + b, :]] for b in range(NB)], xT_hi, xT_lo)

            pe.wait_ge(sq_done, 2)
            pe.wait_ge(z_done, 4)
            pe.wait_ge(consts, 2)
            for a, sq in enumerate((Tm, Nm)):
                for h in range(H):
                    for b in range(NB):
                        c = (a * H + h) * NB + b
                        last = mm(ps[:, 7, c:c + 1], sq[:, h * NB + b, :], ones[:, 0:1], True, True)
            last.then_inc(ss_mm, 1)
            pe.wait_ge(g_dve, 3)
            for b in range(NB):
                mm(ps[:, 6, b * H:(b + 1) * H], tri_incl[:, :], g[:, b, :], True, True)
            mm(ps[:, 6, 2 * H:3 * H], ones[:, :], g[:, 0, :], True, True).then_inc(g_pe, 1)
            pe.wait_ge(conv_step, 12 + 3 * QKV)
            for gr in range(4):
                for i in range(4):
                    last = mm(ps[:, gr, i * P:(i + 1) * P],
                              g[:, gr // 2, 4 * (gr % 2) + i:4 * (gr % 2) + i + 1].to_broadcast([P, P]),
                              tri_incl[:, :], True, True)
                last.then_inc(g_pe, 1)
            pe.wait_ge(silu_done, QKV // 2)
            for i in range(8):
                gr = i % 4
                if i >= 2:
                    pe.wait_ge(kv_taken, i - 1)
                for q in range(4):
                    h = H * (1 + i // 4) + 4 * (gr % 2) + q
                    last = pe.transpose(ps[:, 4 + i % 2, q * P:(q + 1) * P], conv[:, h, P * (gr // 2):P * (gr // 2) + P],
                                        ident[:, :])
                last.then_inc(kv_turned, 1)
            pe.wait_ge(kv_taken, 8)
            pe.wait_ge(g_dve, 4)
            for gr in range(4):
                for q in range(4):
                    last = pe.transpose(ps[:, 4 + gr, q * P:(q + 1) * P], kt[:, gr // 2, 4 * (gr % 2) + q, :], ident[:, :])
                last.then_inc(kback, 1)
            pe.wait_ge(g_act, 7)
            pe.wait_ge(gdiff, 4)
            for gr in range(4):
                pe.wait_ge(kback_taken, gr + 1)
                if gr >= 2:
                    pe.wait_ge(kk_taken, 2 * (gr - 1))
                t = slice(P * (gr // 2), P * (gr // 2) + P)
                for rhs, bank in ((H, 2 * (gr % 2)), (0, 2 * (gr % 2) + 1)):
                    for i in range(4):
                        h = 4 * (gr % 2) + i
                        last = mm(ps[:, bank, i * P:(i + 1) * P], conv[:, H + h, t], conv[:, rhs + h, t], True, True)
                last.then_inc(kk_mm, 1)

            Pm = conv[:, 2 * H:3 * H, :].rearrange("p h (b t) -> p (h b) t", b=2)

            def first(q):
                if q < 4:
                    if q < 2:
                        pe.wait_ge(kk_taken, 8)
                        pe.wait_ge(qg_here, 1)
                    else:
                        pe.wait_ge(inv_rc, q - 1)
                else:
                    pe.wait_ge(inv_rc, q - 1 if q < 6 else q - 3)
                    if q >= 6:
                        pe.wait_ge(inv_pc, q - 5)
                for i in range(4):
                    n_ = 4 * (q % 4) + i
                    dst = ps[:, q % 2, i * P:(i + 1) * P]
                    if q < 4:
                        last = pe.transpose(dst, Dm[:, n_, :], ident[:, :])
                    else:
                        last = mm(dst, Dm[:, n_, :], Nm[:, n_, :], True, True)
                last.then_inc(inv_p, 1)

            def second(q):
                pe.wait_ge(inv_pc, q - 3)
                if q >= 6:
                    pe.wait_ge(inv_rc, q - 1)
                for i in range(4):
                    n_ = 4 * (q % 4) + i
                    c = slice(i * P, (i + 1) * P)
                    if q < 24:
                        mm(ps[:, 2 + q % 2, c], Pm[:, n_, :], Tm[:, n_, :], True, True)
                    last = mm(ps[:, 4 + q % 2, c], Tm[:, n_, :], Pm[:, n_, :], True, True)
                last.then_inc(inv_r, 1)

            for q in range(4 * 7):
                first(q)
                if q >= 5:
                    second(q - 1)
            second(27)

            W_, S_ = Dm[:, 0:H, :], Dm[:, H:2 * H, :]
            pe.wait_ge(inv_rc, 28)
            pe.wait_ge(kscaled, 2)

            def group(bank, products, s):
                for i in range(4):
                    for n_, (lhsT, rhs) in enumerate(products(i)):
                        last = mm(ps[:, bank, i * P:(i + 1) * P], lhsT, rhs, n_ == 0, n_ == len(products(i)) - 1)
                last.then_inc(s, 1)

            for hh in range(2):
                group(hh, lambda i: [(Nm[:, 4 * hh + i, :], vb[:, 0, 4 * hh + i, :])], scan_mm)
            for hh in range(2):
                group(2 + hh, lambda i: [(kt[:, 1, 4 * hh + i, :], Nm[:, H + 4 * hh + i, :])], scan_mm)
            for hh in range(2):
                pe.wait_ge(scan_ev, hh + 1)
                group(4 + hh, lambda i: [(kt[:, 0, 4 * hh + i, :], vb[:, 0, 4 * hh + i, :])], scan_mm)
            for hh in range(2):
                group(6 + hh, lambda i: [(DT[:, 4 * hh + i, :], vb[:, 0, 4 * hh + i, :])], o_mm)
            for hh in range(2):
                pe.wait_ge(scan_ev, 4 + hh + 1)
                group(hh, lambda i: [(Nm[:, H + 4 * hh + i, :], vb[:, 1, 4 * hh + i, :]),
                                     (W_[:, 4 * hh + i, :], S_[:, 4 * hh + i, :])], scan_mm)
            for hh in range(2):
                pe.wait_ge(scan_ev, 6 + hh + 1)
                group(2 + hh, lambda i: [(conv[:, 4 * hh + i, P:T], S_[:, 4 * hh + i, :]),
                                         (DT[:, H + 4 * hh + i, :], vb[:, 1, 4 * hh + i, :])], o_mm)
            pe.wait_ge(o_done, 4)
            turn(1, lambda b, k: Tm[:, b * H + k, :])
            turned_in(1)
            for u in range(4):
                to_tokens(U_OUT + u, 2 * u, 2, u == 0, u == 3, halves(0), xT_hi, xT_lo)
            pe.wait_ge(ln_done, 2)
            turn(2, lambda b, k: x[:, b, k * P:(k + 1) * P])
            turned_in(2)

            for c in range(FC):
                if c >= 3:
                    pe.wait_ge(ffn_act, c - 2)
                for t in range(2):
                    bank = 2 * (c % 3) + t
                    to_channels(U_GU + 2 * c + t, [ps[:, bank, m * T:(m + 1) * T] for m in range(2)])
            pe.wait_ge(ffn_act, FC - 2)
            for u in range(FC):
                pe.wait_ge(ffn_lo, u + 1)
                to_tokens(U_DOWN + u, 2 * u, 2, u == 0, u == FC - 1, halves(4), hT_hi, hT_lo)
            pe.wait_ge(ln_done, 4)
            turn(3, lambda b, k: x[:, b, k * P:(k + 1) * P])
            turned_in(3)

            to_channels(U_KV, [ps[:, m, 0:T] for m in range(2)])
            to_tokens(U_KV + 1, 0, KD, True, True, [[ps[:, 2 + b, 0:HKV * HD]] for b in range(NB)], xT_hi, xT_lo)
            for u in range(4):
                if u >= 2:
                    pe.wait_ge(qB_here, 2 * (u - 1))
                to_channels(U_Q + u, [ps[:, 4 + (2 * u + m) % 4, 0:T] for m in range(2)])
            pe.wait_ge(kB_act, 4)
            pe.wait_ge(kB_dve, 4)
            pe.wait_ge(consts, 3)
            pe.wait_ge(vB_here, 1)
            pe.wait_ge(qB_here, 8)

            def scores(gi):
                if gi >= 2:
                    pe.wait_ge(sc_bias, gi - 1)
                st = 3 * (gi % 2)
                for i in range(GQ):
                    q = qT[:, 2 * gi + i // 2, :]
                    k = kT2[:, gi, i % 2, :]
                    mm(ps[:, st, i * P:(i + 1) * P], q[:, 0:P], k[:, 0:P], True, True)
                    last = mm(ps[:, st + 1 + i // 2, (i % 2) * T:(i % 2) * T + T], q[:, P:T], k, True, True)
                last.then_inc(sc_mm, 1)

            def attend(gi):
                pe.wait_ge(sc_prob, gi + 1)
                for r in range(3):
                    if gi or r:
                        pe.wait_ge(pt_taken, 3 * gi + r)
                    for i in range(GQ):
                        last = pe.transpose(ps[:, 6, i * P:(i + 1) * P], sS[:, gi % 2, i, r * P:(r + 1) * P], ident[:, :])
                    last.then_inc(pt_mm, 1)
                pe.wait_ge(pt_taken, 3 * gi + 3)
                if gi:
                    pe.wait_ge(pv_lo, gi)
                v = slice(gi * HD, (gi + 1) * HD)
                for i in range(GQ):
                    o = 64 * (i % 2)
                    c = (i // 2) * T
                    mm(ps[o:o + 64, 7, c:c + P], vB[:, 0, v], pT[:, i, :], True, True)
                    mm(ps[o:o + 64, 7, c + P:c + T], vB[:, 0, v], pT[:, 4 + i, :], True, False)
                    last = mm(ps[o:o + 64, 7, c + P:c + T], vB[:, 1, v], pT[:, 8 + i, :], False, True)
                last.then_inc(pv_mm, 1)

            scores(0)
            for gi in range(HKV):
                if gi + 1 < HKV:
                    scores(gi + 1)
                attend(gi)
            pe.wait_ge(pv_lo, HKV)
            pe.wait_ge(sc_bias, HKV)
            for u in range(4):
                to_tokens(U_O + u, 2 * u, 2, u == 0, u == 3, halves(0), xT_hi, xT_lo)
            pe.wait_ge(ln_done, 6)
            turn(4, lambda b, k: x[:, b, k * P:(k + 1) * P])
            turned_in(4)
            pe.wait_ge(wr_cut, 2)
            for b in range(NB):
                dst = ps[:, 0, E * b:E * (b + 1)]
                t = slice(b * P, b * P + P)
                for k in range(KD):
                    mm(dst, xT_hi[:, k, t], wr_hi[:, k, :], k == 0, False)
                    mm(dst, xT_hi[:, k, t], wr_lo[:, k, :], False, False)
                    last = mm(dst, xT_lo[:, k, t], wr_hi[:, k, :], False, k == KD - 1)
            last.then_inc(lg_mm, 1)
            pe.wait_ge(sel_here, 1)
            pe.wait_ge(consts, 4)
            mm(ps[:, 1, 0:E], tri_strict[:, :], sel[:, 0, :], True, True)
            mm(ps[:, 1, E:2 * E], tri_strict[:, :], sel[:, 1, :], True, False)
            mm(ps[:, 1, E:2 * E], ones[:, :], sel[:, 0, :], False, True)
            for b in range(NB):
                last = mm(ps[:, 1, 2 * E:3 * E], ones[:, :], sel[:, b, :], b == 0, b == 1)
            last.then_inc(pos_mm, 1)

            def experts(p):
                base = U_MOE + p * E * PER_E

                def gather(ge, it):
                    pe.wait_ge(oneh_here, 9 * p + ge + 1 + 2 * it)
                    for b in range(NB):
                        pe.transpose(ps[:, 4, b * P:(b + 1) * P], oneh[:, b, :].bitcast(F32), ident[:, :])
                    for b in range(NB):
                        mm(ps[:, 5, 0:1], oneh[:, b, :].bitcast(F32), gates[:, b, bass.ds(ge + 2 * it, 1)], b == 0, b == 1)
                    for k in range(KD):
                        dst = ps[:, 6 + k // 4, (k % 4) * P:(k % 4) * P + P]
                        c = slice(k * P, k * P + P)
                        for n_, (part, b) in enumerate(((x3_hi, 0), (x3_hi, 1), (x3_lo, 0), (x3_lo, 1))):
                            last = mm(dst, part[:, b, c], oneh[:, b, :], n_ == 0, n_ == 3)
                    last.then_inc(gathered, 1)

                def turn_h(c, it, b):
                    gc = 88 * p + 11 * b + c
                    pe.wait_ge(act_here, gc + 3 + 22 * it)
                    pe.wait_ge(h_here, gc + 1 + 22 * it)
                    for m in range(2):
                        last = pe.transpose(ps[:, 6 + gc % 2, m * P:(m + 1) * P], actE[:, gc % 2, m * P:(m + 1) * P],
                                            ident[:, :])
                    last.then_inc(ff_turned, 1)

                def scatter(s, it, par):
                    pe.wait_ge(y_here, 8 * p + s + 1 + 2 * it)
                    for b in range(NB):
                        for n_, part in enumerate((y_hi, y_lo)):
                            for i in range(2):
                                bank = (4 if b == 0 else 2) + i
                                last = mm(ps[:, bank, :], onehT[:, par, b, :], part[:, i * 512:(i + 1) * 512],
                                          n_ == 0, n_ == 1)
                        last.then_inc(scattered, 1)

                if p == 0:
                    pe.wait_ge(route_here, 1)
                pe.wait_ge(x3_cut, 2)
                gather(0, 0)
                pe.wait_ge(xg_here, 9 * p + 1)
                pe.wait_ge(moe_zero, 2 * p + 2)
                with pe.Fori(0, TURNS) as it:
                    for b in range(2):
                        for l in range(PER_E):
                            j = base + PER_E * b + l
                            if l < 2 * FC:
                                c = l // 2
                                gc = 88 * p + 11 * b + c
                                if l == 0:
                                    pe.wait_ge(xg_here, 9 * p + b + 1 + 2 * it)
                                if l % 2 == 0:
                                    pe.wait_ge(act_here, gc + 1 + 22 * it)
                                ready(j, it)
                                w_hi = slot(hi, j).rearrange("p (k n) -> p k n", k=4)
                                w_lo = slot(lo, j).rearrange("p (k n) -> p k n", k=4)
                                for kk in range(4):
                                    k = 4 * (l % 2) + kk
                                    mm(ps[:, gc % 2, :], xg_hi[:, k, :], w_hi[:, kk, :], k == 0, False)
                                    mm(ps[:, gc % 2, :], xg_hi[:, k, :], w_lo[:, kk, :], False, False)
                                    last = mm(ps[:, gc % 2, :], xg_lo[:, k, :], w_hi[:, kk, :], False, k == KD - 1)
                                last.then_inc(unit_used, 1)
                                if l % 2 == 1 and c >= 1:
                                    turn_h(c - 1, it, b)
                                if l == 3:
                                    scatter(b, it, (b + 1) % 2)
                            else:
                                d = l - 2 * FC
                                pe.wait_ge(h_here, 88 * p + 11 * b + d + 3 + 22 * it)
                                if d == 0:
                                    pe.wait_ge(acc_added, 18 * p + 2 * b + 4 + 4 * it)
                                ready(j, it)
                                w_hi = slot(hi, j).rearrange("p (k n) -> p k n", k=2)
                                w_lo = slot(lo, j).rearrange("p (k n) -> p k n", k=2)
                                for kk in range(2):
                                    k = 2 * d + kk
                                    for n_, (a, w) in enumerate(((hE_hi, w_hi), (hE_hi, w_lo), (hE_lo, w_hi))):
                                        for i in range(2):
                                            last = mm(ps[:, 2 + i, :], a[:, k, :], w[:, kk, i * 512:(i + 1) * 512],
                                                      k == 0 and n_ == 0, k == 2 * FC - 1 and n_ == 2)
                                last.then_inc(unit_used, 1)
                                if d == 0:
                                    turn_h(FC - 1, it, b)
                                if d == 1:
                                    pe.wait_ge(h_here, 88 * p + 11 * b + FC + 2 + 22 * it)
                                    gather(b + 1, it)
                scatter(E, 0, (E + 1) % 2)

            experts(0)
            full = pe.value_load(cint[0:1, 0:1], min_val=0, max_val=T)
            with pe.If(full > P):
                experts(1)


_INS = ["x", "dn_w_in", "dn_conv_w", "dn_a_log", "dn_dt_bias", "dn_norm_w", "dn_w_out", "w_kv_shared", "sw_w_q",
        "sw_sinks", "sw_w_out", "ffn_w_gu", "ffn_w_down", "moe_w_router", "moe_w_gu", "moe_w_down", "ln_g", "ln_b"]


def kernel(**inputs):
    import numpy as np
    import concourse.bacc as bacc
    from concourse.bass_utils import run_bass_kernel_spmd

    nc = bacc.Bacc("TRN2", target_bir_lowering=False, num_devices=1)
    arrays, args = {}, []
    for name in _INS:
        a = np.ascontiguousarray(inputs[name])
        arrays[f"in_{name}"] = a
        args.append(nc.dram_tensor(f"in_{name}", a.shape, mybir.dt.from_np(a.dtype), kind="ExternalInput").ap())
    args.append(nc.dram_tensor("out_0", inputs["x"].shape, F32, kind="ExternalOutput").ap())
    trunk(nc, *args)
    return run_bass_kernel_spmd(nc, [arrays], core_ids=[0]).results[0]["out_0"]
```

```python
from contextlib import ExitStack

import concourse.bass as bass
from concourse import mybir

ALU = mybir.AluOpType
ACT = mybir.ActivationFunctionType
AX = mybir.AxisListType
F32 = mybir.dt.float32
F32R = mybir.dt.float32r
U32 = mybir.dt.uint32
I32 = mybir.dt.int32

P = 128
BIG = 1.0e30

UNIT = 2048
RAW = 6
CUT = 3
AHEAD = 3


def trunk(nc, x_in, w_in, conv_w, a_log, dt_bias, norm_w, w_out, w_kv, w_q, sinks, w_o, w_gu, w_down,
          w_router, moe_gu, moe_down, ln_g, ln_b, out):
    _, T, D = x_in.shape
    NB = T // P
    KD = D // P
    H = a_log.shape[1]
    DK = P
    TAPS = conv_w.shape[1]
    QKV = conv_w.shape[2] // P
    HQ = sinks.shape[1]
    HKV = 4
    GQ = HQ // HKV
    HD = w_kv.shape[1] // (2 * HKV)
    FF = w_down.shape[1]
    FC = FF // 256
    E = w_router.shape[2]
    ALPHA = float(4 ** 0.25)
    assert (T, D, H, FF, E, NB) == (256, 1024, 8, 2816, 8, 2) and HD == 64

    U_QKV = 0
    U_Z = U_QKV + QKV // 2
    U_OUT = U_Z + 4
    U_GU = U_OUT + 4
    U_DOWN = U_GU + 2 * FC
    U_KV = U_DOWN + FC
    U_Q = U_KV + 2
    U_O = U_Q + 4
    U_MOE = U_O + 4
    PER_E = 3 * FC
    PER_IT = 2 * PER_E
    TURNS = E // 2
    assert PER_IT % RAW == 0 and PER_IT % CUT == 0

    ctx = ExitStack()
    with ctx:
        def sb(name, shape, dt=F32, where=None):
            return (where or ctx).enter_context(nc.sbuf_tensor(name, shape, dt))

        def sem(name):
            return ctx.enter_context(nc.semaphore(name))

        raw = sb("raw", [P, RAW, UNIT])
        hi = sb("hi", [P, CUT, UNIT], F32R)
        lo = sb("lo", [P, CUT, UNIT], F32R)
        x = sb("x", [P, NB, D])
        lng = sb("lng", [P, D])
        lnb = sb("lnb", [P, D])
        ident = sb("ident", [P, P])
        ones = sb("ones", [P, P])
        tri_incl = sb("tri_incl", [P, P])
        mhalf = sb("mhalf", [P, NB * H])
        bnst = sb("bnst", [P, NB, 2, 6])
        bnmv = sb("bnmv", [P, NB, 2])
        lnve = sb("lnve", [P, NB])
        lnrs = sb("lnrs", [P, NB])
        ps = ctx.enter_context(nc.psum_tensor("ps", [P, 8, 512], F32))

        with ExitStack() as a:
            Dm = sb("Dm", [P, NB * H, P], where=a)
            DT = sb("DT", [P, NB * H, P], where=a)
            conv = sb("conv", [P, QKV, T], where=a)
            zn = sb("zn", [P, NB, D], where=a)
            kt = sb("kt", [P, NB, H, P], where=a)
            vb = sb("vb", [P, NB, H, P], where=a)
            Tm = sb("Tm", [P, NB * H, P], where=a)
            Nm = sb("Nm", [P, NB * H, P], where=a)
            masks = sb("masks", [P, 7, P], where=a)
            masksT = sb("masksT", [P, 2, P], where=a)
            cw_rows = sb("cw_rows", [TAPS * QKV, P], where=a)
            cw = sb("cw", [P, TAPS * QKV], where=a)
            wab = sb("wab", [P, KD, 2 * H], where=a)
            wab_hi = sb("wab_hi", [P, KD, 2 * H], F32R, where=a)
            wab_lo = sb("wab_lo", [P, KD, 2 * H], F32R, where=a)
            alog = sb("alog", [P, H], where=a)
            dtb = sb("dtb", [P, H], where=a)
            nw = sb("nw", [P, DK], where=a)
            eG = sb("eG", [P, H, P], where=a)
            abT = sb("abT", [2 * H, T], where=a)
            ab = sb("ab", [P, NB, 2 * H], where=a)
            beta = sb("beta", [P, NB, H], where=a)
            nbeta = sb("nbeta", [P, NB, H], where=a)
            g = sb("g", [P, NB, H], where=a)
            G = sb("G", [P, NB, H], where=a)
            sp = [sb(f"sp{i}", [P, NB, H], where=a) for i in range(6)]
            ea = sb("ea", [P, H], where=a)
            egl = sb("egl", [P, H], where=a)
            eg = sb("eg", [P, H], where=a)
            ss = sb("ss", [P, 2, H, NB], where=a)
            rk = sb("rk", [P, H, NB], where=a)
            ms = sb("ms", [P, NB * H], where=a)
            fo = sb("fo", [P, NB * H], where=a)
        xT_hi = sb("xT_hi", [P, KD, T], F32R)
        xT_lo = sb("xT_lo", [P, KD, T], F32R)
        with ExitStack() as a:
            hT_hi = sb("hT_hi", [P, 2 * FC, T], F32R, where=a)
            hT_lo = sb("hT_lo", [P, 2 * FC, T], F32R, where=a)
            sg = sb("sg", [P, 2, 512], where=a)
            hf = sb("hf", [P, 2, 512], where=a)
        with ExitStack() as a:
            kT2 = sb("kT2", [P, HKV, 2, T], where=a)
            vB = sb("vB", [P, NB, HKV * HD], where=a)
            qT = sb("qT", [P, KD, T], where=a)
            dist = sb("dist", [P, 3 * P], where=a)
            sS = sb("sS", [P, 2, GQ, 3 * P], where=a)
            pT = sb("pT", [P, 3 * GQ, P], where=a)
            oT_hi = sb("oT_hi", [P, KD, T], F32R, where=a)
            oT_lo = sb("oT_lo", [P, KD, T], F32R, where=a)
            sk = sb("sk", [P, HQ], where=a)
            smax = sb("smax", [P, 2, NB, GQ], where=a)
            nmax = sb("nmax", [P, 2, NB, GQ], where=a)
            ske = sb("ske", [P, 2, NB, GQ], where=a)
            ssum = sb("ssum", [P, 2, NB, GQ], where=a)
            sinv = sb("sinv", [P, 2, NB, GQ], where=a)
        x3_hi = sb("x3_hi", [P, NB, D], F32R)
        x3_lo = sb("x3_lo", [P, NB, D], F32R)
        xg_hi = sb("xg_hi", [P, KD, P], F32R)
        xg_lo = sb("xg_lo", [P, KD, P], F32R)
        sgE = sb("sgE", [P, 2, 256])
        actE = sb("actE", [P, 2, 256])
        hE_hi = sb("hE_hi", [P, 2 * FC, P], F32R)
        hE_lo = sb("hE_lo", [P, 2 * FC, P], F32R)
        y_hi = sb("y_hi", [P, D], F32R)
        y_lo = sb("y_lo", [P, D], F32R)
        oneh = sb("oneh", [P, NB, P], F32R)
        onehT = sb("onehT", [P, 2, NB, P], F32R)
        gslot = sb("gslot", [P, 2])
        iota = sb("iota", [P, 2, P])
        tri_strict = sb("tri_strict", [P, P])
        wr = sb("wr", [P, KD, E])
        wr_hi = sb("wr_hi", [P, KD, E], F32R)
        wr_lo = sb("wr_lo", [P, KD, E], F32R)
        rev = sb("rev", [P, E])
        lgT = sb("lgT", [E, T])
        lg = sb("lg", [P, NB, E])
        lg2 = sb("lg2", [P, NB, E])
        eq = sb("eq", [P, NB, E])
        oh1 = sb("oh1", [P, NB, E])
        oh2 = sb("oh2", [P, NB, E])
        sel = sb("sel", [P, NB, E])
        m1 = sb("m1", [P, NB, 1])
        m2 = sb("m2", [P, NB, 1])
        rr = sb("rr", [P, NB, 1])
        gw = sb("gw", [P, NB, 4])
        pos = sb("pos", [P, NB, E + 1])
        gates = sb("gates", [P, NB, E + 1])
        cmax = sb("cmax", [P, 1])
        cint = sb("cint", [P, 1], I32)

        raw_in = [sem(f"raw_in{i}") for i in range(RAW)]
        hi_ready, lo_ready, unit_used = sem("hi_ready"), sem("lo_ready"), sem("unit_used")
        x_here, small_here, bcast_here = sem("x_here"), sem("small_here"), sem("bcast_here")
        ln_here, sink_here = sem("ln_here"), sem("sink_here")
        consts = sem("consts")
        turned, turn_hi, turn_lo = sem("turned"), sem("turn_hi"), sem("turn_lo")
        ln_var, ln_rstd, ln_done = sem("ln_var"), sem("ln_rstd"), sem("ln_done")
        conv_step, tap_ready, silu_done = sem("conv_step"), sem("tap_ready"), sem("silu_done")
        z_done, cw_turned, cw_here = sem("z_done"), sem("cw_turned"), sem("cw_here")
        ab_cut, ab_mm, ab_here = sem("ab_cut"), sem("ab_mm"), sem("ab_here")
        g_act, g_dve, g_pe = sem("g_act"), sem("g_dve"), sem("g_pe")
        block0_done, x_scaled = sem("block0_done"), sem("x_scaled")
        q_turned, q_squared, k_squared, ss_here, rk_here = (
            sem(n) for n in ("q_turned", "q_squared", "k_squared", "ss_here", "rk_here"))
        kv_turned, kv_taken = sem("kv_turned"), sem("kv_taken")
        gdiff, gmin, decay_here, dmul = sem("gdiff"), sem("gmin"), sem("decay_here"), sem("dmul")
        kback, kback_taken = sem("kback"), sem("kback_taken")
        kk_mm, kk_taken = sem("kk_mm"), sem("kk_taken")
        kscaled, qg_here = sem("kscaled"), sem("qg_here")
        inv_id, inv_p, inv_pc, inv_r, inv_rc = (sem(f"inv_{n}") for n in ("id", "p", "pc", "r", "rc"))
        scan_mm, scan_ev = sem("scan_mm"), sem("scan_ev")
        o_mm, o_sq, o_ms, o_rms, o_done = (sem(f"o_{n}") for n in ("mm", "sq", "ms", "rms", "done"))
        zn_done = sem("zn_done")
        ffn_silu, ffn_act, ffn_hi, ffn_lo = sem("ffn_silu"), sem("ffn_act"), sem("ffn_hi"), sem("ffn_lo")
        kB_act, kB_dve, vB_here, qB_here = sem("kB_act"), sem("kB_dve"), sem("vB_here"), sem("qB_here")
        sc_mm, sc_max, sc_exp, sc_prob = sem("sc_mm"), sem("sc_max"), sem("sc_exp"), sem("sc_prob")
        pt_mm, pt_taken, pv_mm, pv_hi, pv_lo = (sem(f"{n}") for n in ("pt_mm", "pt_taken", "pv_mm", "pv_hi", "pv_lo"))
        sc_bias = sem("sc_bias")
        lgT_here, wab_here = sem("lgT_here"), sem("wab_here")
        wr_cut, x3_cut, lg_mm, sel_here, w2_here = (sem(n) for n in ("wr_cut", "x3_cut", "lg_mm", "sel_here", "w2_here"))
        w2_arg, pos_mm, route_here, moe_zero = (sem(n) for n in ("w2_arg", "pos_mm", "route_here", "moe_zero"))
        oneh_here, gathered, xg_hi_here, xg_here = (sem(n) for n in ("oneh_here", "gathered", "xg_hi_here", "xg_here"))
        slots_here = sem("slots_here")
        silu_here, act_here, ff_turned, h_hi, h_here = (sem(n) for n in ("silu_here", "act_here", "ff_turned", "h_hi", "h_here"))
        y_hi_here, y_here, scattered, acc_added = (sem(n) for n in ("y_hi_here", "y_here", "scattered", "acc_added"))
        out_done = sem("out_done")
        dve_chain, act_chain, pool_chain = sem("dve_chain"), sem("act_chain"), sem("pool_chain")

        def columns(w, n0, n1, width):
            return w[:, n0:n1].rearrange("(k p) (c n) -> c p k n", p=P, n=width)

        qkv_v = columns(w_in[0], 0, QKV * P, 256)
        z_v = w_in[0][:, QKV * P:QKV * P + D].rearrange("(a k p) (c n) -> a c p k n", p=P, k=4, n=512)
        out_v = w_out[0].rearrange("(u k p) n -> u p k n", p=P, k=2)
        gu_v = columns(w_gu[0], 0, 2 * FF, 256)
        down_v = w_down[0].rearrange("(u k p) n -> u p k n", p=P, k=2)
        kv_v = columns(w_kv, 0, 2 * HKV * HD, 256)
        q_v = columns(w_q[0], 0, D, 256)
        o_v = w_o[0].rearrange("(u k p) n -> u p k n", p=P, k=2)
        mgu_v = moe_gu[0].rearrange("e (a k p) (t c n) -> a c e p k t n", p=P, k=4, t=2, n=256)
        mdown_v = moe_down[0].rearrange("e (u k p) n -> u e p k n", p=P, k=2)

        block = ctx.enter_context(nc.Block())

        def slot(buf, j):
            return buf[:, j % (RAW if buf is raw else CUT), :]

        def xT_part(buf, s):
            return buf[:, 4 * (s % 2):4 * (s % 2) + 4, (s // 2) * P:(s // 2) * P + P]

        @block.sync
        def _(sp_):
            def load(j, it, src, view, **dims):
                if j >= RAW:
                    sp_.wait_ge(lo_ready, j - RAW + 1 + PER_IT * it)
                dst = slot(raw, j).rearrange(view, **dims)
                for half in range(2):
                    if len(dst.shape) == 4:
                        d, s = dst[:, :, half, :], src[:, :, half, :]
                    else:
                        k = slice(half * dst.shape[1] // 2, (half + 1) * dst.shape[1] // 2)
                        d, s = dst[:, k, :], src[:, k, :]
                    sp_.dma_start(d, s).then_inc(raw_in[j % RAW], 16)

            for u in range(QKV // 2):
                load(U_QKV + u, 0, qkv_v[u], "p (k n) -> p k n", k=KD)
            for u in range(4):
                load(U_Z + u, 0, z_v[u % 2, u // 2], "p (k n) -> p k n", k=4)
            for u in range(4):
                load(U_OUT + u, 0, out_v[u], "p (k n) -> p k n", k=2)
            for c in range(FC):
                for t in range(2):
                    load(U_GU + 2 * c + t, 0, gu_v[t * FC + c], "p (k n) -> p k n", k=KD)
            for u in range(FC):
                load(U_DOWN + u, 0, down_v[u], "p (k n) -> p k n", k=2)
            for u in range(2):
                load(U_KV + u, 0, kv_v[u], "p (k n) -> p k n", k=KD)
            for u in range(4):
                load(U_Q + u, 0, q_v[u], "p (k n) -> p k n", k=KD)
            for u in range(4):
                load(U_O + u, 0, o_v[u], "p (k n) -> p k n", k=2)

            def expert_unit(base, l, it):
                e = 2 * it + l // PER_E
                if l // PER_E == 2:
                    e = e % E
                u = l % PER_E
                if u < 2 * FC:
                    load(base + l, it, mgu_v[u % 2, u // 2][e], "p (k t n) -> p k t n", k=4, t=2)
                else:
                    load(base + l, it, mdown_v[u - 2 * FC][e], "p (k n) -> p k n", k=2)

            for l in range(AHEAD):
                expert_unit(U_MOE, l, 0)

            def experts(base):
                with sp_.Fori(0, TURNS) as it:
                    for l in range(AHEAD, PER_IT + AHEAD):
                        expert_unit(base, l, it)

            experts(U_MOE)
            sp_.wait_ge(route_here, 1)
            full = sp_.value_load(cint[0:1, 0:1], min_val=0, max_val=T)
            with sp_.If(full > P):
                experts(U_MOE + E * PER_E)
            for b in range(NB):
                sp_.wait_ge(ln_done, 2 * 3 + b + 1)
                sp_.dma_start(out[0].rearrange("(b p) d -> b p d", p=P)[b], x[:, b, :]).then_inc(out_done, 16)
            sp_.wait_ge(out_done, 16 * NB)

        @block.gpsimd
        def _(pool):
            n = [0]

            def link(ins):
                n[0] += 1
                ins.then_inc(pool_chain, 1)

            def settle():
                pool.wait_ge(pool_chain, n[0])

            def select(t, op, fill, base, pattern, mult):
                settle()
                link(pool.affine_select(out=t, in_=t, compare_op=op, fill=fill, base=base,
                                        pattern=pattern, channel_multiplier=mult))

            link(pool.memset(ident[:, :], 0.0))
            select(ident[:, :], ALU.not_equal, 1.0, 0, [[-1, P]], 1)
            settle()
            pool.sem_inc(consts, 1)
            pool.dma_start(alog[:, :], a_log[0].partition_broadcast(P)).then_inc(bcast_here, 16)
            pool.dma_start(dtb[:, :], dt_bias[0].partition_broadcast(P)).then_inc(bcast_here, 16)
            pool.dma_start(nw[:, :], norm_w[0].partition_broadcast(P)).then_inc(bcast_here, 16)

            def load_ln(layer, i):
                pool.dma_start(lng[:, :], ln_g[layer, i].partition_broadcast(P)).then_inc(ln_here, 16)
                pool.dma_start(lnb[:, :], ln_b[layer, i].partition_broadcast(P)).then_inc(ln_here, 16)

            load_ln(0, 0)
            link(pool.memset(mhalf[:, :], -0.5))
            link(pool.memset(ones[:, :], 1.0))
            link(pool.memset(tri_incl[:, :], 1.0))
            select(tri_incl[:, :], ALU.is_ge, 0.0, 0, [[1, P]], -1)
            link(pool.memset(masks[:, :, :], 0.0))
            link(pool.memset(masksT[:, :, :], 0.0))
            settle()
            for i in range(7):
                b = 1 << i
                m = masks[:, i, :].rearrange("p (n h b) -> p n h b", h=2, b=b)[:, :, 0, :]
                nb = P // (2 * b)
                link(pool.memset(m, 1.0))
                select(m, ALU.is_ge, 0.0, -b, [[-2 * b, nb], [0, b]], 1)
                select(m, ALU.is_ge, 0.0, 2 * b - 1, [[2 * b, nb], [0, b]], -1)
                if i >= 5:
                    mt = masksT[:, i - 5, :].rearrange("p (n h b) -> p n h b", h=2, b=b)[:, :, 1, :]
                    link(pool.memset(mt, 1.0))
                    select(mt, ALU.is_ge, 0.0, 0, [[-2 * b, nb], [0, b]], 1)
                    select(mt, ALU.is_ge, 0.0, b - 1, [[2 * b, nb], [0, b]], -1)
            settle()
            pool.sem_inc(consts, 1)

            def rsqrt(dst, src):
                return pool.tensor_tensor(dst, src, mhalf[:, 0:src.shape[1]], ALU.pow)

            pool.wait_ge(decay_here, 4)
            for gr in range(4):
                s = slice(4 * gr, 4 * gr + 4)
                link(pool.tensor_tensor(Tm[:, s, :], Nm[:, s, :], tri_incl[:, :].unsqueeze(1).to_broadcast([P, 4, P]),
                                        ALU.mult))
            settle()
            for gr in range(4):
                s = slice(4 * gr, 4 * gr + 4)
                pool.tensor_tensor(Nm[:, s, :], Nm[:, s, :],
                                   nbeta[:, gr // 2, 4 * (gr % 2):4 * (gr % 2) + 4].unsqueeze(2).to_broadcast([P, 4, P]),
                                   ALU.mult).then_inc(dmul, 1)
            pool.wait_ge(ss_here, 1)
            rsqrt(rk[:, :, :].rearrange("p h b -> p (h b)"), ss[:, 1, :, :].rearrange("p h b -> p (h b)")).then_inc(rk_here, 1)
            pool.wait_ge(kback, 4)
            for c, s in ((0, egl), (1, eg)):
                pool.tensor_tensor(kt[:, c, :, :], kt[:, c, :, :],
                                   s[:, :].unsqueeze(2).to_broadcast([P, H, P]), ALU.mult).then_inc(kscaled, 1)
            pool.wait_ge(g_act, 7)
            pool.wait_ge(kk_mm, 4)
            pool.tensor_tensor(conv[:, 0:H, P:T], conv[:, 0:H, P:T], eG[:, :, :], ALU.mult).then_inc(qg_here, 1)
            pool.wait_ge(z_done, 4)
            pool.wait_ge(bcast_here, 48)
            for b in range(NB):
                v = zn[:, b, :].rearrange("p (h d) -> p h d", h=H)
                pool.tensor_tensor(v, v, nw[:, :].unsqueeze(1).to_broadcast([P, H, P]), ALU.mult).then_inc(zn_done, 1)
            for gr in range(4):
                pool.wait_ge(o_ms, gr + 1)
                rsqrt(fo[:, 4 * gr:4 * gr + 4], ms[:, 4 * gr:4 * gr + 4]).then_inc(o_rms, 1)

            def norm(i):
                for b in range(NB):
                    pool.wait_ge(ln_var, 2 * i + b + 1)
                    rsqrt(lnrs[:, b:b + 1], lnve[:, b:b + 1]).then_inc(ln_rstd, 1)
                if i < 3:
                    pool.wait_ge(ln_done, 2 * i + 2)
                    load_ln((i + 1) // 2, (i + 1) % 2)

            norm(0)
            norm(1)
            link(pool.memset(kT2[64:128, :, 0, :], 0.0))
            link(pool.memset(kT2[0:64, :, 1, :], 0.0))
            settle()
            pool.dma_start(sk[:, :], sinks[0].partition_broadcast(P)).then_inc(sink_here, 16)
            for c, (base, op) in enumerate(((0, ALU.is_ge), (P, ALU.is_gt), (0, ALU.is_ge))):
                d = dist[:, c * P:(c + 1) * P]
                link(pool.iota(d, [[-1, P]], base=base, channel_multiplier=1, allow_small_or_imprecise_dtypes=True))
                if c == 1:
                    select(d, ALU.is_gt, BIG, 0, [[1, P]], -1)
                else:
                    select(d, ALU.is_ge, BIG, 0, [[-1, P]], 1)
            settle()
            pool.sem_inc(consts, 1)
            norm(2)
            link(pool.memset(tri_strict[:, :], 1.0))
            select(tri_strict[:, :], ALU.is_gt, 0.0, 0, [[1, P]], -1)
            for i in range(2):
                link(pool.iota(iota[:, i, :], [[1, P]], base=i * P, channel_multiplier=0,
                               allow_small_or_imprecise_dtypes=True))
            link(pool.iota(rev[:, :], [[-1, E]], base=E, channel_multiplier=0, allow_small_or_imprecise_dtypes=True))
            link(pool.memset(pos[:, :, :], -1.0))
            link(pool.memset(gates[:, :, :], 0.0))
            link(pool.memset(onehT[:, 1, :, :].bitcast(F32), 0.0))
            pool.dma_start(wr[:, :, :], w_router[0].rearrange("(k p) e -> p k e", p=P)).then_inc(sink_here, 16)
            settle()
            pool.sem_inc(consts, 1)
            pool.wait_ge(turned, 4 * 5)
            pool.wait_ge(x3_cut, 2)
            pool.tensor_scalar(x[:, :, :], x[:, :, :], ALPHA, None, ALU.mult).then_inc(x_scaled, 1)
            for i in range(2):
                if i == 1:
                    pool.wait_ge(route_here, 1)
                    full = pool.value_load(cint[0:1, 0:1], min_val=0, max_val=T)
                with (pool.If(full > P) if i == 1 else ExitStack()):
                    if i == 1:
                        pool.wait_ge(scattered, 2 * (E + 1))
                    pool.memset(y_hi[:, :].bitcast(F32), 0.0).then_inc(moe_zero, 1)
                    pool.memset(y_lo[:, :].bitcast(F32), 0.0).then_inc(moe_zero, 1)
            norm(3)

        O_BANK = (6, 7, 2, 3)

        def scan_moves():
            vn = vb[:, 0, :, :], vb[:, 1, :, :]
            Wt = Dm[:, 0:H, :]
            S = Dm[:, H:2 * H, :]
            return [(vn[0][:, 0:4, :], 0), (vn[0][:, 4:8, :], 1), (Wt[:, 0:4, :], 2), (Wt[:, 4:8, :], 3),
                    (S[:, 0:4, :], 4), (S[:, 4:8, :], 5), (vn[1][:, 0:4, :], 0), (vn[1][:, 4:8, :], 1)]

        @block.scalar
        def _(act):
            def cut_hi(j, it=0):
                act.wait_ge(raw_in[j % RAW], 32 * (j // RAW + 1) + 32 * (PER_IT // RAW) * it)
                if j >= CUT:
                    act.wait_ge(unit_used, j - CUT + 1 + PER_IT * it)
                act.activation(slot(hi, j), slot(raw, j), ACT.Copy).then_inc(hi_ready, 1)

            def used(j, it=0):
                act.wait_ge(unit_used, j + 1 + PER_IT * it)

            def copy(dst, src, scale=1.0):
                return act.activation(dst, src, ACT.Copy, scale=scale)

            def turn(i):
                for s in range(4):
                    act.wait_ge(turned, 4 * i + s + 1)
                    copy(xT_part(xT_hi, s), ps[:, 4 + s, :].rearrange("p (k t) -> p k t", k=4)).then_inc(turn_hi, 1)

            for b in range(NB):
                act.dma_start(x[:, b, :], x_in[0].rearrange("(b p) d -> b p d", p=P)[b]).then_inc(x_here, 16)
            act.dma_start(cw_rows[:, :], conv_w[0].rearrange("a (c p) -> (a c) p", p=P)).then_inc(small_here, 16)
            act.dma_start(wab[:, :, :], w_in[0][:, QKV * P + D:].rearrange("(k p) n -> p k n", p=P)).then_inc(wab_here, 16)
            cut_hi(0)
            turn(0)
            act.wait_ge(cw_turned, 1)
            copy(cw[:, :], ps[:, 0, 0:TAPS * QKV]).then_inc(cw_here, 1)
            act.wait_ge(wab_here, 16)
            copy(wab_hi[:, :, :], wab[:, :, :]).then_inc(ab_cut, 1)
            cut_hi(1)
            cut_hi(2)
            act.wait_ge(cw_here, 1)

            def project(u):
                used(U_QKV + u)
                for m in range(2):
                    t = 2 * u + m
                    act.activation(conv[:, t, :], ps[:, t % 4, 0:T], ACT.Copy,
                                   scale=cw[:, (TAPS - 1) * QKV + t:(TAPS - 1) * QKV + t + 1]).then_inc(tap_ready, 1)
                cut_hi(U_QKV + u + AHEAD)
                act.wait_ge(conv_step, 12 + 6 * (u + 1))
                act.activation(conv[:, 2 * u:2 * u + 2, :], conv[:, 2 * u:2 * u + 2, :], ACT.Silu).then_inc(silu_done, 1)

            def squares(which, ready_, done, junk):
                for gr in range(4):
                    b, h0 = gr // 2, 4 * (gr % 2)
                    act.wait_ge(ready_, gr + 1)
                    for i in range(4):
                        last = act.activation(junk(gr, i), ps[:, 4 + gr, i * P:(i + 1) * P], ACT.Square,
                                              accum_out=ss[:, which, h0 + i, b:b + 1])
                    last.then_inc(done, 1)

            project(0)
            project(1)
            act.wait_ge(g_dve, 1)
            act.activation(sp[0][:, :, :], ab[:, :, 0:H], ACT.Exp, scale=-1.0).then_inc(g_act, 1)
            act.activation(sp[3][:, :, :], sp[2][:, :, :], ACT.Exp, scale=-1.0).then_inc(g_act, 1)
            act.wait_ge(bcast_here, 48)
            act.activation(ea[:, :], alog[:, :], ACT.Exp).then_inc(g_act, 1)
            project(2)
            act.wait_ge(g_dve, 2)
            act.activation(sp[5][:, :, :], sp[4][:, :, :], ACT.Ln).then_inc(g_act, 1)
            project(3)
            project(4)
            act.wait_ge(g_dve, 4)
            act.activation(eg[:, :], G[:, 1, :], ACT.Exp).then_inc(g_act, 1)
            act.activation(egl[:, :], sp[0][:, 0, :], ACT.Exp).then_inc(g_act, 1)
            project(5)
            act.wait_ge(gdiff, 4)
            act.activation(eG[:, :, :], ps[:, 6:8, :].rearrange("p b (h c) -> p (b h) c", c=P), ACT.Exp).then_inc(g_act, 1)
            project(6)
            squares(0, q_turned, q_squared, lambda gr, i: ps[:, 4 + gr, i * P:(i + 1) * P])
            project(7)
            for gr in range(4):
                s = slice(4 * gr, 4 * gr + 4)
                act.wait_ge(gmin, gr + 1)
                act.activation(Nm[:, s, :], Nm[:, s, :], ACT.Exp).then_inc(decay_here, 1)
            for u in range(8, 11):
                project(u)
            squares(1, kv_turned, k_squared, lambda gr, i: zn[:, gr // 2, (4 * (gr % 2) + i) * P:(4 * (gr % 2) + i + 1) * P])
            project(11)
            act.wait_ge(k_squared, 4)

            def gate(c):
                for b in range(NB):
                    act.activation(zn[:, b, 512 * c:512 * c + 512], ps[:, 2 * c + b, :], ACT.Silu).then_inc(z_done, 1)

            cut_hi(U_Z + 0 + AHEAD)
            used(U_Z + 1)
            gate(0)
            cut_hi(U_Z + 1 + AHEAD)
            cut_hi(U_Z + 2 + AHEAD)
            for gr in range(4):
                act.wait_ge(kback, gr + 1)
                copy(conv[:, H + 4 * (gr % 2):H + 4 * (gr % 2) + 4, P * (gr // 2):P * (gr // 2) + P],
                     ps[:, 4 + gr, :].rearrange("p (h t) -> p h t", h=4)).then_inc(kback_taken, 1)
            used(U_Z + 3)
            gate(1)
            for gr in range(4):
                act.wait_ge(kk_taken, 2 * gr + 2)
                copy(Tm[:, 4 * gr:4 * gr + 4, :], ident[:, :].unsqueeze(1).to_broadcast([P, 4, P])).then_inc(inv_id, 1)
            cut_hi(U_Z + 3 + AHEAD)
            Pm = conv[:, 2 * H:3 * H, :].rearrange("p h (b t) -> p (h b) t", b=2)
            for q in range(4, 4 * 7):
                s = slice(4 * (q % 4), 4 * (q % 4) + 4)
                act.wait_ge(inv_p, q - 3)
                copy(Pm[:, s, :], ps[:, 4 + q % 2, :].rearrange("p (h c) -> p h c", h=4)).then_inc(inv_pc, 1)
            for i, (dst, bank) in enumerate(scan_moves()):
                act.wait_ge(scan_mm, i + 1)
                act.activation(dst, ps[:, bank, :].rearrange("p (h c) -> p h c", h=4), ACT.Copy,
                               scale=-1.0 if i in (2, 3) else 1.0).then_inc(scan_ev, 1)
            for gr in range(4):
                act.wait_ge(o_mm, gr + 1)
                for i in range(4):
                    n_ = 4 * gr + i
                    last = act.activation(Pm[:, n_, :], ps[:, O_BANK[gr], i * P:(i + 1) * P], ACT.Square,
                                          accum_out=ms[:, n_:n_ + 1])
                last.then_inc(o_sq, 1)
            turn(1)
            for u in range(4):
                cut_hi(U_OUT + u + AHEAD)
            turn(2)

            def ffn_round(c):
                act.wait_ge(ffn_act, c + 1)
                copy(hT_hi[:, 2 * c:2 * c + 2, :], hf[:, c % 2, :].rearrange("p (m t) -> p m t", m=2)).then_inc(ffn_hi, 1)

            for c in range(FC):
                cut_hi(U_GU + 2 * c + AHEAD)
                used(U_GU + 2 * c)
                act.activation(sg[:, c % 2, :], ps[:, 2 * (c % 3), :], ACT.Silu).then_inc(ffn_silu, 1)
                cut_hi(U_GU + 2 * c + 1 + AHEAD)
                if c >= 1:
                    ffn_round(c - 1)
            ffn_round(FC - 1)
            for u in range(FC):
                cut_hi(U_DOWN + u + AHEAD)
            turn(3)

            cut_hi(U_KV + AHEAD)
            used(U_KV)
            for m in range(2):
                copy(kT2[0:64, 2 * m, 0, :], ps[0:64, m, 0:T]).then_inc(kB_act, 1)
                copy(kT2[64:128, 2 * m, 1, :], ps[0:64, m, 0:T]).then_inc(kB_act, 1)
            cut_hi(U_KV + 1 + AHEAD)

            def queries(u):
                used(U_Q + u)
                for m in range(2):
                    copy(qT[:, 2 * u + m, :], ps[:, 3, m * T:(m + 1) * T], scale=float(HD) ** -0.5).then_inc(qB_here, 1)
                cut_hi(U_Q + u + AHEAD)

            def exps(gi):
                st = gi % 2
                act.wait_ge(sc_max, gi + 1)
                for b in range(NB):
                    for i in range(GQ):
                        s = sS[:, st, i, 0:P] if b == 0 else sS[:, st, i, P:3 * P]
                        act.activation(s, s, ACT.Exp, bias=nmax[:, st, b, i:i + 1],
                                       accum_out=ssum[:, st, b, i:i + 1])
                act.activation(ske[:, st, :, :], ske[:, st, :, :], ACT.Exp).then_inc(sc_exp, 1)

            def attend(gi):
                for r in range(3):
                    n_ = 3 * gi + r
                    act.wait_ge(pt_mm, n_ + 1)
                    copy(pT[:, 4 * r:4 * r + 4, :], ps[:, 4 + n_ % 2, :].rearrange("p (h q) -> p h q", h=4)).then_inc(pt_taken, 1)
                act.wait_ge(pv_mm, gi + 1)
                copy(oT_hi[:, 2 * gi:2 * gi + 2, :], ps[:, 6, :].rearrange("p (k t) -> p k t", k=2)).then_inc(pv_hi, 1)

            queries(0)
            exps(0)
            queries(1)
            exps(1)
            queries(2)
            attend(0)
            exps(2)
            queries(3)
            attend(1)
            exps(3)
            attend(2)
            cut_hi(U_O + 0 + AHEAD)
            cut_hi(U_O + 1 + AHEAD)
            attend(3)
            cut_hi(U_O + 2 + AHEAD)
            cut_hi(U_O + 3 + AHEAD)

            act.wait_ge(sink_here, 32)
            copy(wr_hi[:, :, :], wr[:, :, :]).then_inc(wr_cut, 1)
            turn(4)
            copy(x3_hi[:, :, :], x[:, :, :]).then_inc(x3_cut, 1)
            act.wait_ge(w2_arg, 1)
            act.activation(gw[:, :, 1:2], gw[:, :, 0:1], ACT.Exp).then_inc(w2_here, 1)

            def experts(p):
                base = U_MOE + p * E * PER_E

                def slots(ge, it, par):
                    act.wait_ge(gathered, 9 * p + ge + 1 + 2 * it)
                    copy(onehT[:, par, :, :], ps[:, 4, 0:2 * P].rearrange("p (b t) -> p b t", b=2))
                    copy(gslot[:, par:par + 1], ps[:, 5, 0:1]).then_inc(slots_here, 1)
                    copy(xg_hi[:, :, :], ps[:, 6:8, :].rearrange("p b (k s) -> p (b k) s", k=4)).then_inc(xg_hi_here, 1)

                def round_h(c, it, b):
                    gc = 88 * p + 11 * b + c
                    act.wait_ge(ff_turned, gc + 1 + 22 * it)
                    copy(hE_hi[:, 2 * c:2 * c + 2, :], ps[:, 6 + gc % 2, 0:2 * P].rearrange(
                        "p (m s) -> p m s", m=2)).then_inc(h_hi, 1)

                slots(0, 0, 0)
                with act.Fori(0, TURNS) as it:
                    for b in range(2):
                        for l in range(PER_E):
                            j = base + PER_E * b + l
                            if l < PER_E - 1:
                                cut_hi(j + AHEAD, it)
                            used(j, it)
                            if l < 2 * FC and l % 2 == 1:
                                c = l // 2
                                gc = 88 * p + 11 * b + c
                                act.activation(sgE[:, gc % 2, :], ps[:, gc % 2, 0:256], ACT.Silu).then_inc(silu_here, 1)
                                if c >= 1:
                                    round_h(c - 1, it, b)
                            elif l == 2 * FC:
                                round_h(FC - 1, it, b)
                            elif l == 2 * FC + 2:
                                slots(b + 1, it, (b + 1) % 2)
                            elif l == PER_E - 1:
                                act.wait_ge(slots_here, 9 * p + b + 1 + 2 * it)
                                act.activation(y_hi[:, :], ps[:, 2:4, :].rearrange("p b n -> p (b n)"), ACT.Copy,
                                               scale=gslot[:, b:b + 1]).then_inc(y_hi_here, 1)
                                cut_hi(j + AHEAD, it)

            experts(0)
            act.wait_ge(route_here, 1)
            full = act.value_load(cint[0:1, 0:1], min_val=0, max_val=T)
            with act.If(full > P):
                experts(1)


        @block.vector
        def _(dve):
            n = [0]

            def link(ins):
                n[0] += 1
                ins.then_inc(dve_chain, 1)

            def settle():
                dve.wait_ge(dve_chain, n[0])

            def step(ins):
                link(ins)
                settle()

            def cut_lo(j, it=0):
                dve.wait_ge(hi_ready, j + 1 + PER_IT * it)
                dve.tensor_tensor(slot(lo, j), slot(raw, j), slot(hi, j).bitcast(F32), ALU.subtract).then_inc(lo_ready, 1)

            def used(j, it=0):
                dve.wait_ge(unit_used, j + 1 + PER_IT * it)

            def turn(i):
                for s in range(4):
                    dve.wait_ge(turn_hi, 4 * i + s + 1)
                    dve.tensor_tensor(xT_part(xT_lo, s), ps[:, 4 + s, :].rearrange("p (k t) -> p k t", k=4),
                                      xT_part(xT_hi, s).bitcast(F32), ALU.subtract).then_inc(turn_lo, 1)

            def norm(i, bank, last=None):
                for b in range(NB):
                    if bank is not None:
                        if b == 0:
                            dve.wait_ge(block0_done, i + 1)
                        else:
                            used(last)
                        step(dve.scalar_tensor_tensor(out=x[:, b, :], in0=x[:, b, :], scalar=ALPHA,
                                                      in1=ps[:, bank + 2 * b:bank + 2 * b + 2, :].rearrange("p b n -> p (b n)"),
                                                      op0=ALU.mult, op1=ALU.add))
                    for q in range(2):
                        link(dve.bn_stats(bnst[:, b, q, :], x[:, b, 512 * q:512 * q + 512]))
                    settle()
                    step(dve.bn_aggr(bnmv[:, b, :], bnst[:, b, :, :].rearrange("p q s -> p (q s)")))
                    dve.tensor_scalar(lnve[:, b:b + 1], bnmv[:, b, 1:2], 1e-5, None, ALU.add).then_inc(ln_var, 1)
                dve.wait_ge(ln_here, 32 * (i + 1))
                for b in range(NB):
                    step(dve.scalar_tensor_tensor(out=x[:, b, :], in0=x[:, b, :], scalar=bnmv[:, b, 0:1], in1=lng[:, :],
                                                  op0=ALU.subtract, op1=ALU.mult))
                    dve.wait_ge(ln_rstd, 2 * i + b + 1)
                    dve.scalar_tensor_tensor(out=x[:, b, :], in0=x[:, b, :], scalar=lnrs[:, b:b + 1], in1=lnb[:, :],
                                             op0=ALU.mult, op1=ALU.add).then_inc(ln_done, 1)

            def over(v, width=P):
                return v.unsqueeze(2).to_broadcast([P, v.shape[1], width])

            dve.sem_inc(conv_step, 12)
            dve.sem_inc(act_here, 2)
            dve.sem_inc(h_here, 2)
            dve.sem_inc(y_here, 1)
            dve.sem_inc(acc_added, 2)
            cut_lo(0)
            turn(0)
            dve.wait_ge(ab_cut, 1)
            dve.tensor_tensor(wab_lo[:, :, :], wab[:, :, :], wab_hi[:, :, :].bitcast(F32), ALU.subtract).then_inc(ab_cut, 1)
            cut_lo(1)
            cut_lo(2)
            dve.wait_ge(cw_here, 1)

            def project(u):
                for d in range(1, TAPS):
                    for m in range(2):
                        t = 2 * u + m
                        if d == 1:
                            dve.wait_ge(tap_ready, t + 1)
                        else:
                            dve.wait_ge(conv_step, 12 + 6 * u + 2 * (d - 2) + m + 1)
                        w = (TAPS - 1 - d) * QKV + t
                        dve.scalar_tensor_tensor(out=conv[:, t, d:T], in0=ps[:, t % 4, 0:T - d], scalar=cw[:, w:w + 1],
                                                 in1=conv[:, t, d:T], op0=ALU.mult, op1=ALU.add).then_inc(conv_step, 1)
                cut_lo(U_QKV + u + AHEAD)

            project(0)
            dve.wait_ge(ab_mm, 1)
            dve.tensor_copy(abT[:, :], ps[0:2 * H, 7, 0:T]).then_inc(ab_here, 1)
            project(1)
            dve.wait_ge(ab_mm, 2)
            step(dve.tensor_copy(ab[:, :, :], ps[:, 7, 0:4 * H].rearrange("p (b n) -> p b n", b=NB)))
            dve.wait_ge(bcast_here, 48)
            step(dve.tensor_tensor(sp[1][:, :, :], ab[:, :, H:2 * H], dtb[:, :].unsqueeze(1).to_broadcast([P, NB, H]), ALU.add))
            dve.scalar_tensor_tensor(out=sp[2][:, :, :], in0=sp[1][:, :, :], scalar=-1.0, in1=sp[1][:, :, :],
                                     op0=ALU.mult, op1=ALU.max).then_inc(g_dve, 1)
            project(2)
            dve.wait_ge(g_act, 2)
            link(dve.tensor_scalar(sp[0][:, :, :], sp[0][:, :, :], 1.0, None, ALU.add))
            dve.tensor_scalar(sp[4][:, :, :], sp[3][:, :, :], 1.0, None, ALU.add).then_inc(g_dve, 1)
            settle()
            step(dve.reciprocal(beta[:, :, :], sp[0][:, :, :]))
            link(dve.tensor_scalar(nbeta[:, :, :], beta[:, :, :], -1.0, None, ALU.mult))
            dve.wait_ge(g_dve, 2)
            link(dve.scalar_tensor_tensor(out=sp[3][:, :, :], in0=sp[4][:, :, :], scalar=-1.0, in1=sp[3][:, :, :],
                                          op0=ALU.add, op1=ALU.subtract))
            step(dve.reciprocal(sp[2][:, :, :], sp[4][:, :, :]))
            step(dve.tensor_tensor(sp[3][:, :, :], sp[3][:, :, :], sp[2][:, :, :], ALU.mult))
            project(3)
            dve.wait_ge(g_act, 4)
            step(dve.tensor_tensor(sp[5][:, :, :], sp[5][:, :, :], sp[3][:, :, :], ALU.subtract))
            step(dve.scalar_tensor_tensor(out=sp[1][:, :, :], in0=sp[1][:, :, :], scalar=0.0, in1=sp[5][:, :, :],
                                          op0=ALU.max, op1=ALU.add))
            dve.scalar_tensor_tensor(out=g[:, :, :], in0=sp[1][:, :, :], scalar=-1.0,
                                     in1=ea[:, :].unsqueeze(1).to_broadcast([P, NB, H]),
                                     op0=ALU.mult, op1=ALU.mult).then_inc(g_dve, 1)
            project(4)
            dve.wait_ge(g_pe, 1)
            step(dve.tensor_copy(G[:, :, :], ps[:, 6, 0:2 * H].rearrange("p (b h) -> p b h", b=NB)))
            dve.tensor_tensor(sp[0][:, 0, :], ps[:, 6, 2 * H:3 * H], G[:, 0, :], ALU.subtract).then_inc(g_dve, 1)
            project(5)
            for gr in range(4):
                s = slice(4 * gr, 4 * gr + 4)
                dve.wait_ge(g_pe, 2 + gr)
                dve.tensor_tensor(Nm[:, s, :], ps[:, 4 + gr, :].rearrange("p (h c) -> p h c", h=4),
                                  over(G[:, gr // 2, 4 * (gr % 2):4 * (gr % 2) + 4]), ALU.subtract).then_inc(gdiff, 1)
            dve.wait_ge(g_act, 5)
            dve.tensor_tensor(eg[:, :], eg[:, :], beta[:, 1, :], ALU.mult).then_inc(g_dve, 1)
            project(6)
            for gr in range(4):
                s = slice(4 * gr, 4 * gr + 4)
                dve.wait_ge(gdiff, gr + 1)
                dve.scalar_tensor_tensor(out=Nm[:, s, :], in0=Nm[:, s, :], scalar=-1.0, in1=Nm[:, s, :],
                                         op0=ALU.mult, op1=ALU.min).then_inc(gmin, 1)
            project(7)
            dve.wait_ge(q_squared, 4)
            link(dve.tensor_scalar(ss[:, 0, :, :], ss[:, 0, :, :], 1e-6, DK * 1e-6, ALU.add, ALU.mult))
            for u in range(8, QKV // 2):
                project(u)
            dve.wait_ge(k_squared, 4)
            dve.tensor_scalar(ss[:, 1, :, :], ss[:, 1, :, :], 1e-6, None, ALU.add).then_inc(ss_here, 1)
            cut_lo(U_Z + 0 + AHEAD)
            dve.wait_ge(rk_here, 1)
            for i in range(8):
                gr, hs = i % 4, slice(4 * (i % 2), 4 * (i % 2) + 4)
                b = gr // 2
                if i == 4:
                    cut_lo(U_Z + 1 + AHEAD)
                dve.wait_ge(kv_turned, i + 1)
                src = ps[:, 4 + gr, :].rearrange("p (h d) -> p h d", h=4)
                if i < 4:
                    dve.tensor_tensor(kt[:, b, hs, :], src, over(rk[:, hs, b]), ALU.mult).then_inc(kv_taken, 1)
                else:
                    dve.tensor_tensor(vb[:, b, hs, :], src, over(beta[:, b, hs]), ALU.mult).then_inc(kv_taken, 1)
            cut_lo(U_Z + 2 + AHEAD)

            def decayed(gr):
                s = slice(4 * gr, 4 * gr + 4)
                dve.wait_ge(kk_mm, gr + 1)
                dve.wait_ge(dmul, gr + 1)
                dve.tensor_tensor(Dm[:, s, :], ps[:, 2 * (gr % 2), :].rearrange("p (h c) -> p h c", h=4), Nm[:, s, :],
                                  ALU.mult).then_inc(kk_taken, 1)
                dve.tensor_tensor(DT[:, s, :], ps[:, 2 * (gr % 2) + 1, :].rearrange("p (h c) -> p h c", h=4), Tm[:, s, :],
                                  ALU.mult).then_inc(kk_taken, 1)

            def join(q):
                s = slice(4 * (q % 4), 4 * (q % 4) + 4)
                lv = q // 4
                mk = masks[:, lv, :].bitcast(U32).unsqueeze(1).to_broadcast([P, 4, P])
                mt = masksT[:, max(lv - 5, 0), :].bitcast(U32).unsqueeze(1).to_broadcast([P, 4, P])
                if lv == 0:
                    dve.wait_ge(inv_id, q + 1)
                    dve.wait_ge(kk_taken, 2 * q + 1)
                    step(dve.copy_predicated(Tm[:, s, :], mk, Dm[:, s, :]))
                else:
                    dve.wait_ge(inv_r, q - 3)
                    if lv < 6:
                        product = ps[:, 6 + q % 2, :].rearrange("p (h c) -> p h c", h=4)
                        link(dve.copy_predicated(Tm[:, s, :], mk, product))
                if lv < 5:
                    settle()
                    dve.transpose(Nm[:, s, :], Tm[:, s, :]).then_inc(inv_rc, 1)
                else:
                    dve.copy_predicated(Nm[:, s, :], mt, ps[:, q % 2, :].rearrange("p (h c) -> p h c", h=4)).then_inc(inv_rc, 1)

            decayed(0)
            decayed(1)
            join(0)
            decayed(2)
            join(1)
            decayed(3)
            for q in range(2, 4 * 7):
                join(q)
            cut_lo(U_Z + 3 + AHEAD)
            for gr in range(4):
                b, hs = gr // 2, slice(4 * (gr % 2), 4 * (gr % 2) + 4)
                dve.wait_ge(o_sq, gr + 1)
                s = slice(4 * gr, 4 * gr + 4)
                dve.scalar_tensor_tensor(out=ms[:, s], in0=ms[:, s], scalar=1.0 / DK, in1=ss[:, 0, hs, b],
                                         op0=ALU.mult, op1=ALU.add).then_inc(o_ms, 1)
                if gr == 0:
                    dve.wait_ge(zn_done, 2)
                dve.wait_ge(o_rms, gr + 1)
                for i in range(4):
                    n_ = 4 * gr + i
                    h = 4 * (gr % 2) + i
                    last = dve.scalar_tensor_tensor(out=Tm[:, n_, :], in0=ps[:, O_BANK[gr], i * P:(i + 1) * P],
                                                    scalar=fo[:, n_:n_ + 1], in1=zn[:, b, h * P:(h + 1) * P],
                                                    op0=ALU.mult, op1=ALU.mult)
                last.then_inc(o_done, 1)
            turn(1)
            for u in range(3):
                cut_lo(U_OUT + u + AHEAD)
            norm(0, 0, U_OUT + 3)
            turn(2)
            cut_lo(U_OUT + 3 + AHEAD)

            def ffn_rest(c):
                dve.wait_ge(ffn_hi, c + 1)
                s = slice(2 * c, 2 * c + 2)
                dve.tensor_tensor(hT_lo[:, s, :], hf[:, c % 2, :].rearrange("p (m t) -> p m t", m=2),
                                  hT_hi[:, s, :].bitcast(F32), ALU.subtract).then_inc(ffn_lo, 1)

            for c in range(FC):
                cut_lo(U_GU + 2 * c + AHEAD)
                if c >= 1:
                    ffn_rest(c - 1)
                cut_lo(U_GU + 2 * c + 1 + AHEAD)
                used(U_GU + 2 * c + 1)
                dve.wait_ge(ffn_silu, c + 1)
                if c >= 2:
                    dve.wait_ge(ffn_lo, c - 1)
                dve.tensor_tensor(hf[:, c % 2, :], ps[:, 2 * (c % 3) + 1, :], sg[:, c % 2, :], ALU.mult).then_inc(ffn_act, 1)
            ffn_rest(FC - 1)
            for u in range(FC - 1):
                cut_lo(U_DOWN + u + AHEAD)
            norm(1, 4, U_DOWN + FC - 1)
            turn(3)
            cut_lo(U_DOWN + FC - 1 + AHEAD)

            cut_lo(U_KV + AHEAD)
            used(U_KV)
            for m in range(2):
                dve.tensor_copy(kT2[0:64, 2 * m + 1, 0, :], ps[64:128, m, 0:T]).then_inc(kB_dve, 1)
                dve.tensor_copy(kT2[64:128, 2 * m + 1, 1, :], ps[64:128, m, 0:T]).then_inc(kB_dve, 1)
            cut_lo(U_KV + 1 + AHEAD)
            used(U_KV + 1)
            dve.tensor_copy(vB[:, :, :], ps[:, 6:8, 0:HKV * HD]).then_inc(vB_here, 1)
            dve.wait_ge(sink_here, 16)
            dve.wait_ge(consts, 3)

            def scores(gi):
                st = gi % 2
                dve.wait_ge(sc_mm, gi + 1)
                if gi >= 2:
                    dve.wait_ge(pt_mm, 3 * (gi - 1))
                for i in range(GQ):
                    slope = 2.0 ** (-8.0 * (GQ * gi + i + 1) / HQ)
                    dve.scalar_tensor_tensor(out=sS[:, st, i, 0:P], in0=dist[:, 0:P], scalar=-slope,
                                             in1=ps[:, 0, i * P:(i + 1) * P], op0=ALU.mult, op1=ALU.add)
                    last = dve.scalar_tensor_tensor(out=sS[:, st, i, P:3 * P], in0=dist[:, P:3 * P], scalar=-slope,
                                                    in1=ps[:, 1 + i // 2, (i % 2) * T:(i % 2) * T + T],
                                                    op0=ALU.mult, op1=ALU.add)
                last.then_inc(sc_bias, 1)
                dve.wait_ge(sc_bias, gi + 1)
                link(dve.tensor_reduce(smax[:, st, 0, :], sS[:, st, :, 0:P], AX.X, ALU.max))
                step(dve.tensor_reduce(smax[:, st, 1, :], sS[:, st, :, P:3 * P], AX.X, ALU.max))
                skb = sk[:, GQ * gi:GQ * gi + GQ].unsqueeze(1).to_broadcast([P, NB, GQ])
                step(dve.tensor_tensor(smax[:, st, :, :], smax[:, st, :, :], skb, ALU.max))
                link(dve.tensor_scalar(nmax[:, st, :, :], smax[:, st, :, :], -1.0, None, ALU.mult))
                dve.tensor_tensor(ske[:, st, :, :], skb, smax[:, st, :, :], ALU.subtract).then_inc(sc_max, 1)

            def probs(gi):
                st = gi % 2
                dve.wait_ge(sc_exp, gi + 1)
                step(dve.tensor_tensor(ssum[:, st, :, :], ssum[:, st, :, :], ske[:, st, :, :], ALU.add))
                step(dve.reciprocal(sinv[:, st, :, :], ssum[:, st, :, :]))
                dve.tensor_tensor(sS[:, st, :, 0:P], sS[:, st, :, 0:P], over(sinv[:, st, 0, :]), ALU.mult)
                dve.tensor_tensor(sS[:, st, :, P:3 * P], sS[:, st, :, P:3 * P], over(sinv[:, st, 1, :], 2 * P),
                                  ALU.mult).then_inc(sc_prob, 1)

            def attended(gi):
                dve.wait_ge(pv_hi, gi + 1)
                s = slice(2 * gi, 2 * gi + 2)
                dve.tensor_tensor(oT_lo[:, s, :], ps[:, 6, :].rearrange("p (k t) -> p k t", k=2),
                                  oT_hi[:, s, :].bitcast(F32), ALU.subtract).then_inc(pv_lo, 1)

            cut_lo(U_Q + 0 + AHEAD)
            scores(0)
            cut_lo(U_Q + 1 + AHEAD)
            scores(1)
            probs(0)
            cut_lo(U_Q + 2 + AHEAD)
            attended(0)
            scores(2)
            probs(1)
            cut_lo(U_Q + 3 + AHEAD)
            attended(1)
            scores(3)
            probs(2)
            attended(2)
            probs(3)
            cut_lo(U_O + 0 + AHEAD)
            cut_lo(U_O + 1 + AHEAD)
            attended(3)
            cut_lo(U_O + 2 + AHEAD)
            norm(2, 0, U_O + 3)

            dve.wait_ge(wr_cut, 1)
            dve.tensor_tensor(wr_lo[:, :, :], wr[:, :, :], wr_hi[:, :, :].bitcast(F32), ALU.subtract).then_inc(wr_cut, 1)
            turn(4)
            dve.wait_ge(x3_cut, 1)
            dve.tensor_tensor(x3_lo[:, :, :], x[:, :, :], x3_hi[:, :, :].bitcast(F32), ALU.subtract).then_inc(x3_cut, 1)
            dve.wait_ge(lg_mm, 1)
            dve.tensor_copy(lgT[:, :], ps[0:E, 0, 0:T]).then_inc(lgT_here, 1)
            dve.wait_ge(lg_mm, 2)
            step(dve.tensor_copy(lg[:, :, :], ps[:, 0, 0:2 * E].rearrange("p (b e) -> p b e", b=NB)))

            def first_max(src, m, oh):
                bc = [P, NB, E]
                step(dve.tensor_reduce(m[:, :, :], src[:, :, :], AX.X, ALU.max))
                step(dve.tensor_tensor(eq[:, :, :], src[:, :, :], m[:, :, :].to_broadcast(bc), ALU.is_equal))
                step(dve.tensor_tensor(eq[:, :, :], eq[:, :, :], rev[:, :].unsqueeze(1).to_broadcast(bc), ALU.mult))
                step(dve.tensor_reduce(rr[:, :, :], eq[:, :, :], AX.X, ALU.max))
                step(dve.tensor_tensor(oh[:, :, :], eq[:, :, :], rr[:, :, :].to_broadcast(bc), ALU.is_equal))

            dve.wait_ge(consts, 4)
            first_max(lg, m1, oh1)
            step(dve.scalar_tensor_tensor(out=lg2[:, :, :], in0=oh1[:, :, :], scalar=-3.0e38, in1=lg[:, :, :],
                                          op0=ALU.mult, op1=ALU.add))
            first_max(lg2, m2, oh2)
            dve.tensor_tensor(gw[:, :, 0:1], m2[:, :, :], m1[:, :, :], ALU.subtract).then_inc(w2_arg, 1)
            dve.tensor_tensor(sel[:, :, :], oh1[:, :, :], oh2[:, :, :], ALU.add).then_inc(sel_here, 1)
            dve.wait_ge(w2_here, 1)
            step(dve.tensor_scalar(gw[:, :, 2:3], gw[:, :, 1:2], 1.0, None, ALU.add))
            step(dve.reciprocal(gw[:, :, 2:3], gw[:, :, 2:3]))
            step(dve.tensor_tensor(gw[:, :, 3:4], gw[:, :, 1:2], gw[:, :, 2:3], ALU.mult))
            for b in range(NB):
                step(dve.tensor_scalar(gates[:, b, 0:E], oh1[:, b, :], gw[:, b, 2:3], None, ALU.mult))
                step(dve.scalar_tensor_tensor(out=gates[:, b, 0:E], in0=oh2[:, b, :], scalar=gw[:, b, 3:4],
                                              in1=gates[:, b, 0:E], op0=ALU.mult, op1=ALU.add))
            dve.wait_ge(pos_mm, 1)
            step(dve.scalar_tensor_tensor(out=lg2[:, :, :], in0=ps[:, 1, 0:2 * E].rearrange("p (b e) -> p b e", b=NB),
                                          scalar=1.0, in1=sel[:, :, :], op0=ALU.add, op1=ALU.mult))
            step(dve.tensor_scalar(pos[:, :, 0:E], lg2[:, :, :], -1.0, None, ALU.add))
            step(dve.tensor_reduce(cmax[:, :], ps[:, 1, 2 * E:3 * E], AX.X, ALU.max))
            dve.tensor_copy(cint[:, :], cmax[:, :]).then_inc(route_here, 1)

            def experts(p):
                base = U_MOE + p * E * PER_E

                def build(ge, it):
                    dve.wait_ge(gathered, 9 * p + ge + 2 * it) if (p or ge) else None
                    e = ge + 2 * it
                    for b in range(NB):
                        last = dve.tensor_scalar(oneh[:, b, :], iota[:, p, :], pos[:, b, bass.ds(e, 1)], None, ALU.is_equal)
                    last.then_inc(oneh_here, 1)

                def rest_xg(ge, it):
                    dve.wait_ge(xg_hi_here, 9 * p + ge + 1 + 2 * it)
                    dve.tensor_tensor(xg_lo[:, :, :], ps[:, 6:8, :].rearrange("p b (k s) -> p (b k) s", k=4),
                                      xg_hi[:, :, :].bitcast(F32), ALU.subtract).then_inc(xg_here, 1)

                def rest_h(c, it, b):
                    gc = 88 * p + 11 * b + c
                    dve.wait_ge(h_hi, gc + 1 + 22 * it)
                    dve.tensor_tensor(hE_lo[:, 2 * c:2 * c + 2, :],
                                      ps[:, 6 + gc % 2, 0:2 * P].rearrange("p (m s) -> p m s", m=2),
                                      hE_hi[:, 2 * c:2 * c + 2, :].bitcast(F32), ALU.subtract).then_inc(h_here, 1)

                def add(s, it, b):
                    dve.wait_ge(scattered, 18 * p + 2 * s + b + 1 + 4 * it)
                    dve.wait_ge(acc_added, 18 * p + 2 * s + b + 1 + 4 * it)
                    bank = 4 if b == 0 else 2
                    dve.tensor_tensor(x[:, b, :], x[:, b, :], ps[:, bank:bank + 2, :].rearrange("p b n -> p (b n)"),
                                      ALU.add).then_inc(acc_added, 1)

                build(0, 0)
                if p == 0:
                    cut_lo(U_O + 3 + AHEAD)
                rest_xg(0, 0)
                with dve.Fori(0, TURNS) as it:
                    for b in range(2):
                        for l in range(PER_E):
                            j = base + PER_E * b + l
                            if l < PER_E - 1:
                                cut_lo(j + AHEAD, it)
                            if l < 2 * FC and l % 2 == 1:
                                c = l // 2
                                gc = 88 * p + 11 * b + c
                                used(j, it)
                                dve.wait_ge(silu_here, gc + 1 + 22 * it)
                                dve.tensor_tensor(actE[:, gc % 2, :], sgE[:, gc % 2, :], ps[:, gc % 2, 256:512],
                                                  ALU.mult).then_inc(act_here, 1)
                                if c >= 1:
                                    rest_h(c - 1, it, b)
                            elif l in (4, 6):
                                add(b, it, l // 2 - 2)
                            elif l == 10:
                                build(b + 1, it)
                            elif l == 2 * FC:
                                rest_h(FC - 1, it, b)
                            elif l == 2 * FC + 2:
                                rest_xg(b + 1, it)
                            elif l == PER_E - 1:
                                dve.wait_ge(y_hi_here, 8 * p + b + 1 + 2 * it)
                                dve.scalar_tensor_tensor(out=y_lo[:, :], in0=ps[:, 2:4, :].rearrange("p b n -> p (b n)"),
                                                         scalar=gslot[:, b:b + 1], in1=y_hi[:, :].bitcast(F32),
                                                         op0=ALU.mult, op1=ALU.subtract).then_inc(y_here, 1)
                                cut_lo(j + AHEAD, it)
                add(E, 0, 0)
                add(E, 0, 1)
                dve.wait_ge(acc_added, 18 * p + 20)

            settle()
            dve.wait_ge(x_scaled, 1)
            experts(0)
            full = dve.value_load(cint[0:1, 0:1], min_val=0, max_val=T)
            with dve.If(full > P):
                experts(1)
            norm(3, None)

        @block.tensor
        def _(pe):
            def mm(dst, lhsT, rhs, start, stop):
                return pe.matmul(dst, lhsT, rhs, start=start, stop=stop)

            def ready(j, it=0):
                pe.wait_ge(lo_ready, j + 1 + PER_IT * it)

            def turn(i, src, made=None):
                for s in range(4):
                    if made is not None:
                        made(s)
                    for q in range(4):
                        last = pe.transpose(ps[:, 4 + s, q * P:(q + 1) * P], src(s // 2, 4 * (s % 2) + q), ident[:, :])
                    last.then_inc(turned, 1)

            def turn_x(i, norms):
                turn(i, lambda b, k: x[:, b, k * P:(k + 1) * P],
                     lambda s: pe.wait_ge(ln_done, 2 * (norms - 1) + s // 2 + 1) if s % 2 == 0 else None)
                turned_in(i)

            def turned_in(i):
                pe.wait_ge(turn_lo, 4 * i + 4)

            def to_channels(j, banks):
                ready(j)
                w_hi = slot(hi, j).rearrange("p (k n) -> p k n", k=KD)
                w_lo = slot(lo, j).rearrange("p (k n) -> p k n", k=KD)
                for m in range(2):
                    dst = banks[m]
                    c = slice(m * P, m * P + P)
                    for k in range(KD):
                        mm(dst, w_hi[:, k, c], xT_hi[:, k, :], k == 0, False)
                        mm(dst, w_hi[:, k, c], xT_lo[:, k, :], False, False)
                        last = mm(dst, w_lo[:, k, c], xT_hi[:, k, :], False, k == KD - 1)
                last.then_inc(unit_used, 1)

            def to_tokens(j, k0, nk, first, final, dsts, a_hi, a_lo, norm_follows=False):
                ready(j)
                w_hi = slot(hi, j).rearrange("p (k n) -> p k n", k=nk)
                w_lo = slot(lo, j).rearrange("p (k n) -> p k n", k=nk)
                width = dsts[0][0].shape[1]
                order = [(b, kk) for kk in range(nk) for b in range(NB)]
                if norm_follows:
                    order.sort()
                for b, kk in order:
                    t = slice(b * P, b * P + P)
                    for a, w, p in ((a_hi, w_hi, 0), (a_hi, w_lo, 1), (a_lo, w_hi, 2)):
                        for i, dst in enumerate(dsts[b]):
                            last = mm(dst, a[:, k0 + kk, t], w[:, kk, i * width:(i + 1) * width],
                                      first and kk == 0 and p == 0, final and kk == nk - 1 and p == 2)
                    if norm_follows and (b, kk) == (0, nk - 1):
                        last.then_inc(block0_done, 1)
                last.then_inc(unit_used, 1)

            def halves(bank):
                return [[ps[:, bank + 2 * b + i, :] for i in range(2)] for b in range(NB)]

            pe.wait_ge(consts, 1)
            turn(0, lambda b, k: x[:, b, k * P:(k + 1) * P],
                 lambda s: pe.wait_ge(x_here, 16 * NB) if s == 0 else None)
            pe.wait_ge(small_here, 16)
            pe.transpose(ps[:, 0, 0:TAPS * QKV], cw_rows[:, :], ident[0:TAPS * QKV, 0:TAPS * QKV]).then_inc(cw_turned, 1)
            turned_in(0)
            pe.wait_ge(cw_here, 1)

            def project(u):
                pe.wait_ge(conv_step, 6 * u + 6)
                to_channels(U_QKV + u, [ps[:, (2 * u + m) % 4, 0:T] for m in range(2)])

            def small_product(dst, w_hi, w_lo):
                for k in range(KD):
                    mm(dst, w_hi[:, k, :], xT_hi[:, k, :], k == 0, False)
                    mm(dst, w_hi[:, k, :], xT_lo[:, k, :], False, False)
                    last = mm(dst, w_lo[:, k, :], xT_hi[:, k, :], False, k == KD - 1)
                return last

            def turn_heads(tile0, signal, wait):
                for gr in range(4):
                    wait(gr)
                    for i in range(4):
                        last = pe.transpose(ps[:, 4 + gr, i * P:(i + 1) * P],
                                            conv[:, tile0 + 4 * (gr % 2) + i, P * (gr // 2):P * (gr // 2) + P], ident[:, :])
                    last.then_inc(signal, 1)

            project(0)
            pe.wait_ge(ab_cut, 2)
            small_product(ps[0:2 * H, 7, 0:T], wab_hi, wab_lo).then_inc(ab_mm, 1)
            project(1)
            pe.wait_ge(ab_here, 1)
            for b in range(NB):
                last = pe.transpose(ps[:, 7, 2 * H * b:2 * H * (b + 1)], abT[:, b * P:(b + 1) * P], ident[0:2 * H, 0:2 * H])
            last.then_inc(ab_mm, 1)
            for u in range(2, 5):
                project(u)
            pe.wait_ge(consts, 2)
            pe.wait_ge(g_dve, 3)
            for b in range(NB):
                mm(ps[:, 6, b * H:(b + 1) * H], tri_incl[:, :], g[:, b, :], True, True)
            mm(ps[:, 6, 2 * H:3 * H], ones[:, :], g[:, 0, :], True, True).then_inc(g_pe, 1)
            project(5)
            pe.wait_ge(g_dve, 4)
            for gr in range(4):
                for i in range(4):
                    last = mm(ps[:, 4 + gr, i * P:(i + 1) * P],
                              g[:, gr // 2, 4 * (gr % 2) + i:4 * (gr % 2) + i + 1].to_broadcast([P, P]),
                              tri_incl[:, :], True, True)
                last.then_inc(g_pe, 1)
            project(6)
            pe.wait_ge(silu_done, 4)
            pe.wait_ge(g_act, 7)
            turn_heads(0, q_turned, lambda gr: None)
            for u in range(7, 11):
                project(u)
            pe.wait_ge(silu_done, 8)
            turn_heads(H, kv_turned, lambda gr: pe.wait_ge(q_squared, gr + 1))
            project(11)

            def project_z(u):
                c = u // 2
                if u % 2 == 0:
                    pe.wait_ge(conv_step, 12 + 6 * (QKV // 2 - 1 + c))
                to_tokens(U_Z + u, 4 * (u % 2), 4, u % 2 == 0, u % 2 == 1,
                          [[ps[:, 2 * c + b, :]] for b in range(NB)], xT_hi, xT_lo)

            project_z(0)
            project_z(1)
            pe.wait_ge(silu_done, 12)
            turn_heads(2 * H, kv_turned, lambda gr: pe.wait_ge(kv_taken, gr + 1))
            project_z(2)
            for gr in range(4):
                pe.wait_ge(kv_taken, 5 + gr)
                for i in range(4):
                    last = pe.transpose(ps[:, 4 + gr, i * P:(i + 1) * P], kt[:, gr // 2, 4 * (gr % 2) + i, :], ident[:, :])
                last.then_inc(kback, 1)
            project_z(3)
            for gr in range(4):
                pe.wait_ge(kback_taken, gr + 1)
                if gr < 2:
                    pe.wait_ge(z_done, 2 * (gr + 1))
                else:
                    pe.wait_ge(kk_taken, 2 * (gr - 1))
                t = slice(P * (gr // 2), P * (gr // 2) + P)
                for rhs, bank in ((H, 2 * (gr % 2)), (0, 2 * (gr % 2) + 1)):
                    for i in range(4):
                        h = 4 * (gr % 2) + i
                        last = mm(ps[:, bank, i * P:(i + 1) * P], conv[:, H + h, t], conv[:, rhs + h, t], True, True)
                last.then_inc(kk_mm, 1)

            Pm = conv[:, 2 * H:3 * H, :].rearrange("p h (b t) -> p (h b) t", b=2)

            def first(q):
                pe.wait_ge(inv_rc, q - 3)
                if q >= 6:
                    pe.wait_ge(inv_pc, q - 5)
                for i in range(4):
                    n_ = 4 * (q % 4) + i
                    last = mm(ps[:, 4 + q % 2, i * P:(i + 1) * P], Dm[:, n_, :], Nm[:, n_, :], True, True)
                last.then_inc(inv_p, 1)

            def second(q):
                pe.wait_ge(inv_pc, q - 3)
                if q >= 6:
                    pe.wait_ge(inv_rc, q - 1)
                for i in range(4):
                    n_ = 4 * (q % 4) + i
                    c = slice(i * P, (i + 1) * P)
                    if q < 24:
                        last = mm(ps[:, 6 + q % 2, c], Pm[:, n_, :], Tm[:, n_, :], True, True)
                    if q >= 20:
                        last = mm(ps[:, q % 2, c], Tm[:, n_, :], Pm[:, n_, :], True, True)
                last.then_inc(inv_r, 1)

            pe.wait_ge(kk_taken, 8)
            for q in range(4, 4 * 7):
                first(q)
                if q >= 5:
                    second(q - 1)
            second(27)

            W_, S_ = Dm[:, 0:H, :], Dm[:, H:2 * H, :]
            pe.wait_ge(inv_rc, 28)
            pe.wait_ge(kscaled, 2)

            def group(bank, products, s):
                for i in range(4):
                    for n_, (lhsT, rhs) in enumerate(products(i)):
                        last = mm(ps[:, bank, i * P:(i + 1) * P], lhsT, rhs, n_ == 0, n_ == len(products(i)) - 1)
                last.then_inc(s, 1)

            for hh in range(2):
                group(hh, lambda i: [(Nm[:, 4 * hh + i, :], vb[:, 0, 4 * hh + i, :])], scan_mm)
            for hh in range(2):
                group(2 + hh, lambda i: [(kt[:, 1, 4 * hh + i, :], Nm[:, H + 4 * hh + i, :])], scan_mm)
            for hh in range(2):
                pe.wait_ge(scan_ev, hh + 1)
                group(4 + hh, lambda i: [(kt[:, 0, 4 * hh + i, :], vb[:, 0, 4 * hh + i, :])], scan_mm)
            for hh in range(2):
                group(6 + hh, lambda i: [(DT[:, 4 * hh + i, :], vb[:, 0, 4 * hh + i, :])], o_mm)
            for hh in range(2):
                pe.wait_ge(scan_ev, 4 + hh + 1)
                group(hh, lambda i: [(Nm[:, H + 4 * hh + i, :], vb[:, 1, 4 * hh + i, :]),
                                     (W_[:, 4 * hh + i, :], S_[:, 4 * hh + i, :])], scan_mm)
            for hh in range(2):
                pe.wait_ge(scan_ev, 6 + hh + 1)
                pe.wait_ge(qg_here, 1)
                group(2 + hh, lambda i: [(conv[:, 4 * hh + i, P:T], S_[:, 4 * hh + i, :]),
                                         (DT[:, H + 4 * hh + i, :], vb[:, 1, 4 * hh + i, :])], o_mm)
            turn(1, lambda b, k: Tm[:, b * H + k, :], lambda s: pe.wait_ge(o_done, s + 1))
            turned_in(1)
            for u in range(4):
                to_tokens(U_OUT + u, 2 * u, 2, u == 0, u == 3, halves(0), xT_hi, xT_lo, u == 3)
            turn_x(2, 1)

            for c in range(FC):
                if c >= 3:
                    pe.wait_ge(ffn_act, c - 2)
                for t in range(2):
                    bank = 2 * (c % 3) + t
                    to_channels(U_GU + 2 * c + t, [ps[:, bank, m * T:(m + 1) * T] for m in range(2)])
            pe.wait_ge(ffn_act, FC - 2)
            for u in range(FC):
                pe.wait_ge(ffn_lo, u + 1)
                to_tokens(U_DOWN + u, 2 * u, 2, u == 0, u == FC - 1, halves(4), hT_hi, hT_lo, u == FC - 1)
            turn_x(3, 2)

            to_channels(U_KV, [ps[:, m, 0:T] for m in range(2)])
            to_tokens(U_KV + 1, 0, KD, True, True, [[ps[:, 6 + b, 0:HKV * HD]] for b in range(NB)], xT_hi, xT_lo)
            pe.wait_ge(kB_act, 4)
            pe.wait_ge(kB_dve, 4)
            pe.wait_ge(vB_here, 1)
            pe.wait_ge(consts, 3)

            def queries(gi):
                if gi:
                    pe.wait_ge(qB_here, 2 * gi)
                to_channels(U_Q + gi, [ps[:, 3, m * T:(m + 1) * T] for m in range(2)])

            def scores(gi):
                pe.wait_ge(qB_here, 2 * gi + 2)
                if gi:
                    pe.wait_ge(sc_bias, gi)
                for i in range(GQ):
                    q = qT[:, 2 * gi + i // 2, :]
                    k = kT2[:, gi, i % 2, :]
                    mm(ps[:, 0, i * P:(i + 1) * P], q[:, 0:P], k[:, 0:P], True, True)
                    last = mm(ps[:, 1 + i // 2, (i % 2) * T:(i % 2) * T + T], q[:, P:T], k, True, True)
                last.then_inc(sc_mm, 1)

            def attend(gi):
                pe.wait_ge(sc_prob, gi + 1)
                for r in range(3):
                    n_ = 3 * gi + r
                    if n_ >= 2:
                        pe.wait_ge(pt_taken, n_ - 1)
                    for i in range(GQ):
                        last = pe.transpose(ps[:, 4 + n_ % 2, i * P:(i + 1) * P], sS[:, gi % 2, i, r * P:(r + 1) * P],
                                            ident[:, :])
                    last.then_inc(pt_mm, 1)
                pe.wait_ge(pt_taken, 3 * gi + 3)
                if gi:
                    pe.wait_ge(pv_lo, gi)
                v = slice(gi * HD, (gi + 1) * HD)
                for i in range(GQ):
                    o = 64 * (i % 2)
                    c = (i // 2) * T
                    mm(ps[o:o + 64, 6, c:c + P], vB[:, 0, v], pT[:, i, :], True, True)
                    mm(ps[o:o + 64, 6, c + P:c + T], vB[:, 0, v], pT[:, 4 + i, :], True, False)
                    last = mm(ps[o:o + 64, 6, c + P:c + T], vB[:, 1, v], pT[:, 8 + i, :], False, True)
                last.then_inc(pv_mm, 1)

            def project_out(u):
                pe.wait_ge(pv_lo, u + 1)
                to_tokens(U_O + u, 2 * u, 2, u == 0, u == 3, halves(0), oT_hi, oT_lo, u == 3)

            queries(0)
            scores(0)
            queries(1)
            scores(1)
            queries(2)
            attend(0)
            scores(2)
            queries(3)
            attend(1)
            scores(3)
            attend(2)
            pe.wait_ge(sc_bias, 4)
            project_out(0)
            project_out(1)
            attend(3)
            project_out(2)
            project_out(3)
            turn_x(4, 3)

            pe.wait_ge(wr_cut, 2)
            small_product(ps[0:E, 0, 0:T], wr_hi, wr_lo).then_inc(lg_mm, 1)
            pe.wait_ge(lgT_here, 1)
            for b in range(NB):
                last = pe.transpose(ps[:, 0, E * b:E * (b + 1)], lgT[:, b * P:(b + 1) * P], ident[0:E, 0:E])
            last.then_inc(lg_mm, 1)
            pe.wait_ge(sel_here, 1)
            pe.wait_ge(consts, 4)
            mm(ps[:, 1, 0:E], tri_strict[:, :], sel[:, 0, :], True, True)
            mm(ps[:, 1, E:2 * E], tri_strict[:, :], sel[:, 1, :], True, False)
            mm(ps[:, 1, E:2 * E], ones[:, :], sel[:, 0, :], False, True)
            for b in range(NB):
                last = mm(ps[:, 1, 2 * E:3 * E], ones[:, :], sel[:, b, :], b == 0, b == 1)
            last.then_inc(pos_mm, 1)

            def experts(p):
                base = U_MOE + p * E * PER_E

                def gather(ge, it):
                    pe.wait_ge(oneh_here, 9 * p + ge + 1 + 2 * it)
                    for b in range(NB):
                        pe.transpose(ps[:, 4, b * P:(b + 1) * P], oneh[:, b, :].bitcast(F32), ident[:, :])
                    for b in range(NB):
                        mm(ps[:, 5, 0:1], oneh[:, b, :].bitcast(F32), gates[:, b, bass.ds(ge + 2 * it, 1)], b == 0, b == 1)
                    for k in range(KD):
                        dst = ps[:, 6 + k // 4, (k % 4) * P:(k % 4) * P + P]
                        c = slice(k * P, k * P + P)
                        for n_, (part, b) in enumerate(((x3_hi, 0), (x3_hi, 1), (x3_lo, 0), (x3_lo, 1))):
                            last = mm(dst, part[:, b, c], oneh[:, b, :], n_ == 0, n_ == 3)
                    last.then_inc(gathered, 1)

                def turn_h(c, it, b):
                    gc = 88 * p + 11 * b + c
                    pe.wait_ge(act_here, gc + 3 + 22 * it)
                    pe.wait_ge(h_here, gc + 1 + 22 * it)
                    for m in range(2):
                        last = pe.transpose(ps[:, 6 + gc % 2, m * P:(m + 1) * P], actE[:, gc % 2, m * P:(m + 1) * P],
                                            ident[:, :])
                    last.then_inc(ff_turned, 1)

                def scatter(s, it, par):
                    pe.wait_ge(y_here, 8 * p + s + 1 + 2 * it)
                    for b in range(NB):
                        for n_, part in enumerate((y_hi, y_lo)):
                            for i in range(2):
                                bank = (4 if b == 0 else 2) + i
                                last = mm(ps[:, bank, :], onehT[:, par, b, :], part[:, i * 512:(i + 1) * 512],
                                          n_ == 0, n_ == 1)
                        last.then_inc(scattered, 1)

                if p == 0:
                    pe.wait_ge(route_here, 1)
                pe.wait_ge(x3_cut, 2)
                gather(0, 0)
                pe.wait_ge(xg_here, 9 * p + 1)
                pe.wait_ge(moe_zero, 2 * p + 2)
                with pe.Fori(0, TURNS) as it:
                    for b in range(2):
                        for l in range(PER_E):
                            j = base + PER_E * b + l
                            if l < 2 * FC:
                                c = l // 2
                                gc = 88 * p + 11 * b + c
                                if l == 0:
                                    pe.wait_ge(xg_here, 9 * p + b + 1 + 2 * it)
                                if l % 2 == 0:
                                    pe.wait_ge(act_here, gc + 1 + 22 * it)
                                ready(j, it)
                                w_hi = slot(hi, j).rearrange("p (k n) -> p k n", k=4)
                                w_lo = slot(lo, j).rearrange("p (k n) -> p k n", k=4)
                                for kk in range(4):
                                    k = 4 * (l % 2) + kk
                                    mm(ps[:, gc % 2, :], xg_hi[:, k, :], w_hi[:, kk, :], k == 0, False)
                                    mm(ps[:, gc % 2, :], xg_hi[:, k, :], w_lo[:, kk, :], False, False)
                                    last = mm(ps[:, gc % 2, :], xg_lo[:, k, :], w_hi[:, kk, :], False, k == KD - 1)
                                last.then_inc(unit_used, 1)
                                if l % 2 == 1 and c >= 1:
                                    turn_h(c - 1, it, b)
                                if l == 3:
                                    scatter(b, it, (b + 1) % 2)
                            else:
                                d = l - 2 * FC
                                pe.wait_ge(h_here, 88 * p + 11 * b + d + 3 + 22 * it)
                                if d == 0:
                                    pe.wait_ge(acc_added, 18 * p + 2 * b + 4 + 4 * it)
                                ready(j, it)
                                w_hi = slot(hi, j).rearrange("p (k n) -> p k n", k=2)
                                w_lo = slot(lo, j).rearrange("p (k n) -> p k n", k=2)
                                for kk in range(2):
                                    k = 2 * d + kk
                                    for n_, (a, w) in enumerate(((hE_hi, w_hi), (hE_hi, w_lo), (hE_lo, w_hi))):
                                        for i in range(2):
                                            last = mm(ps[:, 2 + i, :], a[:, k, :], w[:, kk, i * 512:(i + 1) * 512],
                                                      k == 0 and n_ == 0, k == 2 * FC - 1 and n_ == 2)
                                last.then_inc(unit_used, 1)
                                if d == 0:
                                    turn_h(FC - 1, it, b)
                                if d == 1:
                                    pe.wait_ge(h_here, 88 * p + 11 * b + FC + 2 + 22 * it)
                                    gather(b + 1, it)
                scatter(E, 0, (E + 1) % 2)

            experts(0)
            full = pe.value_load(cint[0:1, 0:1], min_val=0, max_val=T)
            with pe.If(full > P):
                experts(1)


_INS = ["x", "dn_w_in", "dn_conv_w", "dn_a_log", "dn_dt_bias", "dn_norm_w", "dn_w_out", "w_kv_shared", "sw_w_q",
        "sw_sinks", "sw_w_out", "ffn_w_gu", "ffn_w_down", "moe_w_router", "moe_w_gu", "moe_w_down", "ln_g", "ln_b"]


def kernel(**inputs):
    import numpy as np
    import concourse.bacc as bacc
    from concourse.bass_utils import run_bass_kernel_spmd

    nc = bacc.Bacc("TRN2", target_bir_lowering=False, num_devices=1)
    arrays, args = {}, []
    for name in _INS:
        a = np.ascontiguousarray(inputs[name])
        arrays[f"in_{name}"] = a
        args.append(nc.dram_tensor(f"in_{name}", a.shape, mybir.dt.from_np(a.dtype), kind="ExternalInput").ap())
    args.append(nc.dram_tensor("out_0", inputs["x"].shape, F32, kind="ExternalOutput").ap())
    trunk(nc, *args)
    return run_bass_kernel_spmd(nc, [arrays], core_ids=[0]).results[0]["out_0"]
```

```python
from contextlib import ExitStack

import concourse.bass as bass
from concourse import mybir

ALU = mybir.AluOpType
ACT = mybir.ActivationFunctionType
AX = mybir.AxisListType
F32 = mybir.dt.float32
F32R = mybir.dt.float32r
U32 = mybir.dt.uint32
I32 = mybir.dt.int32

P = 128
BIG = 1.0e30

UNIT = 2048
RAW = 6
CUT = 3
AHEAD = 3


def trunk(nc, x_in, w_in, conv_w, a_log, dt_bias, norm_w, w_out, w_kv, w_q, sinks, w_o, w_gu, w_down,
          w_router, moe_gu, moe_down, ln_g, ln_b, out):
    _, T, D = x_in.shape
    NB = T // P
    KD = D // P
    H = a_log.shape[1]
    DK = P
    TAPS = conv_w.shape[1]
    QKV = conv_w.shape[2] // P
    HQ = sinks.shape[1]
    HKV = 4
    GQ = HQ // HKV
    HD = w_kv.shape[1] // (2 * HKV)
    FF = w_down.shape[1]
    FC = FF // 256
    E = w_router.shape[2]
    ALPHA = float(4 ** 0.25)
    assert (T, D, H, FF, E, NB) == (256, 1024, 8, 2816, 8, 2) and HD == 64

    U_QKV = 0
    U_Z = U_QKV + QKV // 2
    U_OUT = U_Z + 4
    U_GU = U_OUT + 4
    U_DOWN = U_GU + 2 * FC
    U_KV = U_DOWN + FC
    U_Q = U_KV + 2
    U_O = U_Q + 4
    U_MOE = U_O + 4
    PER_E = 3 * FC
    PER_IT = 2 * PER_E
    TURNS = E // 2
    assert PER_IT % RAW == 0 and PER_IT % CUT == 0

    ctx = ExitStack()
    with ctx:
        def sb(name, shape, dt=F32, where=None):
            return (where or ctx).enter_context(nc.sbuf_tensor(name, shape, dt))

        def sem(name):
            return ctx.enter_context(nc.semaphore(name))

        raw = sb("raw", [P, RAW, UNIT])
        hi = sb("hi", [P, CUT, UNIT], F32R)
        lo = sb("lo", [P, CUT, UNIT], F32R)
        x = sb("x", [P, NB, D])
        lng = sb("lng", [P, D])
        lnb = sb("lnb", [P, D])
        ident = sb("ident", [P, P])
        ones = sb("ones", [P, P])
        tri_incl = sb("tri_incl", [P, P])
        mhalf = sb("mhalf", [P, NB * H])
        bnst = sb("bnst", [P, NB, 2, 6])
        bnmv = sb("bnmv", [P, NB, 2])
        lnve = sb("lnve", [P, NB])
        lnrs = sb("lnrs", [P, NB])
        ps = ctx.enter_context(nc.psum_tensor("ps", [P, 8, 512], F32))

        with ExitStack() as a:
            Dm = sb("Dm", [P, NB * H, P], where=a)
            DT = sb("DT", [P, NB * H, P], where=a)
            conv = sb("conv", [P, QKV, T], where=a)
            zn = sb("zn", [P, NB, D], where=a)
            kt = sb("kt", [P, NB, H, P], where=a)
            vb = sb("vb", [P, NB, H, P], where=a)
            Tm = sb("Tm", [P, NB * H, P], where=a)
            Nm = sb("Nm", [P, NB * H, P], where=a)
            masks = sb("masks", [P, 7, P], where=a)
            masksT = sb("masksT", [P, 2, P], where=a)
            cw_rows = sb("cw_rows", [TAPS * QKV, P], where=a)
            cw = sb("cw", [P, TAPS * QKV], where=a)
            wab = sb("wab", [P, KD, 2 * H], where=a)
            wab_hi = sb("wab_hi", [P, KD, 2 * H], F32R, where=a)
            wab_lo = sb("wab_lo", [P, KD, 2 * H], F32R, where=a)
            alog = sb("alog", [P, H], where=a)
            dtb = sb("dtb", [P, H], where=a)
            nw = sb("nw", [P, DK], where=a)
            eG = sb("eG", [P, H, P], where=a)
            abT = sb("abT", [2 * H, T], where=a)
            ab = sb("ab", [P, NB, 2 * H], where=a)
            beta = sb("beta", [P, NB, H], where=a)
            nbeta = sb("nbeta", [P, NB, H], where=a)
            g = sb("g", [P, NB, H], where=a)
            G = sb("G", [P, NB, H], where=a)
            sp = [sb(f"sp{i}", [P, NB, H], where=a) for i in range(6)]
            ea = sb("ea", [P, H], where=a)
            egl = sb("egl", [P, H], where=a)
            eg = sb("eg", [P, H], where=a)
            ss = sb("ss", [P, 2, H, NB], where=a)
            rk = sb("rk", [P, H, NB], where=a)
            ms = sb("ms", [P, NB * H], where=a)
            fo = sb("fo", [P, NB * H], where=a)
        xT_hi = sb("xT_hi", [P, KD, T], F32R)
        xT_lo = sb("xT_lo", [P, KD, T], F32R)
        with ExitStack() as a:
            hT_hi = sb("hT_hi", [P, 2 * FC, T], F32R, where=a)
            hT_lo = sb("hT_lo", [P, 2 * FC, T], F32R, where=a)
            sg = sb("sg", [P, 2, 512], where=a)
            hf = sb("hf", [P, 2, 512], where=a)
        with ExitStack() as a:
            kT2 = sb("kT2", [P, HKV, 2, T], where=a)
            vB = sb("vB", [P, NB, HKV * HD], where=a)
            qT = sb("qT", [P, KD, T], where=a)
            dist = sb("dist", [P, 3 * P], where=a)
            sS = sb("sS", [P, 2, GQ, 3 * P], where=a)
            pT = sb("pT", [P, 3 * GQ, P], where=a)
            oT_hi = sb("oT_hi", [P, KD, T], F32R, where=a)
            oT_lo = sb("oT_lo", [P, KD, T], F32R, where=a)
            sk = sb("sk", [P, HQ], where=a)
            smax = sb("smax", [P, 2, NB, GQ], where=a)
            nmax = sb("nmax", [P, 2, NB, GQ], where=a)
            ske = sb("ske", [P, 2, NB, GQ], where=a)
            ssum = sb("ssum", [P, 2, NB, GQ], where=a)
            sinv = sb("sinv", [P, 2, NB, GQ], where=a)
        x3_hi = sb("x3_hi", [P, NB, D], F32R)
        x3_lo = sb("x3_lo", [P, NB, D], F32R)
        xg_hi = sb("xg_hi", [P, KD, 2, P], F32R)
        xg_lo = sb("xg_lo", [P, KD, 2, P], F32R)
        sgE = sb("sgE", [P, 2, 256])
        actE = sb("actE", [P, 2, 256])
        hE_hi = sb("hE_hi", [P, 2 * FC, P], F32R)
        hE_lo = sb("hE_lo", [P, 2 * FC, P], F32R)
        y_hi = sb("y_hi", [P, D], F32R)
        y_lo = sb("y_lo", [P, D], F32R)
        oneh = sb("oneh", [P, NB, 2, P], F32R)
        onehT = sb("onehT", [P, 2, NB, P], F32R)
        gslot = sb("gslot", [P, 2])
        iota = sb("iota", [P, 2, P])
        tri_strict = sb("tri_strict", [P, P])
        wr = sb("wr", [P, KD, E])
        wr_hi = sb("wr_hi", [P, KD, E], F32R)
        wr_lo = sb("wr_lo", [P, KD, E], F32R)
        rev = sb("rev", [P, E])
        lgT = sb("lgT", [E, T])
        lg = sb("lg", [P, NB, E])
        lg2 = sb("lg2", [P, NB, E])
        eq = sb("eq", [P, NB, E])
        oh1 = sb("oh1", [P, NB, E])
        oh2 = sb("oh2", [P, NB, E])
        sel = sb("sel", [P, NB, E])
        m1 = sb("m1", [P, NB, 1])
        m2 = sb("m2", [P, NB, 1])
        rr = sb("rr", [P, NB, 1])
        gw = sb("gw", [P, NB, 4])
        pos = sb("pos", [P, NB, E + 2])
        gates = sb("gates", [P, NB, E + 2])
        cmax = sb("cmax", [P, 1])
        cint = sb("cint", [P, 1], I32)

        raw_in = [sem(f"raw_in{i}") for i in range(RAW)]
        hi_ready, lo_ready, unit_used = sem("hi_ready"), sem("lo_ready"), sem("unit_used")
        x_here, small_here, bcast_here = sem("x_here"), sem("small_here"), sem("bcast_here")
        ln_here, sink_here = sem("ln_here"), sem("sink_here")
        consts = sem("consts")
        turned, turn_hi, turn_lo = sem("turned"), sem("turn_hi"), sem("turn_lo")
        ln_var, ln_rstd, ln_done = sem("ln_var"), sem("ln_rstd"), [sem(f"ln_done{b}") for b in range(NB)]
        conv_step, tap_ready, silu_done = sem("conv_step"), sem("tap_ready"), sem("silu_done")
        z_done, cw_turned, cw_here = sem("z_done"), sem("cw_turned"), sem("cw_here")
        ab_cut, ab_mm, ab_here = sem("ab_cut"), sem("ab_mm"), sem("ab_here")
        g_act, g_dve, g_pe = sem("g_act"), sem("g_dve"), sem("g_pe")
        block0_done, x_scaled = sem("block0_done"), sem("x_scaled")
        q_turned, q_squared, k_squared, ss_here, rk_here = (
            sem(n) for n in ("q_turned", "q_squared", "k_squared", "ss_here", "rk_here"))
        kv_turned, kv_taken = sem("kv_turned"), sem("kv_taken")
        gdiff, gmin, decay_here, dmul = sem("gdiff"), sem("gmin"), sem("decay_here"), sem("dmul")
        kback, kback_taken = sem("kback"), sem("kback_taken")
        kk_mm, kk_taken, kq_taken, kq_decayed = (sem(n) for n in ("kk_mm", "kk_taken", "kq_taken", "kq_decayed"))
        kscaled, qg_here = sem("kscaled"), sem("qg_here")
        inv_id, inv_p, inv_pc, inv_r, inv_rc = (sem(f"inv_{n}") for n in ("id", "p", "pc", "r", "rc"))
        scan_mm, scan_ev = sem("scan_mm"), sem("scan_ev")
        o_mm, o_sq, o_ms, o_rms, o_done = (sem(f"o_{n}") for n in ("mm", "sq", "ms", "rms", "done"))
        zn_done = sem("zn_done")
        ffn_silu, ffn_act, ffn_hi, ffn_lo = sem("ffn_silu"), sem("ffn_act"), sem("ffn_hi"), sem("ffn_lo")
        kB_act, kB_dve, vB_here, qB_here = sem("kB_act"), sem("kB_dve"), sem("vB_here"), sem("qB_here")
        sc_mm, sc_max, sc_exp, sc_prob = sem("sc_mm"), sem("sc_max"), sem("sc_exp"), sem("sc_prob")
        pt_mm, pt_taken, pv_mm, pv_hi, pv_lo = (sem(f"{n}") for n in ("pt_mm", "pt_taken", "pv_mm", "pv_hi", "pv_lo"))
        sc_bias = sem("sc_bias")
        lgT_here, wab_here, wr_here, slots_mm = sem("lgT_here"), sem("wab_here"), sem("wr_here"), sem("slots_mm")
        wr_cut, x3_cut, lg_mm, sel_here, w2_here = (sem(n) for n in ("wr_cut", "x3_cut", "lg_mm", "sel_here", "w2_here"))
        w2_arg, pos_mm, route_here, moe_zero = (sem(n) for n in ("w2_arg", "pos_mm", "route_here", "moe_zero"))
        oneh_here, gathered, xg_hi_here, xg_here = (sem(n) for n in ("oneh_here", "gathered", "xg_hi_here", "xg_here"))
        slots_here = sem("slots_here")
        silu_here, act_here, ff_turned, h_hi, h_here = (sem(n) for n in ("silu_here", "act_here", "ff_turned", "h_hi", "h_here"))
        y_hi_here, y_here, scattered, acc_added = (sem(n) for n in ("y_hi_here", "y_here", "scattered", "acc_added"))
        out_done = sem("out_done")
        dve_chain, act_chain, pool_chain = sem("dve_chain"), sem("act_chain"), sem("pool_chain")

        def columns(w, n0, n1, width):
            return w[:, n0:n1].rearrange("(k p) (c n) -> c p k n", p=P, n=width)

        qkv_v = columns(w_in[0], 0, QKV * P, 256)
        z_v = w_in[0][:, QKV * P:QKV * P + D].rearrange("(a k p) (c n) -> a c p k n", p=P, k=4, n=512)
        out_v = w_out[0].rearrange("(u k p) n -> u p k n", p=P, k=2)
        gu_v = columns(w_gu[0], 0, 2 * FF, 256)
        down_v = w_down[0].rearrange("(u k p) n -> u p k n", p=P, k=2)
        kv_v = columns(w_kv, 0, 2 * HKV * HD, 256)
        q_v = columns(w_q[0], 0, D, 256)
        o_v = w_o[0].rearrange("(u k p) n -> u p k n", p=P, k=2)
        mgu_v = moe_gu[0].rearrange("e (a k p) (t c n) -> a c e p k t n", p=P, k=4, t=2, n=256)
        mdown_v = moe_down[0].rearrange("e (u k p) n -> u e p k n", p=P, k=2)

        block = ctx.enter_context(nc.Block())

        def slot(buf, j):
            return buf[:, j % (RAW if buf is raw else CUT), :]

        def xT_part(buf, s):
            return buf[:, 4 * (s % 2):4 * (s % 2) + 4, (s // 2) * P:(s // 2) * P + P]

        @block.sync
        def _(sp_):
            def load(j, it, src, view, **dims):
                if j >= RAW:
                    sp_.wait_ge(lo_ready, j - RAW + 1 + PER_IT * it)
                dst = slot(raw, j).rearrange(view, **dims)
                for half in range(2):
                    if len(dst.shape) == 4:
                        d, s = dst[:, :, half, :], src[:, :, half, :]
                    else:
                        k = slice(half * dst.shape[1] // 2, (half + 1) * dst.shape[1] // 2)
                        d, s = dst[:, k, :], src[:, k, :]
                    sp_.dma_start(d, s).then_inc(raw_in[j % RAW], 16)

            for b in range(NB):
                sp_.dma_start(x[:, b, :], x_in[0].rearrange("(b p) d -> b p d", p=P)[b]).then_inc(x_here, 16)
            for u in range(QKV // 2):
                load(U_QKV + u, 0, qkv_v[u], "p (k n) -> p k n", k=KD)
            for u in range(4):
                load(U_Z + u, 0, z_v[u % 2, u // 2], "p (k n) -> p k n", k=4)
            for u in range(4):
                load(U_OUT + u, 0, out_v[u], "p (k n) -> p k n", k=2)
            for c in range(FC):
                for t in range(2):
                    load(U_GU + 2 * c + t, 0, gu_v[t * FC + c], "p (k n) -> p k n", k=KD)
            for u in range(FC):
                load(U_DOWN + u, 0, down_v[u], "p (k n) -> p k n", k=2)
            for u in range(2):
                load(U_KV + u, 0, kv_v[u], "p (k n) -> p k n", k=KD)
            for u in range(4):
                load(U_Q + u, 0, q_v[u], "p (k n) -> p k n", k=KD)
            for u in range(4):
                load(U_O + u, 0, o_v[u], "p (k n) -> p k n", k=2)

            def expert_unit(base, l, it):
                e = 2 * it + l // PER_E
                if l // PER_E == 2:
                    e = e % E
                u = l % PER_E
                if u < 2 * FC:
                    load(base + l, it, mgu_v[u % 2, u // 2][e], "p (k t n) -> p k t n", k=4, t=2)
                else:
                    load(base + l, it, mdown_v[u - 2 * FC][e], "p (k n) -> p k n", k=2)

            for l in range(AHEAD):
                expert_unit(U_MOE, l, 0)

            def experts(base):
                with sp_.Fori(0, TURNS) as it:
                    for l in range(AHEAD, PER_IT + AHEAD):
                        expert_unit(base, l, it)

            experts(U_MOE)
            sp_.wait_ge(route_here, 1)
            full = sp_.value_load(cint[0:1, 0:1], min_val=0, max_val=T)
            with sp_.If(full > P):
                experts(U_MOE + E * PER_E)
            for b in range(NB):
                sp_.wait_ge(ln_done[b], 4)
                sp_.dma_start(out[0].rearrange("(b p) d -> b p d", p=P)[b], x[:, b, :]).then_inc(out_done, 16)
            sp_.wait_ge(out_done, 16 * NB)

        @block.gpsimd
        def _(pool):
            n = [0]

            def link(ins):
                n[0] += 1
                ins.then_inc(pool_chain, 1)

            def settle():
                pool.wait_ge(pool_chain, n[0])

            def select(t, op, fill, base, pattern, mult):
                settle()
                link(pool.affine_select(out=t, in_=t, compare_op=op, fill=fill, base=base,
                                        pattern=pattern, channel_multiplier=mult))

            link(pool.memset(ident[:, :], 0.0))
            select(ident[:, :], ALU.not_equal, 1.0, 0, [[-1, P]], 1)
            settle()
            pool.sem_inc(consts, 1)
            pool.dma_start(alog[:, :], a_log[0].partition_broadcast(P)).then_inc(bcast_here, 16)
            pool.dma_start(dtb[:, :], dt_bias[0].partition_broadcast(P)).then_inc(bcast_here, 16)
            pool.dma_start(nw[:, :], norm_w[0].partition_broadcast(P)).then_inc(bcast_here, 16)

            def load_ln(layer, i):
                pool.dma_start(lng[:, :], ln_g[layer, i].partition_broadcast(P)).then_inc(ln_here, 16)
                pool.dma_start(lnb[:, :], ln_b[layer, i].partition_broadcast(P)).then_inc(ln_here, 16)

            load_ln(0, 0)
            link(pool.memset(mhalf[:, :], -0.5))
            link(pool.memset(ones[:, :], 1.0))
            link(pool.memset(tri_incl[:, :], 1.0))
            select(tri_incl[:, :], ALU.is_ge, 0.0, 0, [[1, P]], -1)
            link(pool.memset(masks[:, :, :], 0.0))
            link(pool.memset(masksT[:, :, :], 0.0))
            settle()
            for i in range(7):
                b = 1 << i
                m = masks[:, i, :].rearrange("p (n h b) -> p n h b", h=2, b=b)[:, :, 0, :]
                nb = P // (2 * b)
                link(pool.memset(m, 1.0))
                select(m, ALU.is_ge, 0.0, -b, [[-2 * b, nb], [0, b]], 1)
                select(m, ALU.is_ge, 0.0, 2 * b - 1, [[2 * b, nb], [0, b]], -1)
                if i >= 5:
                    mt = masksT[:, i - 5, :].rearrange("p (n h b) -> p n h b", h=2, b=b)[:, :, 1, :]
                    link(pool.memset(mt, 1.0))
                    select(mt, ALU.is_ge, 0.0, 0, [[-2 * b, nb], [0, b]], 1)
                    select(mt, ALU.is_ge, 0.0, b - 1, [[2 * b, nb], [0, b]], -1)
            settle()
            pool.sem_inc(consts, 1)

            def rsqrt(dst, src):
                return pool.tensor_tensor(dst, src, mhalf[:, 0:src.shape[1]], ALU.pow)

            pool.wait_ge(decay_here, 4)
            for gr in range(4):
                s = slice(4 * gr, 4 * gr + 4)
                link(pool.tensor_tensor(Tm[:, s, :], Nm[:, s, :], tri_incl[:, :].unsqueeze(1).to_broadcast([P, 4, P]),
                                        ALU.mult))
            settle()
            for gr in range(4):
                s = slice(4 * gr, 4 * gr + 4)
                pool.tensor_tensor(Nm[:, s, :], Nm[:, s, :],
                                   nbeta[:, gr // 2, 4 * (gr % 2):4 * (gr % 2) + 4].unsqueeze(2).to_broadcast([P, 4, P]),
                                   ALU.mult).then_inc(dmul, 1)
            pool.wait_ge(ss_here, 1)
            rsqrt(rk[:, :, :].rearrange("p h b -> p (h b)"), ss[:, 1, :, :].rearrange("p h b -> p (h b)")).then_inc(rk_here, 1)
            pool.wait_ge(kback, 4)
            for c, s in ((0, egl), (1, eg)):
                pool.tensor_tensor(kt[:, c, :, :], kt[:, c, :, :],
                                   s[:, :].unsqueeze(2).to_broadcast([P, H, P]), ALU.mult).then_inc(kscaled, 1)
            for gr in range(4):
                s = slice(4 * gr, 4 * gr + 4)
                pool.wait_ge(kq_taken, gr + 1)
                pool.tensor_tensor(DT[:, s, :], DT[:, s, :], Tm[:, s, :], ALU.mult).then_inc(kq_decayed, 1)
            pool.wait_ge(g_act, 7)
            pool.wait_ge(kk_mm, 4)
            pool.tensor_tensor(conv[:, 0:H, P:T], conv[:, 0:H, P:T], eG[:, :, :], ALU.mult).then_inc(qg_here, 1)
            pool.wait_ge(z_done, 4)
            pool.wait_ge(bcast_here, 48)
            for b in range(NB):
                v = zn[:, b, :].rearrange("p (h d) -> p h d", h=H)
                pool.tensor_tensor(v, v, nw[:, :].unsqueeze(1).to_broadcast([P, H, P]), ALU.mult).then_inc(zn_done, 1)
            for gr in range(4):
                pool.wait_ge(o_ms, gr + 1)
                rsqrt(fo[:, 4 * gr:4 * gr + 4], ms[:, 4 * gr:4 * gr + 4]).then_inc(o_rms, 1)

            def norm(i):
                for b in range(NB):
                    pool.wait_ge(ln_var, 2 * i + b + 1)
                    rsqrt(lnrs[:, b:b + 1], lnve[:, b:b + 1]).then_inc(ln_rstd, 1)
                if i < 3:
                    pool.wait_ge(ln_done[0], i + 1)
                    pool.wait_ge(ln_done[1], i + 1)
                    load_ln((i + 1) // 2, (i + 1) % 2)

            norm(0)
            link(pool.memset(tri_strict[:, :], 1.0))
            select(tri_strict[:, :], ALU.is_gt, 0.0, 0, [[1, P]], -1)
            for i in range(2):
                link(pool.iota(iota[:, i, :], [[1, P]], base=i * P, channel_multiplier=0,
                               allow_small_or_imprecise_dtypes=True))
            link(pool.iota(rev[:, :], [[-1, E]], base=E, channel_multiplier=0, allow_small_or_imprecise_dtypes=True))
            link(pool.memset(pos[:, :, :], -1.0))
            link(pool.memset(gates[:, :, :], 0.0))
            link(pool.memset(onehT[:, 1, :, :].bitcast(F32), 0.0))
            pool.dma_start(wr[:, :, :], w_router[0].rearrange("(k p) e -> p k e", p=P)).then_inc(wr_here, 16)
            settle()
            pool.sem_inc(consts, 1)
            norm(1)
            link(pool.memset(kT2[64:128, :, 0, :], 0.0))
            link(pool.memset(kT2[0:64, :, 1, :], 0.0))
            settle()
            pool.dma_start(sk[:, :], sinks[0].partition_broadcast(P)).then_inc(sink_here, 16)
            for c, (base, op) in enumerate(((0, ALU.is_ge), (P, ALU.is_gt), (0, ALU.is_ge))):
                d = dist[:, c * P:(c + 1) * P]
                link(pool.iota(d, [[-1, P]], base=base, channel_multiplier=1, allow_small_or_imprecise_dtypes=True))
                if c == 1:
                    select(d, ALU.is_gt, BIG, 0, [[1, P]], -1)
                else:
                    select(d, ALU.is_ge, BIG, 0, [[-1, P]], 1)
            settle()
            pool.sem_inc(consts, 1)
            norm(2)
            for i in range(2):
                if i == 1:
                    pool.wait_ge(route_here, 1)
                    full = pool.value_load(cint[0:1, 0:1], min_val=0, max_val=T)
                with (pool.If(full > P) if i == 1 else ExitStack()):
                    if i == 1:
                        pool.wait_ge(scattered, 2 * (E + 1))
                    pool.memset(y_hi[:, :].bitcast(F32), 0.0).then_inc(moe_zero, 1)
                    pool.memset(y_lo[:, :].bitcast(F32), 0.0).then_inc(moe_zero, 1)
            norm(3)

        Q_BANK = (3, 7)
        O_BANK = (6, 7, 2, 3)

        def scan_moves():
            vn = vb[:, 0, :, :], vb[:, 1, :, :]
            Wt = Dm[:, 0:H, :]
            S = Dm[:, H:2 * H, :]
            return [(vn[0][:, 0:4, :], 0), (vn[0][:, 4:8, :], 1), (Wt[:, 0:4, :], 2), (Wt[:, 4:8, :], 3),
                    (S[:, 0:4, :], 4), (S[:, 4:8, :], 5), (vn[1][:, 0:4, :], 0), (vn[1][:, 4:8, :], 1)]

        @block.scalar
        def _(act):
            def cut_hi(j, it=0):
                act.wait_ge(raw_in[j % RAW], 32 * (j // RAW + 1) + 32 * (PER_IT // RAW) * it)
                if j >= CUT:
                    act.wait_ge(unit_used, j - CUT + 1 + PER_IT * it)
                act.activation(slot(hi, j), slot(raw, j), ACT.Copy).then_inc(hi_ready, 1)

            def used(j, it=0):
                act.wait_ge(unit_used, j + 1 + PER_IT * it)

            def copy(dst, src, scale=1.0):
                return act.activation(dst, src, ACT.Copy, scale=scale)

            def turn(i):
                for s in range(4):
                    act.wait_ge(turned, 4 * i + s + 1)
                    copy(xT_part(xT_hi, s), ps[:, 4 + s, :].rearrange("p (k t) -> p k t", k=4)).then_inc(turn_hi, 1)

            act.dma_start(wab[:, :, :], w_in[0][:, QKV * P + D:].rearrange("(k p) n -> p k n", p=P)).then_inc(wab_here, 16)
            act.dma_start(cw_rows[:, :], conv_w[0].rearrange("a (c p) -> (a c) p", p=P)).then_inc(small_here, 16)
            act.wait_ge(wab_here, 16)
            copy(wab_hi[:, :, :], wab[:, :, :]).then_inc(ab_cut, 1)
            turn(0)
            cut_hi(0)
            act.wait_ge(cw_turned, 1)
            copy(cw[:, :], ps[:, 0, 0:TAPS * QKV]).then_inc(cw_here, 1)
            cut_hi(1)
            cut_hi(2)
            act.wait_ge(cw_here, 1)

            def project(u):
                used(U_QKV + u)
                for m in range(2):
                    t = 2 * u + m
                    act.activation(conv[:, t, :], ps[:, t % 4, 0:T], ACT.Copy,
                                   scale=cw[:, (TAPS - 1) * QKV + t:(TAPS - 1) * QKV + t + 1]).then_inc(tap_ready, 1)
                cut_hi(U_QKV + u + AHEAD)
                act.wait_ge(conv_step, 12 + 6 * (u + 1))
                act.activation(conv[:, 2 * u:2 * u + 2, :], conv[:, 2 * u:2 * u + 2, :], ACT.Silu).then_inc(silu_done, 1)

            def squares(which, ready_, done, junk):
                for gr in range(4):
                    b, h0 = gr // 2, 4 * (gr % 2)
                    act.wait_ge(ready_, gr + 1)
                    for i in range(4):
                        last = act.activation(junk(gr, i), ps[:, 4 + gr, i * P:(i + 1) * P], ACT.Square,
                                              accum_out=ss[:, which, h0 + i, b:b + 1])
                    last.then_inc(done, 1)

            project(0)
            project(1)
            act.wait_ge(g_dve, 1)
            act.activation(sp[0][:, :, :], ab[:, :, 0:H], ACT.Exp, scale=-1.0).then_inc(g_act, 1)
            act.activation(sp[3][:, :, :], sp[2][:, :, :], ACT.Exp, scale=-1.0).then_inc(g_act, 1)
            act.wait_ge(bcast_here, 48)
            act.activation(ea[:, :], alog[:, :], ACT.Exp).then_inc(g_act, 1)
            project(2)
            act.wait_ge(g_dve, 2)
            act.activation(sp[5][:, :, :], sp[4][:, :, :], ACT.Ln).then_inc(g_act, 1)
            for u in range(3, 6):
                project(u)
            act.wait_ge(g_dve, 4)
            act.activation(eg[:, :], G[:, 1, :], ACT.Exp).then_inc(g_act, 1)
            act.activation(egl[:, :], sp[0][:, 0, :], ACT.Exp).then_inc(g_act, 1)
            project(6)
            act.wait_ge(gdiff, 4)
            act.activation(eG[:, :, :], ps[:, 6:8, :].rearrange("p b (h c) -> p (b h) c", c=P), ACT.Exp).then_inc(g_act, 1)
            project(7)
            squares(0, q_turned, q_squared, lambda gr, i: ps[:, 4 + gr, i * P:(i + 1) * P])
            project(8)
            for gr in range(4):
                s = slice(4 * gr, 4 * gr + 4)
                act.wait_ge(gmin, gr + 1)
                act.activation(Nm[:, s, :], Nm[:, s, :], ACT.Exp).then_inc(decay_here, 1)
            for u in range(9, 11):
                project(u)
            squares(1, kv_turned, k_squared, lambda gr, i: zn[:, gr // 2, (4 * (gr % 2) + i) * P:(4 * (gr % 2) + i + 1) * P])
            project(11)
            act.wait_ge(k_squared, 4)

            def gate(c):
                for b in range(NB):
                    act.activation(zn[:, b, 512 * c:512 * c + 512], ps[:, 2 * c + b, :], ACT.Silu).then_inc(z_done, 1)

            cut_hi(U_Z + 0 + AHEAD)
            used(U_Z + 1)
            gate(0)
            cut_hi(U_Z + 1 + AHEAD)
            cut_hi(U_Z + 2 + AHEAD)
            for gr in range(4):
                act.wait_ge(kback, gr + 1)
                copy(conv[:, H + 4 * (gr % 2):H + 4 * (gr % 2) + 4, P * (gr // 2):P * (gr // 2) + P],
                     ps[:, 4 + gr, :].rearrange("p (h t) -> p h t", h=4)).then_inc(kback_taken, 1)
            used(U_Z + 3)
            gate(1)

            def take_kq(gr):
                act.wait_ge(kk_mm, gr + 1)
                copy(DT[:, 4 * gr:4 * gr + 4, :], ps[:, 2 * (gr % 2) + 1, :].rearrange("p (h c) -> p h c", h=4)).then_inc(kq_taken, 1)

            def identity(gr):
                act.wait_ge(kq_decayed, gr + 1)
                copy(Tm[:, 4 * gr:4 * gr + 4, :], ident[:, :].unsqueeze(1).to_broadcast([P, 4, P])).then_inc(inv_id, 1)

            take_kq(0)
            for gr in range(1, 4):
                take_kq(gr)
                identity(gr - 1)
            identity(3)
            Pm = conv[:, 2 * H:3 * H, :].rearrange("p h (b t) -> p (h b) t", b=2)
            for q in range(4, 4 * 7):
                s = slice(4 * (q % 4), 4 * (q % 4) + 4)
                act.wait_ge(inv_p, q - 3)
                copy(Pm[:, s, :], ps[:, 4 + q % 2, :].rearrange("p (h c) -> p h c", h=4)).then_inc(inv_pc, 1)
            def take(first, end):
                for i, (dst, bank) in list(enumerate(scan_moves()))[first:end]:
                    act.wait_ge(scan_mm, i + 1)
                    act.activation(dst, ps[:, bank, :].rearrange("p (h c) -> p h c", h=4), ACT.Copy,
                                   scale=-1.0 if i in (2, 3) else 1.0).then_inc(scan_ev, 1)

            def o_squares(gr):
                act.wait_ge(o_mm, gr + 1)
                for i in range(4):
                    n_ = 4 * gr + i
                    last = act.activation(Pm[:, n_, :], ps[:, O_BANK[gr], i * P:(i + 1) * P], ACT.Square,
                                          accum_out=ms[:, n_:n_ + 1])
                last.then_inc(o_sq, 1)

            cut_hi(U_Z + 3 + AHEAD)
            take(0, 6)
            o_squares(0)
            o_squares(1)
            take(6, 8)
            o_squares(2)
            o_squares(3)
            turn(1)
            for u in range(4):
                cut_hi(U_OUT + u + AHEAD)
            turn(2)

            def ffn_round(c):
                act.wait_ge(ffn_act, c + 1)
                copy(hT_hi[:, 2 * c:2 * c + 2, :], hf[:, c % 2, :].rearrange("p (m t) -> p m t", m=2)).then_inc(ffn_hi, 1)

            for c in range(FC):
                cut_hi(U_GU + 2 * c + AHEAD)
                used(U_GU + 2 * c)
                act.activation(sg[:, c % 2, :], ps[:, 2 * (c % 3), :], ACT.Silu).then_inc(ffn_silu, 1)
                cut_hi(U_GU + 2 * c + 1 + AHEAD)
                if c >= 1:
                    ffn_round(c - 1)
            ffn_round(FC - 1)
            for u in range(FC):
                cut_hi(U_DOWN + u + AHEAD)
            turn(3)

            cut_hi(U_KV + AHEAD)
            used(U_KV)
            for m in range(2):
                copy(kT2[0:64, 2 * m, 0, :], ps[0:64, m, 0:T]).then_inc(kB_act, 1)
                copy(kT2[64:128, 2 * m, 1, :], ps[0:64, m, 0:T]).then_inc(kB_act, 1)
            cut_hi(U_KV + 1 + AHEAD)

            def queries(u):
                used(U_Q + u)
                for m in range(2):
                    copy(qT[:, 2 * u + m, :], ps[:, Q_BANK[u % 2], m * T:(m + 1) * T],
                         scale=float(HD) ** -0.5).then_inc(qB_here, 1)

            def exps(gi):
                st = gi % 2
                act.wait_ge(sc_max, gi + 1)
                for b in range(NB):
                    for i in range(GQ):
                        s = sS[:, st, i, 0:P] if b == 0 else sS[:, st, i, P:3 * P]
                        act.activation(s, s, ACT.Exp, bias=nmax[:, st, b, i:i + 1],
                                       accum_out=ssum[:, st, b, i:i + 1])
                act.activation(ske[:, st, :, :], ske[:, st, :, :], ACT.Exp).then_inc(sc_exp, 1)

            def turn_probs(gi):
                for r in range(3):
                    n_ = 3 * gi + r
                    act.wait_ge(pt_mm, n_ + 1)
                    copy(pT[:, 4 * r:4 * r + 4, :], ps[:, 4 + n_ % 2, :].rearrange("p (h q) -> p h q", h=4)).then_inc(pt_taken, 1)

            def attended(gi):
                act.wait_ge(pv_mm, gi + 1)
                copy(oT_hi[:, 2 * gi:2 * gi + 2, :], ps[:, 6, :].rearrange("p (k t) -> p k t", k=2)).then_inc(pv_hi, 1)

            queries(0)
            cut_hi(U_Q + 0 + AHEAD)
            queries(1)
            exps(0)
            queries(2)
            cut_hi(U_Q + 1 + AHEAD)
            queries(3)
            turn_probs(0)
            exps(1)
            attended(0)
            cut_hi(U_Q + 2 + AHEAD)
            turn_probs(1)
            exps(2)
            attended(1)
            cut_hi(U_Q + 3 + AHEAD)
            turn_probs(2)
            exps(3)
            attended(2)
            cut_hi(U_O + 0 + AHEAD)
            turn_probs(3)
            attended(3)
            for u in range(1, 4):
                cut_hi(U_O + u + AHEAD)

            act.wait_ge(wr_here, 16)
            copy(wr_hi[:, :, :], wr[:, :, :]).then_inc(wr_cut, 1)
            turn(4)
            copy(x3_hi[:, :, :], x[:, :, :]).then_inc(x3_cut, 1)
            act.wait_ge(x3_cut, 2)
            copy(x[:, :, :], x[:, :, :], scale=ALPHA).then_inc(x_scaled, 1)
            act.wait_ge(w2_arg, 1)
            act.activation(gw[:, :, 1:2], gw[:, :, 0:1], ACT.Exp).then_inc(w2_here, 1)

            def experts(p):
                base = U_MOE + p * E * PER_E

                def round_xg(pair, it):
                    act.wait_ge(gathered, 5 * p + pair + 1 + it)
                    for i in range(2):
                        copy(xg_hi[:, 4 * i:4 * i + 4, :, :].rearrange("p k e s -> p k (e s)"),
                             ps[:, 6 * i:6 * i + 2, :].rearrange("p b (k s) -> p (b k) s", k=2)).then_inc(xg_hi_here, 1)

                def slots(ge, it, par):
                    act.wait_ge(slots_mm, 9 * p + ge + 1 + 2 * it)
                    copy(onehT[:, par, :, :], ps[:, 4, 0:2 * P].rearrange("p (b t) -> p b t", b=2))
                    copy(gslot[:, par:par + 1], ps[:, 5, 0:1]).then_inc(slots_here, 1)

                def round_h(c, it, b):
                    gc = 88 * p + 11 * b + c
                    act.wait_ge(ff_turned, gc + 1 + 22 * it)
                    copy(hE_hi[:, 2 * c:2 * c + 2, :], ps[:, 6 + gc % 2, 0:2 * P].rearrange(
                        "p (m s) -> p m s", m=2)).then_inc(h_hi, 1)

                round_xg(0, 0)
                slots(0, 0, 0)
                with act.Fori(0, TURNS) as it:
                    for b in range(2):
                        for l in range(PER_E):
                            j = base + PER_E * b + l
                            if l < PER_E - 1:
                                cut_hi(j + AHEAD, it)
                            used(j, it)
                            if l < 2 * FC and l % 2 == 1:
                                c = l // 2
                                gc = 88 * p + 11 * b + c
                                act.activation(sgE[:, gc % 2, :], ps[:, gc % 2, 0:256], ACT.Silu).then_inc(silu_here, 1)
                                if c >= 1:
                                    round_h(c - 1, it, b)
                            elif l == 2 * FC + 1:
                                round_h(FC - 1, it, b)
                            elif l == 2 * FC + 4:
                                if b == 1:
                                    round_xg(1, it)
                                slots(b + 1, it, (b + 1) % 2)
                            elif l == PER_E - 1:
                                act.wait_ge(slots_here, 9 * p + b + 1 + 2 * it)
                                act.activation(y_hi[:, :], ps[:, 2:4, :].rearrange("p b n -> p (b n)"), ACT.Copy,
                                               scale=gslot[:, b:b + 1]).then_inc(y_hi_here, 1)
                                cut_hi(j + AHEAD, it)

            experts(0)
            act.wait_ge(route_here, 1)
            full = act.value_load(cint[0:1, 0:1], min_val=0, max_val=T)
            with act.If(full > P):
                experts(1)


        @block.vector
        def _(dve):
            n = [0]

            def link(ins):
                n[0] += 1
                ins.then_inc(dve_chain, 1)

            def settle():
                dve.wait_ge(dve_chain, n[0])

            def step(ins):
                link(ins)
                settle()

            def cut_lo(j, it=0):
                dve.wait_ge(hi_ready, j + 1 + PER_IT * it)
                dve.tensor_tensor(slot(lo, j), slot(raw, j), slot(hi, j).bitcast(F32), ALU.subtract).then_inc(lo_ready, 1)

            def used(j, it=0):
                dve.wait_ge(unit_used, j + 1 + PER_IT * it)

            def turn(i):
                for s in range(4):
                    dve.wait_ge(turn_hi, 4 * i + s + 1)
                    dve.tensor_tensor(xT_part(xT_lo, s), ps[:, 4 + s, :].rearrange("p (k t) -> p k t", k=4),
                                      xT_part(xT_hi, s).bitcast(F32), ALU.subtract).then_inc(turn_lo, 1)

            def norm(i, bank, last=None):
                for b in range(NB):
                    if bank is not None:
                        if b == 0:
                            dve.wait_ge(block0_done, i + 1)
                        else:
                            used(last)
                        step(dve.scalar_tensor_tensor(out=x[:, b, :], in0=x[:, b, :], scalar=ALPHA,
                                                      in1=ps[:, bank + 2 * b:bank + 2 * b + 2, :].rearrange("p b n -> p (b n)"),
                                                      op0=ALU.mult, op1=ALU.add))
                    for q in range(2):
                        link(dve.bn_stats(bnst[:, b, q, :], x[:, b, 512 * q:512 * q + 512]))
                    settle()
                    step(dve.bn_aggr(bnmv[:, b, :], bnst[:, b, :, :].rearrange("p q s -> p (q s)")))
                    dve.tensor_scalar(lnve[:, b:b + 1], bnmv[:, b, 1:2], 1e-5, None, ALU.add).then_inc(ln_var, 1)
                    if b == 0:
                        dve.wait_ge(ln_here, 32 * (i + 1))
                    step(dve.scalar_tensor_tensor(out=x[:, b, :], in0=x[:, b, :], scalar=bnmv[:, b, 0:1], in1=lng[:, :],
                                                  op0=ALU.subtract, op1=ALU.mult))
                    dve.wait_ge(ln_rstd, 2 * i + b + 1)
                    dve.scalar_tensor_tensor(out=x[:, b, :], in0=x[:, b, :], scalar=lnrs[:, b:b + 1], in1=lnb[:, :],
                                             op0=ALU.mult, op1=ALU.add).then_inc(ln_done[b], 1)

            def over(v, width=P):
                return v.unsqueeze(2).to_broadcast([P, v.shape[1], width])

            dve.sem_inc(conv_step, 12)
            dve.sem_inc(act_here, 2)
            dve.sem_inc(h_here, 2)
            dve.sem_inc(y_here, 1)
            dve.sem_inc(acc_added, 2)
            dve.wait_ge(ab_cut, 1)
            dve.tensor_tensor(wab_lo[:, :, :], wab[:, :, :], wab_hi[:, :, :].bitcast(F32), ALU.subtract).then_inc(ab_cut, 1)
            turn(0)
            cut_lo(0)
            cut_lo(1)
            cut_lo(2)
            dve.wait_ge(cw_here, 1)

            def project(u):
                for d in range(1, TAPS):
                    for m in range(2):
                        t = 2 * u + m
                        if d == 1:
                            dve.wait_ge(tap_ready, t + 1)
                        else:
                            dve.wait_ge(conv_step, 12 + 6 * u + 2 * (d - 2) + m + 1)
                        w = (TAPS - 1 - d) * QKV + t
                        dve.scalar_tensor_tensor(out=conv[:, t, d:T], in0=ps[:, t % 4, 0:T - d], scalar=cw[:, w:w + 1],
                                                 in1=conv[:, t, d:T], op0=ALU.mult, op1=ALU.add).then_inc(conv_step, 1)
                cut_lo(U_QKV + u + AHEAD)

            project(0)
            dve.wait_ge(ab_mm, 1)
            dve.tensor_copy(abT[:, :], ps[0:2 * H, 7, 0:T]).then_inc(ab_here, 1)
            project(1)
            dve.wait_ge(ab_mm, 2)
            step(dve.tensor_copy(ab[:, :, :], ps[:, 7, 0:4 * H].rearrange("p (b n) -> p b n", b=NB)))
            dve.wait_ge(bcast_here, 48)
            step(dve.tensor_tensor(sp[1][:, :, :], ab[:, :, H:2 * H], dtb[:, :].unsqueeze(1).to_broadcast([P, NB, H]), ALU.add))
            dve.scalar_tensor_tensor(out=sp[2][:, :, :], in0=sp[1][:, :, :], scalar=-1.0, in1=sp[1][:, :, :],
                                     op0=ALU.mult, op1=ALU.max).then_inc(g_dve, 1)
            project(2)
            dve.wait_ge(g_act, 2)
            link(dve.tensor_scalar(sp[0][:, :, :], sp[0][:, :, :], 1.0, None, ALU.add))
            dve.tensor_scalar(sp[4][:, :, :], sp[3][:, :, :], 1.0, None, ALU.add).then_inc(g_dve, 1)
            settle()
            step(dve.reciprocal(beta[:, :, :], sp[0][:, :, :]))
            link(dve.tensor_scalar(nbeta[:, :, :], beta[:, :, :], -1.0, None, ALU.mult))
            dve.wait_ge(g_dve, 2)
            link(dve.scalar_tensor_tensor(out=sp[3][:, :, :], in0=sp[4][:, :, :], scalar=-1.0, in1=sp[3][:, :, :],
                                          op0=ALU.add, op1=ALU.subtract))
            step(dve.reciprocal(sp[2][:, :, :], sp[4][:, :, :]))
            step(dve.tensor_tensor(sp[3][:, :, :], sp[3][:, :, :], sp[2][:, :, :], ALU.mult))
            project(3)
            dve.wait_ge(g_act, 4)
            step(dve.tensor_tensor(sp[5][:, :, :], sp[5][:, :, :], sp[3][:, :, :], ALU.subtract))
            step(dve.scalar_tensor_tensor(out=sp[1][:, :, :], in0=sp[1][:, :, :], scalar=0.0, in1=sp[5][:, :, :],
                                          op0=ALU.max, op1=ALU.add))
            dve.scalar_tensor_tensor(out=g[:, :, :], in0=sp[1][:, :, :], scalar=-1.0,
                                     in1=ea[:, :].unsqueeze(1).to_broadcast([P, NB, H]),
                                     op0=ALU.mult, op1=ALU.mult).then_inc(g_dve, 1)
            project(4)
            project(5)
            dve.wait_ge(g_pe, 1)
            step(dve.tensor_copy(G[:, :, :], ps[:, 6, 0:2 * H].rearrange("p (b h) -> p b h", b=NB)))
            dve.tensor_tensor(sp[0][:, 0, :], ps[:, 6, 2 * H:3 * H], G[:, 0, :], ALU.subtract).then_inc(g_dve, 1)
            project(6)
            for gr in range(4):
                s = slice(4 * gr, 4 * gr + 4)
                dve.wait_ge(g_pe, 2 + gr)
                dve.tensor_tensor(Nm[:, s, :], ps[:, 4 + gr, :].rearrange("p (h c) -> p h c", h=4),
                                  over(G[:, gr // 2, 4 * (gr % 2):4 * (gr % 2) + 4]), ALU.subtract).then_inc(gdiff, 1)
            dve.wait_ge(g_act, 5)
            dve.tensor_tensor(eg[:, :], eg[:, :], beta[:, 1, :], ALU.mult).then_inc(g_dve, 1)
            project(7)
            for gr in range(4):
                s = slice(4 * gr, 4 * gr + 4)
                dve.wait_ge(gdiff, gr + 1)
                dve.scalar_tensor_tensor(out=Nm[:, s, :], in0=Nm[:, s, :], scalar=-1.0, in1=Nm[:, s, :],
                                         op0=ALU.mult, op1=ALU.min).then_inc(gmin, 1)
            project(8)
            dve.wait_ge(q_squared, 4)
            link(dve.tensor_scalar(ss[:, 0, :, :], ss[:, 0, :, :], 1e-6, DK * 1e-6, ALU.add, ALU.mult))
            for u in range(9, QKV // 2):
                project(u)
            dve.wait_ge(k_squared, 4)
            dve.tensor_scalar(ss[:, 1, :, :], ss[:, 1, :, :], 1e-6, None, ALU.add).then_inc(ss_here, 1)
            cut_lo(U_Z + 0 + AHEAD)
            dve.wait_ge(rk_here, 1)
            for i in range(8):
                gr, hs = i % 4, slice(4 * (i % 2), 4 * (i % 2) + 4)
                b = gr // 2
                if i == 4:
                    cut_lo(U_Z + 1 + AHEAD)
                dve.wait_ge(kv_turned, i + 1)
                src = ps[:, 4 + gr, :].rearrange("p (h d) -> p h d", h=4)
                if i < 4:
                    dve.tensor_tensor(kt[:, b, hs, :], src, over(rk[:, hs, b]), ALU.mult).then_inc(kv_taken, 1)
                else:
                    dve.tensor_tensor(vb[:, b, hs, :], src, over(beta[:, b, hs]), ALU.mult).then_inc(kv_taken, 1)
            cut_lo(U_Z + 2 + AHEAD)

            def decayed(gr):
                s = slice(4 * gr, 4 * gr + 4)
                dve.wait_ge(kk_mm, gr + 1)
                dve.wait_ge(dmul, gr + 1)
                dve.tensor_tensor(Dm[:, s, :], ps[:, 2 * (gr % 2), :].rearrange("p (h c) -> p h c", h=4), Nm[:, s, :],
                                  ALU.mult).then_inc(kk_taken, 1)

            def join(q):
                s = slice(4 * (q % 4), 4 * (q % 4) + 4)
                lv = q // 4
                mk = masks[:, lv, :].bitcast(U32).unsqueeze(1).to_broadcast([P, 4, P])
                mt = masksT[:, max(lv - 5, 0), :].bitcast(U32).unsqueeze(1).to_broadcast([P, 4, P])
                if lv == 0:
                    dve.wait_ge(inv_id, q + 1)
                    dve.wait_ge(kk_taken, q + 1)
                    step(dve.copy_predicated(Tm[:, s, :], mk, Dm[:, s, :]))
                else:
                    dve.wait_ge(inv_r, q - 3)
                    if lv < 6:
                        product = ps[:, 6 + q % 2, :].rearrange("p (h c) -> p h c", h=4)
                        link(dve.copy_predicated(Tm[:, s, :], mk, product))
                if lv < 5:
                    settle()
                    dve.transpose(Nm[:, s, :], Tm[:, s, :]).then_inc(inv_rc, 1)
                else:
                    dve.copy_predicated(Nm[:, s, :], mt, ps[:, q % 2, :].rearrange("p (h c) -> p h c", h=4)).then_inc(inv_rc, 1)

            for gr in range(4):
                decayed(gr)
                join(gr)
            for q in range(4, 4 * 7):
                join(q)
            cut_lo(U_Z + 3 + AHEAD)
            def mean_square(gr):
                b, hs = gr // 2, slice(4 * (gr % 2), 4 * (gr % 2) + 4)
                dve.wait_ge(o_sq, gr + 1)
                s = slice(4 * gr, 4 * gr + 4)
                dve.scalar_tensor_tensor(out=ms[:, s], in0=ms[:, s], scalar=1.0 / DK, in1=ss[:, 0, hs, b],
                                         op0=ALU.mult, op1=ALU.add).then_inc(o_ms, 1)

            def gated(gr):
                dve.wait_ge(o_rms, gr + 1)
                for i in range(4):
                    n_ = 4 * gr + i
                    h = 4 * (gr % 2) + i
                    last = dve.scalar_tensor_tensor(out=Tm[:, n_, :], in0=ps[:, O_BANK[gr], i * P:(i + 1) * P],
                                                    scalar=fo[:, n_:n_ + 1], in1=zn[:, gr // 2, h * P:(h + 1) * P],
                                                    op0=ALU.mult, op1=ALU.mult)
                last.then_inc(o_done, 1)

            dve.wait_ge(zn_done, 2)
            for gr in (0, 2):
                mean_square(gr)
                mean_square(gr + 1)
                gated(gr)
                gated(gr + 1)
            turn(1)
            for u in range(2):
                cut_lo(U_OUT + u + AHEAD)
            norm(0, 0, U_OUT + 3)
            turn(2)
            for u in range(2, 4):
                cut_lo(U_OUT + u + AHEAD)

            def ffn_rest(c):
                dve.wait_ge(ffn_hi, c + 1)
                s = slice(2 * c, 2 * c + 2)
                dve.tensor_tensor(hT_lo[:, s, :], hf[:, c % 2, :].rearrange("p (m t) -> p m t", m=2),
                                  hT_hi[:, s, :].bitcast(F32), ALU.subtract).then_inc(ffn_lo, 1)

            for c in range(FC):
                cut_lo(U_GU + 2 * c + AHEAD)
                if c >= 1:
                    ffn_rest(c - 1)
                cut_lo(U_GU + 2 * c + 1 + AHEAD)
                used(U_GU + 2 * c + 1)
                dve.wait_ge(ffn_silu, c + 1)
                if c >= 2:
                    dve.wait_ge(ffn_lo, c - 1)
                dve.tensor_tensor(hf[:, c % 2, :], ps[:, 2 * (c % 3) + 1, :], sg[:, c % 2, :], ALU.mult).then_inc(ffn_act, 1)
            ffn_rest(FC - 1)
            for u in range(FC - 2):
                cut_lo(U_DOWN + u + AHEAD)
            norm(1, 4, U_DOWN + FC - 1)
            turn(3)
            for u in range(FC - 2, FC):
                cut_lo(U_DOWN + u + AHEAD)

            cut_lo(U_KV + AHEAD)
            used(U_KV)
            for m in range(2):
                dve.tensor_copy(kT2[0:64, 2 * m + 1, 0, :], ps[64:128, m, 0:T]).then_inc(kB_dve, 1)
                dve.tensor_copy(kT2[64:128, 2 * m + 1, 1, :], ps[64:128, m, 0:T]).then_inc(kB_dve, 1)
            cut_lo(U_KV + 1 + AHEAD)
            used(U_KV + 1)
            dve.tensor_copy(vB[:, :, :], ps[:, 6:8, 0:HKV * HD]).then_inc(vB_here, 1)
            dve.wait_ge(sink_here, 16)
            dve.wait_ge(consts, 4)

            def scores(gi):
                st = gi % 2
                dve.wait_ge(sc_mm, gi + 1)
                if gi >= 2:
                    dve.wait_ge(pt_mm, 3 * (gi - 1))
                for i in range(GQ):
                    slope = 2.0 ** (-8.0 * (GQ * gi + i + 1) / HQ)
                    dve.scalar_tensor_tensor(out=sS[:, st, i, 0:P], in0=dist[:, 0:P], scalar=-slope,
                                             in1=ps[:, 0, i * P:(i + 1) * P], op0=ALU.mult, op1=ALU.add)
                    last = dve.scalar_tensor_tensor(out=sS[:, st, i, P:3 * P], in0=dist[:, P:3 * P], scalar=-slope,
                                                    in1=ps[:, 1 + i // 2, (i % 2) * T:(i % 2) * T + T],
                                                    op0=ALU.mult, op1=ALU.add)
                last.then_inc(sc_bias, 1)
                dve.wait_ge(sc_bias, gi + 1)
                link(dve.tensor_reduce(smax[:, st, 0, :], sS[:, st, :, 0:P], AX.X, ALU.max))
                step(dve.tensor_reduce(smax[:, st, 1, :], sS[:, st, :, P:3 * P], AX.X, ALU.max))
                skb = sk[:, GQ * gi:GQ * gi + GQ].unsqueeze(1).to_broadcast([P, NB, GQ])
                step(dve.tensor_tensor(smax[:, st, :, :], smax[:, st, :, :], skb, ALU.max))
                link(dve.tensor_scalar(nmax[:, st, :, :], smax[:, st, :, :], -1.0, None, ALU.mult))
                dve.tensor_tensor(ske[:, st, :, :], skb, smax[:, st, :, :], ALU.subtract).then_inc(sc_max, 1)

            def probs(gi):
                st = gi % 2
                dve.wait_ge(sc_exp, gi + 1)
                step(dve.tensor_tensor(ssum[:, st, :, :], ssum[:, st, :, :], ske[:, st, :, :], ALU.add))
                step(dve.reciprocal(sinv[:, st, :, :], ssum[:, st, :, :]))
                dve.tensor_tensor(sS[:, st, :, 0:P], sS[:, st, :, 0:P], over(sinv[:, st, 0, :]), ALU.mult)
                dve.tensor_tensor(sS[:, st, :, P:3 * P], sS[:, st, :, P:3 * P], over(sinv[:, st, 1, :], 2 * P),
                                  ALU.mult).then_inc(sc_prob, 1)

            def attended(gi):
                dve.wait_ge(pv_hi, gi + 1)
                s = slice(2 * gi, 2 * gi + 2)
                dve.tensor_tensor(oT_lo[:, s, :], ps[:, 6, :].rearrange("p (k t) -> p k t", k=2),
                                  oT_hi[:, s, :].bitcast(F32), ALU.subtract).then_inc(pv_lo, 1)

            cut_lo(U_Q + 0 + AHEAD)
            scores(0)
            probs(0)
            scores(1)
            cut_lo(U_Q + 1 + AHEAD)
            probs(1)
            attended(0)
            scores(2)
            cut_lo(U_Q + 2 + AHEAD)
            probs(2)
            attended(1)
            scores(3)
            cut_lo(U_Q + 3 + AHEAD)
            attended(2)
            probs(3)
            cut_lo(U_O + 0 + AHEAD)
            attended(3)
            cut_lo(U_O + 1 + AHEAD)
            norm(2, 0, U_O + 3)

            dve.wait_ge(wr_cut, 1)
            dve.tensor_tensor(wr_lo[:, :, :], wr[:, :, :], wr_hi[:, :, :].bitcast(F32), ALU.subtract).then_inc(wr_cut, 1)
            turn(4)
            dve.wait_ge(x3_cut, 1)
            dve.tensor_tensor(x3_lo[:, :, :], x[:, :, :], x3_hi[:, :, :].bitcast(F32), ALU.subtract).then_inc(x3_cut, 1)
            dve.wait_ge(lg_mm, 1)
            dve.tensor_copy(lgT[:, :], ps[0:E, 0, 0:T]).then_inc(lgT_here, 1)
            dve.wait_ge(lg_mm, 2)
            step(dve.tensor_copy(lg[:, :, :], ps[:, 0, 0:2 * E].rearrange("p (b e) -> p b e", b=NB)))

            def first_max(src, m, oh):
                bc = [P, NB, E]
                step(dve.tensor_reduce(m[:, :, :], src[:, :, :], AX.X, ALU.max))
                step(dve.tensor_tensor(eq[:, :, :], src[:, :, :], m[:, :, :].to_broadcast(bc), ALU.is_equal))
                step(dve.tensor_tensor(eq[:, :, :], eq[:, :, :], rev[:, :].unsqueeze(1).to_broadcast(bc), ALU.mult))
                step(dve.tensor_reduce(rr[:, :, :], eq[:, :, :], AX.X, ALU.max))
                step(dve.tensor_tensor(oh[:, :, :], eq[:, :, :], rr[:, :, :].to_broadcast(bc), ALU.is_equal))

            dve.wait_ge(consts, 3)
            first_max(lg, m1, oh1)
            step(dve.scalar_tensor_tensor(out=lg2[:, :, :], in0=oh1[:, :, :], scalar=-3.0e38, in1=lg[:, :, :],
                                          op0=ALU.mult, op1=ALU.add))
            first_max(lg2, m2, oh2)
            dve.tensor_tensor(gw[:, :, 0:1], m2[:, :, :], m1[:, :, :], ALU.subtract).then_inc(w2_arg, 1)
            dve.tensor_tensor(sel[:, :, :], oh1[:, :, :], oh2[:, :, :], ALU.add).then_inc(sel_here, 1)
            dve.wait_ge(w2_here, 1)
            step(dve.tensor_scalar(gw[:, :, 2:3], gw[:, :, 1:2], 1.0, None, ALU.add))
            step(dve.reciprocal(gw[:, :, 2:3], gw[:, :, 2:3]))
            step(dve.tensor_tensor(gw[:, :, 3:4], gw[:, :, 1:2], gw[:, :, 2:3], ALU.mult))
            for b in range(NB):
                step(dve.tensor_scalar(gates[:, b, 0:E], oh1[:, b, :], gw[:, b, 2:3], None, ALU.mult))
                step(dve.scalar_tensor_tensor(out=gates[:, b, 0:E], in0=oh2[:, b, :], scalar=gw[:, b, 3:4],
                                              in1=gates[:, b, 0:E], op0=ALU.mult, op1=ALU.add))
            dve.wait_ge(pos_mm, 1)
            step(dve.scalar_tensor_tensor(out=lg2[:, :, :], in0=ps[:, 1, 0:2 * E].rearrange("p (b e) -> p b e", b=NB),
                                          scalar=1.0, in1=sel[:, :, :], op0=ALU.add, op1=ALU.mult))
            step(dve.tensor_scalar(pos[:, :, 0:E], lg2[:, :, :], -1.0, None, ALU.add))
            step(dve.tensor_reduce(cmax[:, :], ps[:, 1, 2 * E:3 * E], AX.X, ALU.max))
            dve.tensor_copy(cint[:, :], cmax[:, :]).then_inc(route_here, 1)

            def experts(p):
                base = U_MOE + p * E * PER_E

                def build(pair, it):
                    if p or pair:
                        dve.wait_ge(slots_mm, 9 * p + 2 * pair + 2 * it)
                    for i in range(2):
                        for b in range(NB):
                            last = dve.tensor_scalar(oneh[:, b, i, :], iota[:, p, :],
                                                     pos[:, b, bass.ds(2 * pair + i + 2 * it, 1)], None, ALU.is_equal)
                    last.then_inc(oneh_here, 1)

                def rest_xg(pair, it):
                    for i in range(2):
                        dve.wait_ge(xg_hi_here, 10 * p + 2 * pair + i + 1 + 2 * it)
                        part = slice(4 * i, 4 * i + 4)
                        last = dve.tensor_tensor(xg_lo[:, part, :, :].rearrange("p k e s -> p k (e s)"),
                                                 ps[:, 6 * i:6 * i + 2, :].rearrange("p b (k s) -> p (b k) s", k=2),
                                                 xg_hi[:, part, :, :].rearrange("p k e s -> p k (e s)").bitcast(F32), ALU.subtract)
                    last.then_inc(xg_here, 1)

                def rest_h(c, it, b):
                    gc = 88 * p + 11 * b + c
                    dve.wait_ge(h_hi, gc + 1 + 22 * it)
                    dve.tensor_tensor(hE_lo[:, 2 * c:2 * c + 2, :],
                                      ps[:, 6 + gc % 2, 0:2 * P].rearrange("p (m s) -> p m s", m=2),
                                      hE_hi[:, 2 * c:2 * c + 2, :].bitcast(F32), ALU.subtract).then_inc(h_here, 1)

                def add(s, it, b):
                    dve.wait_ge(scattered, 18 * p + 2 * s + b + 1 + 4 * it)
                    dve.wait_ge(acc_added, 18 * p + 2 * s + b + 1 + 4 * it)
                    bank = 4 if b == 0 else 2
                    dve.tensor_tensor(x[:, b, :], x[:, b, :], ps[:, bank:bank + 2, :].rearrange("p b n -> p (b n)"),
                                      ALU.add).then_inc(acc_added, 1)

                build(0, 0)
                if p == 0:
                    for u in range(2, 4):
                        cut_lo(U_O + u + AHEAD)
                rest_xg(0, 0)
                with dve.Fori(0, TURNS) as it:
                    for b in range(2):
                        for l in range(PER_E):
                            j = base + PER_E * b + l
                            if l < PER_E - 1:
                                cut_lo(j + AHEAD, it)
                            if l < 2 * FC and l % 2 == 1:
                                c = l // 2
                                gc = 88 * p + 11 * b + c
                                used(j, it)
                                dve.wait_ge(silu_here, gc + 1 + 22 * it)
                                dve.tensor_tensor(actE[:, gc % 2, :], sgE[:, gc % 2, :], ps[:, gc % 2, 256:512],
                                                  ALU.mult).then_inc(act_here, 1)
                                if c >= 1:
                                    rest_h(c - 1, it, b)
                            elif l in (4, 6):
                                add(b, it, l // 2 - 2)
                            elif l == 10 and b == 1:
                                build(1, it)
                            elif l == 2 * FC + 1:
                                rest_h(FC - 1, it, b)
                            elif l == 2 * FC + 4 and b == 1:
                                rest_xg(1, it)
                            elif l == PER_E - 1:
                                dve.wait_ge(y_hi_here, 8 * p + b + 1 + 2 * it)
                                dve.scalar_tensor_tensor(out=y_lo[:, :], in0=ps[:, 2:4, :].rearrange("p b n -> p (b n)"),
                                                         scalar=gslot[:, b:b + 1], in1=y_hi[:, :].bitcast(F32),
                                                         op0=ALU.mult, op1=ALU.subtract).then_inc(y_here, 1)
                                cut_lo(j + AHEAD, it)
                add(E, 0, 0)
                add(E, 0, 1)
                dve.wait_ge(acc_added, 18 * p + 20)

            settle()
            dve.wait_ge(x_scaled, 1)
            experts(0)
            full = dve.value_load(cint[0:1, 0:1], min_val=0, max_val=T)
            with dve.If(full > P):
                experts(1)
            norm(3, None)

        @block.tensor
        def _(pe):
            def mm(dst, lhsT, rhs, start, stop):
                return pe.matmul(dst, lhsT, rhs, start=start, stop=stop)

            def ready(j, it=0):
                pe.wait_ge(lo_ready, j + 1 + PER_IT * it)

            def turn(i, src, made=None):
                for s in range(4):
                    if made is not None:
                        made(s)
                    for q in range(4):
                        last = pe.transpose(ps[:, 4 + s, q * P:(q + 1) * P], src(s // 2, 4 * (s % 2) + q), ident[:, :])
                    last.then_inc(turned, 1)

            def turn_x(i, norms):
                turn(i, lambda b, k: x[:, b, k * P:(k + 1) * P],
                     lambda s: pe.wait_ge(ln_done[s // 2], norms) if s % 2 == 0 else None)

            def turned_in(i):
                pe.wait_ge(turn_lo, 4 * i + 4)

            def to_channels(j, banks, turned_now=None):
                ready(j)
                w_hi = slot(hi, j).rearrange("p (k n) -> p k n", k=KD)
                w_lo = slot(lo, j).rearrange("p (k n) -> p k n", k=KD)
                for m in range(2):
                    dst = banks[m]
                    c = slice(m * P, m * P + P)
                    for k in range(KD):
                        if m == 0 and k % 4 == 0 and turned_now is not None:
                            pe.wait_ge(turn_lo, 4 * turned_now + 3 + k // 4)
                        mm(dst, w_hi[:, k, c], xT_hi[:, k, :], k == 0, False)
                        mm(dst, w_hi[:, k, c], xT_lo[:, k, :], False, False)
                        last = mm(dst, w_lo[:, k, c], xT_hi[:, k, :], False, k == KD - 1)
                last.then_inc(unit_used, 1)

            def to_tokens(units, k0, nk, first, final, dsts, a_hi, a_lo, norm_follows=False):
                width = dsts[0][0].shape[1]
                for n_, j in enumerate(units):
                    ready(j)
                for b in range(NB):
                    t = slice(b * P, b * P + P)
                    for n_, j in enumerate(units):
                        w_hi = slot(hi, j).rearrange("p (k n) -> p k n", k=nk)
                        w_lo = slot(lo, j).rearrange("p (k n) -> p k n", k=nk)
                        for kk in range(nk):
                            k = k0 + n_ * nk + kk
                            begin = first and n_ == 0 and kk == 0
                            end = final and j == units[-1] and kk == nk - 1
                            for a, w, p in ((a_hi, w_hi, 0), (a_hi, w_lo, 1), (a_lo, w_hi, 2)):
                                for i, dst in enumerate(dsts[b]):
                                    last = mm(dst, a[:, k, t], w[:, kk, i * width:(i + 1) * width],
                                              begin and p == 0, end and p == 2)
                        if b == NB - 1:
                            last.then_inc(unit_used, 1)
                    if norm_follows and b == 0:
                        last.then_inc(block0_done, 1)

            def halves(bank):
                return [[ps[:, bank + 2 * b + i, :] for i in range(2)] for b in range(NB)]

            pe.wait_ge(consts, 1)
            turn(0, lambda b, k: x[:, b, k * P:(k + 1) * P],
                 lambda s: pe.wait_ge(x_here, 16 * NB) if s == 0 else None)
            pe.wait_ge(small_here, 16)
            pe.transpose(ps[:, 0, 0:TAPS * QKV], cw_rows[:, :], ident[0:TAPS * QKV, 0:TAPS * QKV]).then_inc(cw_turned, 1)
            turned_in(0)
            pe.wait_ge(cw_here, 1)

            def project(u):
                pe.wait_ge(conv_step, 6 * u + 6)
                to_channels(U_QKV + u, [ps[:, (2 * u + m) % 4, 0:T] for m in range(2)])

            def small_product(dst, w_hi, w_lo):
                for k in range(KD):
                    mm(dst, w_hi[:, k, :], xT_hi[:, k, :], k == 0, False)
                    mm(dst, w_hi[:, k, :], xT_lo[:, k, :], False, False)
                    last = mm(dst, w_lo[:, k, :], xT_hi[:, k, :], False, k == KD - 1)
                return last

            def turn_heads(tile0, signal, wait):
                for gr in range(4):
                    wait(gr)
                    for i in range(4):
                        last = pe.transpose(ps[:, 4 + gr, i * P:(i + 1) * P],
                                            conv[:, tile0 + 4 * (gr % 2) + i, P * (gr // 2):P * (gr // 2) + P], ident[:, :])
                    last.then_inc(signal, 1)

            pe.wait_ge(ab_cut, 2)
            small_product(ps[0:2 * H, 7, 0:T], wab_hi, wab_lo).then_inc(ab_mm, 1)
            project(0)
            project(1)
            pe.wait_ge(ab_here, 1)
            for b in range(NB):
                last = pe.transpose(ps[:, 7, 2 * H * b:2 * H * (b + 1)], abT[:, b * P:(b + 1) * P], ident[0:2 * H, 0:2 * H])
            last.then_inc(ab_mm, 1)
            for u in range(2, 6):
                project(u)
            pe.wait_ge(consts, 2)
            pe.wait_ge(g_dve, 3)
            for b in range(NB):
                mm(ps[:, 6, b * H:(b + 1) * H], tri_incl[:, :], g[:, b, :], True, True)
            mm(ps[:, 6, 2 * H:3 * H], ones[:, :], g[:, 0, :], True, True).then_inc(g_pe, 1)
            project(6)
            pe.wait_ge(g_dve, 4)
            for gr in range(4):
                for i in range(4):
                    last = mm(ps[:, 4 + gr, i * P:(i + 1) * P],
                              g[:, gr // 2, 4 * (gr % 2) + i:4 * (gr % 2) + i + 1].to_broadcast([P, P]),
                              tri_incl[:, :], True, True)
                last.then_inc(g_pe, 1)
            project(7)
            pe.wait_ge(silu_done, 4)
            pe.wait_ge(g_act, 7)
            turn_heads(0, q_turned, lambda gr: None)
            for u in range(8, 11):
                project(u)
            pe.wait_ge(silu_done, 8)
            turn_heads(H, kv_turned, lambda gr: pe.wait_ge(q_squared, gr + 1))
            project(11)

            def project_z(u):
                c = u // 2
                if u % 2 == 0:
                    pe.wait_ge(conv_step, 12 + 6 * (QKV // 2 - 1 + c))
                to_tokens([U_Z + u], 4 * (u % 2), 4, u % 2 == 0, u % 2 == 1,
                          [[ps[:, 2 * c + b, :]] for b in range(NB)], xT_hi, xT_lo)

            project_z(0)
            project_z(1)
            pe.wait_ge(silu_done, 12)
            turn_heads(2 * H, kv_turned, lambda gr: pe.wait_ge(kv_taken, gr + 1))
            project_z(2)
            for gr in range(4):
                pe.wait_ge(kv_taken, 5 + gr)
                for i in range(4):
                    last = pe.transpose(ps[:, 4 + gr, i * P:(i + 1) * P], kt[:, gr // 2, 4 * (gr % 2) + i, :], ident[:, :])
                last.then_inc(kback, 1)
            project_z(3)
            for gr in range(4):
                pe.wait_ge(kback_taken, gr + 1)
                if gr < 2:
                    pe.wait_ge(z_done, 2 * (gr + 1))
                else:
                    pe.wait_ge(kk_taken, gr - 1)
                    pe.wait_ge(kq_taken, gr - 1)
                t = slice(P * (gr // 2), P * (gr // 2) + P)
                for rhs, bank in ((H, 2 * (gr % 2)), (0, 2 * (gr % 2) + 1)):
                    for i in range(4):
                        h = 4 * (gr % 2) + i
                        last = mm(ps[:, bank, i * P:(i + 1) * P], conv[:, H + h, t], conv[:, rhs + h, t], True, True)
                last.then_inc(kk_mm, 1)

            Pm = conv[:, 2 * H:3 * H, :].rearrange("p h (b t) -> p (h b) t", b=2)

            def first(q):
                pe.wait_ge(inv_rc, q - 3)
                if q >= 6:
                    pe.wait_ge(inv_pc, q - 5)
                for i in range(4):
                    n_ = 4 * (q % 4) + i
                    last = mm(ps[:, 4 + q % 2, i * P:(i + 1) * P], Dm[:, n_, :], Nm[:, n_, :], True, True)
                last.then_inc(inv_p, 1)

            def second(q):
                pe.wait_ge(inv_pc, q - 3)
                if q >= 6:
                    pe.wait_ge(inv_rc, q - 1)
                for i in range(4):
                    n_ = 4 * (q % 4) + i
                    c = slice(i * P, (i + 1) * P)
                    if q < 24:
                        last = mm(ps[:, 6 + q % 2, c], Pm[:, n_, :], Tm[:, n_, :], True, True)
                    if q >= 20:
                        last = mm(ps[:, q % 2, c], Tm[:, n_, :], Pm[:, n_, :], True, True)
                last.then_inc(inv_r, 1)

            for q in range(4, 4 * 7):
                first(q)
                if q >= 5:
                    second(q - 1)
            second(27)

            W_, S_ = Dm[:, 0:H, :], Dm[:, H:2 * H, :]
            pe.wait_ge(inv_rc, 28)
            pe.wait_ge(kscaled, 2)

            def group(bank, products, s):
                for i in range(4):
                    for n_, (lhsT, rhs) in enumerate(products(i)):
                        last = mm(ps[:, bank, i * P:(i + 1) * P], lhsT, rhs, n_ == 0, n_ == len(products(i)) - 1)
                last.then_inc(s, 1)

            for hh in range(2):
                group(hh, lambda i: [(Nm[:, 4 * hh + i, :], vb[:, 0, 4 * hh + i, :])], scan_mm)
            for hh in range(2):
                group(2 + hh, lambda i: [(kt[:, 1, 4 * hh + i, :], Nm[:, H + 4 * hh + i, :])], scan_mm)
            for hh in range(2):
                pe.wait_ge(scan_ev, hh + 1)
                group(4 + hh, lambda i: [(kt[:, 0, 4 * hh + i, :], vb[:, 0, 4 * hh + i, :])], scan_mm)
            for hh in range(2):
                group(6 + hh, lambda i: [(DT[:, 4 * hh + i, :], vb[:, 0, 4 * hh + i, :])], o_mm)
            for hh in range(2):
                pe.wait_ge(scan_ev, 4 + hh + 1)
                group(hh, lambda i: [(Nm[:, H + 4 * hh + i, :], vb[:, 1, 4 * hh + i, :]),
                                     (W_[:, 4 * hh + i, :], S_[:, 4 * hh + i, :])], scan_mm)
            for hh in range(2):
                pe.wait_ge(scan_ev, 6 + hh + 1)
                pe.wait_ge(qg_here, 1)
                group(2 + hh, lambda i: [(conv[:, 4 * hh + i, P:T], S_[:, 4 * hh + i, :]),
                                         (DT[:, H + 4 * hh + i, :], vb[:, 1, 4 * hh + i, :])], o_mm)
            turn(1, lambda b, k: Tm[:, b * H + k, :], lambda s: pe.wait_ge(o_done, s + 1))
            turned_in(1)
            for u in range(2):
                to_tokens([U_OUT + u], 2 * u, 2, u == 0, False, halves(0), xT_hi, xT_lo)
            to_tokens([U_OUT + 2, U_OUT + 3], 4, 2, False, True, halves(0), xT_hi, xT_lo, True)
            turn_x(2, 1)

            for c in range(FC):
                if c >= 3:
                    pe.wait_ge(ffn_act, c - 2)
                for t in range(2):
                    bank = 2 * (c % 3) + t
                    to_channels(U_GU + 2 * c + t, [ps[:, bank, m * T:(m + 1) * T] for m in range(2)],
                                2 if (c, t) == (0, 0) else None)
            pe.wait_ge(ffn_act, FC - 2)
            for u in range(FC - 2):
                pe.wait_ge(ffn_lo, u + 1)
                to_tokens([U_DOWN + u], 2 * u, 2, u == 0, False, halves(4), hT_hi, hT_lo)
            pe.wait_ge(ffn_lo, FC)
            to_tokens([U_DOWN + FC - 2, U_DOWN + FC - 1], 2 * (FC - 2), 2, False, True, halves(4), hT_hi, hT_lo, True)
            turn_x(3, 2)

            to_channels(U_KV, [ps[:, m, 0:T] for m in range(2)], 3)
            to_tokens([U_KV + 1], 0, KD, True, True, [[ps[:, 6 + b, 0:HKV * HD]] for b in range(NB)], xT_hi, xT_lo)
            def queries(gi):
                if gi == 1:
                    pe.wait_ge(vB_here, 1)
                if gi >= 2:
                    pe.wait_ge(qB_here, 2 * gi - 2)
                to_channels(U_Q + gi, [ps[:, Q_BANK[gi % 2], m * T:(m + 1) * T] for m in range(2)])

            def scores(gi):
                pe.wait_ge(qB_here, 2 * gi + 2)
                if gi:
                    pe.wait_ge(sc_bias, gi)
                for i in range(GQ):
                    q = qT[:, 2 * gi + i // 2, :]
                    k = kT2[:, gi, i % 2, :]
                    mm(ps[:, 0, i * P:(i + 1) * P], q[:, 0:P], k[:, 0:P], True, True)
                    last = mm(ps[:, 1 + i // 2, (i % 2) * T:(i % 2) * T + T], q[:, P:T], k, True, True)
                last.then_inc(sc_mm, 1)

            def attend(gi):
                pe.wait_ge(sc_prob, gi + 1)
                for r in range(3):
                    n_ = 3 * gi + r
                    if n_ >= 2:
                        pe.wait_ge(pt_taken, n_ - 1)
                    for i in range(GQ):
                        last = pe.transpose(ps[:, 4 + n_ % 2, i * P:(i + 1) * P], sS[:, gi % 2, i, r * P:(r + 1) * P],
                                            ident[:, :])
                    last.then_inc(pt_mm, 1)
                pe.wait_ge(pt_taken, 3 * gi + 3)
                if gi:
                    pe.wait_ge(pv_lo, gi)
                v = slice(gi * HD, (gi + 1) * HD)
                for i in range(GQ):
                    o = 64 * (i % 2)
                    c = (i // 2) * T
                    mm(ps[o:o + 64, 6, c:c + P], vB[:, 0, v], pT[:, i, :], True, True)
                    mm(ps[o:o + 64, 6, c + P:c + T], vB[:, 0, v], pT[:, 4 + i, :], True, False)
                    last = mm(ps[o:o + 64, 6, c + P:c + T], vB[:, 1, v], pT[:, 8 + i, :], False, True)
                last.then_inc(pv_mm, 1)

            def project_out(u):
                pe.wait_ge(pv_lo, u + 1)
                to_tokens([U_O + u], 2 * u, 2, u == 0, False, halves(0), oT_hi, oT_lo)

            queries(0)
            queries(1)
            pe.wait_ge(kB_act, 4)
            pe.wait_ge(kB_dve, 4)
            pe.wait_ge(consts, 4)
            scores(0)
            queries(2)
            scores(1)
            queries(3)
            attend(0)
            scores(2)
            attend(1)
            scores(3)
            attend(2)
            pe.wait_ge(sc_bias, 4)
            pe.wait_ge(qB_here, 8)
            project_out(0)
            attend(3)
            project_out(1)
            pe.wait_ge(pv_lo, HKV)
            to_tokens([U_O + 2, U_O + 3], 4, 2, False, True, halves(0), oT_hi, oT_lo, True)
            turn_x(4, 3)

            turned_in(4)
            pe.wait_ge(wr_cut, 2)
            small_product(ps[0:E, 0, 0:T], wr_hi, wr_lo).then_inc(lg_mm, 1)
            pe.wait_ge(lgT_here, 1)
            for b in range(NB):
                last = pe.transpose(ps[:, 0, E * b:E * (b + 1)], lgT[:, b * P:(b + 1) * P], ident[0:E, 0:E])
            last.then_inc(lg_mm, 1)
            pe.wait_ge(sel_here, 1)
            pe.wait_ge(consts, 3)
            mm(ps[:, 1, 0:E], tri_strict[:, :], sel[:, 0, :], True, True)
            mm(ps[:, 1, E:2 * E], tri_strict[:, :], sel[:, 1, :], True, False)
            mm(ps[:, 1, E:2 * E], ones[:, :], sel[:, 0, :], False, True)
            for b in range(NB):
                last = mm(ps[:, 1, 2 * E:3 * E], ones[:, :], sel[:, b, :], b == 0, b == 1)
            last.then_inc(pos_mm, 1)

            def experts(p):
                base = U_MOE + p * E * PER_E

                def gather(pair, it):
                    pe.wait_ge(oneh_here, 5 * p + pair + 1 + it)
                    for k in range(KD):
                        bank = 6 * (k // 4) + k % 4 // 2
                        dst = ps[:, bank, (k % 2) * 2 * P:(k % 2) * 2 * P + 2 * P]
                        c = slice(k * P, k * P + P)
                        for n_, (part, b) in enumerate(((x3_hi, 0), (x3_hi, 1), (x3_lo, 0), (x3_lo, 1))):
                            last = mm(dst, part[:, b, c], oneh[:, b, :, :].rearrange("p e s -> p (e s)"), n_ == 0, n_ == 3)
                    last.then_inc(gathered, 1)

                def slots(ge, it, i):
                    for b in range(NB):
                        pe.transpose(ps[:, 4, b * P:(b + 1) * P], oneh[:, b, i, :].bitcast(F32), ident[:, :])
                    for b in range(NB):
                        last = mm(ps[:, 5, 0:1], oneh[:, b, i, :].bitcast(F32), gates[:, b, bass.ds(ge + 2 * it, 1)],
                                  b == 0, b == 1)
                    last.then_inc(slots_mm, 1)

                def turn_h(c, it, b):
                    gc = 88 * p + 11 * b + c
                    pe.wait_ge(act_here, gc + 3 + 22 * it)
                    pe.wait_ge(h_here, gc + 1 + 22 * it)
                    for m in range(2):
                        last = pe.transpose(ps[:, 6 + gc % 2, m * P:(m + 1) * P], actE[:, gc % 2, m * P:(m + 1) * P],
                                            ident[:, :])
                    last.then_inc(ff_turned, 1)

                def scatter(s, it, par):
                    pe.wait_ge(y_here, 8 * p + s + 1 + 2 * it)
                    for b in range(NB):
                        for n_, part in enumerate((y_hi, y_lo)):
                            for i in range(2):
                                bank = (4 if b == 0 else 2) + i
                                last = mm(ps[:, bank, :], onehT[:, par, b, :], part[:, i * 512:(i + 1) * 512],
                                          n_ == 0, n_ == 1)
                        last.then_inc(scattered, 1)

                if p == 0:
                    pe.wait_ge(route_here, 1)
                pe.wait_ge(x3_cut, 2)
                gather(0, 0)
                slots(0, 0, 0)
                pe.wait_ge(xg_here, 5 * p + 1)
                pe.wait_ge(moe_zero, 2 * p + 2)
                with pe.Fori(0, TURNS) as it:
                    for b in range(2):
                        for l in range(PER_E):
                            j = base + PER_E * b + l
                            if l < 2 * FC:
                                c = l // 2
                                gc = 88 * p + 11 * b + c
                                if l == 0 and b == 0:
                                    pe.wait_ge(xg_here, 5 * p + 1 + it)
                                if l % 2 == 0:
                                    pe.wait_ge(act_here, gc + 1 + 22 * it)
                                ready(j, it)
                                w_hi = slot(hi, j).rearrange("p (k n) -> p k n", k=4)
                                w_lo = slot(lo, j).rearrange("p (k n) -> p k n", k=4)
                                for kk in range(4):
                                    k = 4 * (l % 2) + kk
                                    mm(ps[:, gc % 2, :], xg_hi[:, k, b, :], w_hi[:, kk, :], k == 0, False)
                                    mm(ps[:, gc % 2, :], xg_hi[:, k, b, :], w_lo[:, kk, :], False, False)
                                    last = mm(ps[:, gc % 2, :], xg_lo[:, k, b, :], w_hi[:, kk, :], False, k == KD - 1)
                                last.then_inc(unit_used, 1)
                                if l % 2 == 1 and c >= 1:
                                    turn_h(c - 1, it, b)
                                if l == 3:
                                    scatter(b, it, (b + 1) % 2)
                            else:
                                d = l - 2 * FC
                                pe.wait_ge(h_here, 88 * p + 11 * b + d + 3 + 22 * it)
                                if d == 0:
                                    pe.wait_ge(acc_added, 18 * p + 2 * b + 4 + 4 * it)
                                ready(j, it)
                                w_hi = slot(hi, j).rearrange("p (k n) -> p k n", k=2)
                                w_lo = slot(lo, j).rearrange("p (k n) -> p k n", k=2)
                                for kk in range(2):
                                    k = 2 * d + kk
                                    for n_, (a, w) in enumerate(((hE_hi, w_hi), (hE_hi, w_lo), (hE_lo, w_hi))):
                                        for i in range(2):
                                            last = mm(ps[:, 2 + i, :], a[:, k, :], w[:, kk, i * 512:(i + 1) * 512],
                                                      k == 0 and n_ == 0, k == 2 * FC - 1 and n_ == 2)
                                last.then_inc(unit_used, 1)
                                if d == 1:
                                    turn_h(FC - 1, it, b)
                                if d == 3:
                                    if b == 1:
                                        pe.wait_ge(h_here, 88 * p + 2 * FC + 2 + 22 * it)
                                        pe.wait_ge(act_here, 88 * p + 2 * FC + 2 + 22 * it)
                                        gather(1, it)
                                    slots(b + 1, it, (b + 1) % 2)
                scatter(E, 0, (E + 1) % 2)

            experts(0)
            full = pe.value_load(cint[0:1, 0:1], min_val=0, max_val=T)
            with pe.If(full > P):
                experts(1)


_INS = ["x", "dn_w_in", "dn_conv_w", "dn_a_log", "dn_dt_bias", "dn_norm_w", "dn_w_out", "w_kv_shared", "sw_w_q",
        "sw_sinks", "sw_w_out", "ffn_w_gu", "ffn_w_down", "moe_w_router", "moe_w_gu", "moe_w_down", "ln_g", "ln_b"]


def kernel(**inputs):
    import numpy as np
    import concourse.bacc as bacc
    from concourse.bass_utils import run_bass_kernel_spmd

    nc = bacc.Bacc("TRN2", target_bir_lowering=False, num_devices=1)
    arrays, args = {}, []
    for name in _INS:
        a = np.ascontiguousarray(inputs[name])
        arrays[f"in_{name}"] = a
        args.append(nc.dram_tensor(f"in_{name}", a.shape, mybir.dt.from_np(a.dtype), kind="ExternalInput").ap())
    args.append(nc.dram_tensor("out_0", inputs["x"].shape, F32, kind="ExternalOutput").ap())
    trunk(nc, *args)
    return run_bass_kernel_spmd(nc, [arrays], core_ids=[0]).results[0]["out_0"]
```
